# Optimizing a Trainium2 kernel written in Bass

```python
import math
import jax, jax.numpy as jnp
from jax import lax
import numpy as np
import jax
import jax.numpy as jnp

D_MODEL = 1024
BATCH = 1
SEQ = 512
DEPTH = 1

HEAD_DIM = 64
N_ATTN_HEADS = 8
N_DELTA_HEADS = 8
ATTN_WIDTH = N_ATTN_HEADS * HEAD_DIM
DELTA_WIDTH = N_DELTA_HEADS * HEAD_DIM
MIX_WIDTH = ATTN_WIDTH + DELTA_WIDTH
DILATED_BRANCHES = ((128, 1), (512, 4), (2048, 16))
PAD_UNIT = 2048
N_BUCKETS = 32
MAX_DISTANCE = 2048
CONV_WIDTH = 4
CHUNK = 64
D_FF = (8 * D_MODEL + 3 * 256 - 1) // (3 * 256) * 256
IN_WIDTH = 3 * ATTN_WIDTH + 4 * DELTA_WIDTH + 2 * N_DELTA_HEADS
EPS = 1e-6
NEG_INF = -1e30


def _rmsnorm(x, g):
    x32 = x.astype(jnp.float32)
    y = x32 * lax.rsqrt(jnp.mean(x32 * x32, axis=-1, keepdims=True) + EPS)
    return (y * g.astype(jnp.float32)).astype(x.dtype)

def _l2norm(x):
    return x * lax.rsqrt(jnp.sum(x * x, axis=-1, keepdims=True) + EPS)

def _t5_bucket(distance):
    max_exact = N_BUCKETS // 2
    dist_f = jnp.maximum(distance, 1).astype(jnp.float32)
    large = max_exact + (jnp.log(dist_f / max_exact) / math.log(MAX_DISTANCE / max_exact)
                         * (N_BUCKETS - max_exact)).astype(jnp.int32)
    return jnp.where(distance < max_exact, distance, jnp.minimum(large, N_BUCKETS - 1))

def _dilated_branch(q, k, v, rel_bias, window, dilation):
    b, h, p, dh = q.shape
    band = window // dilation
    length = p // dilation
    n_blocks = length // band

    def to_blocks(t):
        t = t.reshape(b, h, length, dilation, dh).transpose(0, 1, 3, 2, 4)
        return t.reshape(b, h, dilation, n_blocks, band, dh)

    qb, kb, vb = to_blocks(q), to_blocks(k), to_blocks(v)

    def with_prev(t):
        prev = jnp.pad(t, ((0, 0), (0, 0), (0, 0), (1, 0), (0, 0), (0, 0)))[:, :, :, :-1]
        return jnp.concatenate([prev, t], axis=-2)

    kw, vw = with_prev(kb), with_prev(vb)
    qi = jnp.arange(band)[:, None]
    kj = jnp.arange(2 * band)[None, :]
    steps = qi + band - kj
    in_window = (steps >= 0) & (steps <= band)
    not_before_start = (jnp.arange(n_blocks)[:, None, None] > 0) | (kj >= band)[None]
    valid = in_window[None] & not_before_start
    bias = rel_bias.astype(jnp.float32)[_t5_bucket(jnp.maximum(steps, 0) * dilation)]
    bias = bias.transpose(2, 0, 1)
    s = jnp.einsum('bhrnqd,bhrnkd->bhrnqk', qb * dh ** -0.5, kw) + bias[None, :, None, None]
    s = jnp.where(valid, s, NEG_INF)
    m = jnp.max(s, axis=-1, keepdims=True)
    e = jnp.exp(s - m)
    denom = jnp.sum(e, axis=-1, keepdims=True)
    o = jnp.einsum('bhrnqk,bhrnkd->bhrnqd', e, vw) / denom
    lse = (m + jnp.log(denom))[..., 0]
    o = o.reshape(b, h, dilation, length, dh).transpose(0, 1, 3, 2, 4).reshape(b, h, p, dh)
    lse = lse.reshape(b, h, dilation, length).transpose(0, 1, 3, 2).reshape(b, h, p)
    return o, lse

def _dilated_attention(q, k, v, rel_bias):
    b, s, h, dh = q.shape
    p = (s + PAD_UNIT - 1) // PAD_UNIT * PAD_UNIT

    def to_bhpd(t):
        t = jnp.pad(t.astype(jnp.float32), ((0, 0), (0, p - s), (0, 0), (0, 0)))
        return t.transpose(0, 2, 1, 3)

    q, k, v = to_bhpd(q), to_bhpd(k), to_bhpd(v)
    outs, lses = [], []
    for window, dilation in DILATED_BRANCHES:
        o_i, lse_i = _dilated_branch(q, k, v, rel_bias, window, dilation)
        outs.append(o_i)
        lses.append(lse_i)
    w = jax.nn.softmax(jnp.stack(lses), axis=0)
    o = jnp.sum(w[..., None] * jnp.stack(outs), axis=0)
    return o[:, :, :s].transpose(0, 2, 1, 3).reshape(b, s, h * dh)

def _causal_conv(x, w):
    return lax.conv_general_dilated(x, w[:, None, :], window_strides=(1,),
                                    padding=((CONV_WIDTH - 1, 0),),
                                    dimension_numbers=('NWC', 'WIO', 'NWC'),
                                    feature_group_count=x.shape[-1])

def _chunk_gated_delta_rule(q, k, v, g, beta):
    b, s, h, dk = q.shape
    dv = v.shape[-1]
    nc = s // CHUNK

    def chunks(t):
        return t.reshape(b, nc, CHUNK, h, t.shape[-1]).transpose(1, 0, 3, 2, 4)

    qc, kc, vc = chunks(q), chunks(k), chunks(v)
    gcum = jnp.cumsum(g.reshape(b, nc, CHUNK, h).transpose(1, 0, 3, 2), axis=-1)
    bc = beta.reshape(b, nc, CHUNK, h).transpose(1, 0, 3, 2)
    causal = jnp.tril(jnp.ones((CHUNK, CHUNK), dtype=bool))
    strict = jnp.tril(jnp.ones((CHUNK, CHUNK), dtype=bool), k=-1)
    diff = gcum[..., :, None] - gcum[..., None, :]
    decay = jnp.where(causal, jnp.exp(jnp.where(causal, diff, 0.0)), 0.0)
    k_beta = kc * bc[..., None]
    a_mat = jnp.where(strict, jnp.einsum('nbhcd,nbhed->nbhce', k_beta, kc) * decay, 0.0)
    rhs = jnp.concatenate([vc * bc[..., None], k_beta * jnp.exp(gcum)[..., None]], axis=-1)
    sol = lax.linalg.triangular_solve(a_mat + jnp.eye(CHUNK, dtype=a_mat.dtype), rhs,
                                      left_side=True, lower=True, unit_diagonal=True)
    u, w = sol[..., :dv], sol[..., dv:]
    qk = jnp.where(causal, jnp.einsum('nbhcd,nbhed->nbhce', qc, kc) * decay, 0.0)

    def step(state, xs):
        q_i, k_i, u_i, w_i, g_i, qk_i = xs
        v_new = u_i - jnp.einsum('bhck,bhkv->bhcv', w_i, state)
        o_i = (jnp.einsum('bhck,bhkv->bhcv', q_i * jnp.exp(g_i)[..., None], state)
               + jnp.einsum('bhce,bhev->bhcv', qk_i, v_new))
        g_last = g_i[..., -1]
        k_dec = k_i * jnp.exp(g_last[..., None] - g_i)[..., None]
        state = state * jnp.exp(g_last)[..., None, None] + jnp.einsum('bhck,bhcv->bhkv', k_dec, v_new)
        return state, o_i

    state0 = jnp.zeros((b, h, dk, dv), jnp.float32)
    _, o = lax.scan(step, state0, (qc, kc, u, w, gcum, qk))
    return o.transpose(1, 0, 3, 2, 4).reshape(b, s, h, dv)

def _gated_deltanet(q, k, v, z, b_logit, a_logit, conv_w, a_log, dt_bias, norm_g):
    bsz, s, _ = q.shape
    qkv = jax.nn.silu(_causal_conv(jnp.concatenate([q, k, v], axis=-1), conv_w))
    q, k, v = jnp.split(qkv.astype(jnp.float32), 3, axis=-1)
    shp = (bsz, s, N_DELTA_HEADS, HEAD_DIM)
    q = _l2norm(q.reshape(shp)) * HEAD_DIM ** -0.5
    k = _l2norm(k.reshape(shp))
    v = v.reshape(shp)
    beta = jax.nn.sigmoid(b_logit.astype(jnp.float32))
    g = -jnp.exp(a_log.astype(jnp.float32)) * jax.nn.softplus(
        a_logit.astype(jnp.float32) + dt_bias.astype(jnp.float32))
    o = _chunk_gated_delta_rule(q, k, v, g, beta)
    o = _rmsnorm(o, norm_g) * jax.nn.silu(z.astype(jnp.float32).reshape(shp))
    return o.reshape(bsz, s, DELTA_WIDTH).astype(z.dtype)

def first_inputs(seed: int = 0) -> dict:
    key = jax.random.key(seed)
    ks = jax.random.split(key, 20)
    f32 = jnp.float32

    def nrm(k, shape, scale):
        return jax.random.normal(k, shape, f32) * scale

    dt = jnp.exp(jax.random.uniform(ks[9], (DEPTH, N_DELTA_HEADS), f32,
                                    minval=math.log(1e-3), maxval=math.log(1e-1)))
    return {
        'x': nrm(ks[0], (BATCH, SEQ, D_MODEL), 1.0),
        'c': nrm(ks[1], (BATCH, D_MODEL), 1.0),
        'w_ada': nrm(ks[2], (DEPTH, D_MODEL, 6 * D_MODEL), 0.5 * D_MODEL ** -0.5),
        'b_ada': nrm(ks[3], (DEPTH, 6 * D_MODEL), 0.02),
        'norm_attn_g': 1.0 + nrm(ks[4], (DEPTH, D_MODEL), 0.05),
        'w_in': nrm(ks[5], (DEPTH, D_MODEL, IN_WIDTH), D_MODEL ** -0.5),
        'rel_bias': nrm(ks[6], (N_BUCKETS, N_ATTN_HEADS), 0.5),
        'conv_w': nrm(ks[7], (DEPTH, CONV_WIDTH, 3 * DELTA_WIDTH), CONV_WIDTH ** -0.5),
        'a_log': jnp.log(jax.random.uniform(ks[8], (DEPTH, N_DELTA_HEADS), f32, minval=1.0, maxval=16.0)),
        'dt_bias': dt + jnp.log(-jnp.expm1(-dt)),
        'delta_norm_g': 1.0 + nrm(ks[10], (DEPTH, HEAD_DIM), 0.05),
        'w_out': nrm(ks[11], (DEPTH, MIX_WIDTH, D_MODEL), MIX_WIDTH ** -0.5),
        'norm_ffn_g': 1.0 + nrm(ks[12], (DEPTH, D_MODEL), 0.05),
        'w_gate': nrm(ks[13], (DEPTH, D_MODEL, D_FF), D_MODEL ** -0.5),
        'w_up': nrm(ks[14], (DEPTH, D_MODEL, D_FF), D_MODEL ** -0.5),
        'w_down': nrm(ks[15], (DEPTH, D_FF, D_MODEL), D_FF ** -0.5),
        'final_norm_g': 1.0 + nrm(ks[16], (D_MODEL,), 0.05),
    }

def first_block(x, c, w_ada, b_ada, norm_attn_g, w_in, rel_bias, conv_w, a_log, dt_bias,
              delta_norm_g, w_out, norm_ffn_g, w_gate, w_up, w_down, final_norm_g):
    bsz, s, _ = x.shape
    split_points = np.cumsum([ATTN_WIDTH] * 3 + [DELTA_WIDTH] * 4 + [N_DELTA_HEADS])
    c_act = jax.nn.silu(c)
    for l in range(DEPTH):
        mod = c_act @ w_ada[l] + b_ada[l]
        sh1, sc1, g1, sh2, sc2, g2 = [m[:, None, :] for m in jnp.split(mod, 6, axis=-1)]
        h = _rmsnorm(x, norm_attn_g[l]) * (1.0 + sc1) + sh1
        proj = h @ w_in[l]
        q_a, k_a, v_a, q_d, k_d, v_d, z_d, b_d, a_d = jnp.split(proj, split_points, axis=-1)
        hs = (bsz, s, N_ATTN_HEADS, HEAD_DIM)
        y_attn = _dilated_attention(q_a.reshape(hs), k_a.reshape(hs), v_a.reshape(hs), rel_bias).astype(x.dtype)
        y_delta = _gated_deltanet(q_d, k_d, v_d, z_d, b_d, a_d, conv_w[l], a_log[l], dt_bias[l], delta_norm_g[l])
        y = jnp.concatenate([y_attn, y_delta], axis=-1) @ w_out[l]
        x = x + g1 * y
        h = _rmsnorm(x, norm_ffn_g[l]) * (1.0 + sc2) + sh2
        y = (jax.nn.silu(h @ w_gate[l]) * (h @ w_up[l])) @ w_down[l]
        x = x + g2 * y
    return _rmsnorm(x, final_norm_g)


DEPTH_2 = 2

CTX_LEN = 256
GRID_W = 64
N_MOD = 9

GROUP_W = 256
MIX_W = 4 * GROUP_W

FNET_HEADS = 4
FNET_HD = GROUP_W // FNET_HEADS

MLA_HEADS = 4
QK_NOPE = 64
QK_ROPE = 32
AXIS_ROPE = QK_ROPE // 2
V_HD = 64
Q_RANK = 192
KV_RANK = 128
ROPE_BASE = 10000.0
Q_BLOCK = 128

SGU_HEADS = 4
SGU_HD = GROUP_W // SGU_HEADS
SGU_CHUNK = 128

POOL_WINDOWS = (2, 4, 8, 16)
POOL_GROUPS = len(POOL_WINDOWS)
POOL_HD = GROUP_W // POOL_GROUPS

D_FF_2 = 2816

OFF_F = 0
OFF_Q = OFF_F + GROUP_W
OFF_KV = OFF_Q + Q_RANK
OFF_KR = OFF_KV + KV_RANK
OFF_G = OFF_KR + QK_ROPE
OFF_P = OFF_G + 2 * GROUP_W
IN_W = OFF_P + GROUP_W


def rms_norm(x, g):
    xf = x.astype(jnp.float32)
    y = xf * lax.rsqrt(jnp.mean(xf * xf, axis=-1, keepdims=True) + EPS)
    return (y * g.astype(jnp.float32)).astype(x.dtype)

def modulate(x, shift, scale):
    return x * (1 + scale) + shift

def swiglu(x, w13, w2):
    a, b = jnp.split(x @ w13, 2, axis=-1)
    return (jax.nn.silu(a) * b) @ w2

def ffn_half_step(h, g, shift, scale, gate, w13, w2):
    return h + 0.5 * gate * swiglu(modulate(rms_norm(h, g), shift, scale), w13, w2)

def axial_rope_tables(n_tokens):
    rows = n_tokens // GRID_W
    row = jnp.repeat(jnp.arange(rows, dtype=jnp.float32), GRID_W)
    col = (jnp.arange(n_tokens) % GRID_W).astype(jnp.float32)
    inv = jnp.power(ROPE_BASE, -jnp.arange(0, AXIS_ROPE, 2, dtype=jnp.float32) / AXIS_ROPE)
    ang = jnp.stack([row[:, None] * inv, col[:, None] * inv], axis=1)
    return jnp.cos(ang), jnp.sin(ang)

def apply_axial_rope(x, cos, sin):
    xs = x.reshape(x.shape[:-1] + (2, 2, AXIS_ROPE // 2)).astype(jnp.float32)
    x1, x2 = xs[..., 0, :], xs[..., 1, :]
    c = cos[None, :, None]
    s = sin[None, :, None]
    out = jnp.stack([x1 * c - x2 * s, x1 * s + x2 * c], axis=-2)
    return out.reshape(x.shape).astype(x.dtype)

def fourier_mixer(z, w_f):
    B, L, _ = z.shape
    zh = z.reshape(B, L, FNET_HEADS, FNET_HD).astype(jnp.float32)
    f = jnp.fft.fft2(zh, axes=(1, 3), norm="ortho").real.astype(z.dtype)
    return jnp.einsum('blhc,hcd->blhd', f, w_f).reshape(B, L, GROUP_W)

def mla_query(cq, g_q, w_uq, rope):
    B, L, _ = cq.shape
    q = (rms_norm(cq, g_q) @ w_uq).reshape(B, L, MLA_HEADS, QK_NOPE + QK_ROPE)
    if rope is not None:
        q = jnp.concatenate([q[..., :QK_NOPE], apply_axial_rope(q[..., QK_NOPE:], *rope)], axis=-1)
    return q

def mla_keys_values(ckv, kr, g_kv, w_ukv, rope):
    B, L, _ = ckv.shape
    kv = (rms_norm(ckv, g_kv) @ w_ukv).reshape(B, L, MLA_HEADS, QK_NOPE + V_HD)
    k_rope = kr[:, :, None, :]
    if rope is not None:
        k_rope = apply_axial_rope(k_rope, *rope)
    k = jnp.concatenate([kv[..., :QK_NOPE], jnp.broadcast_to(k_rope, (B, L, MLA_HEADS, QK_ROPE))], axis=-1)
    return k, kv[..., QK_NOPE:]

def attend(q, k, v):
    s = jnp.einsum('bqhd,bkhd->bhqk', q, k).astype(jnp.float32) * (QK_NOPE + QK_ROPE) ** -0.5
    p = jax.nn.softmax(s, axis=-1).astype(v.dtype)
    return jnp.einsum('bhqk,bkhd->bqhd', p, v)

def blocked_attention(q, k, v):
    B, L, H, dk = q.shape
    qb = q.reshape(B, L // Q_BLOCK, Q_BLOCK, H, dk).transpose(1, 0, 2, 3, 4)
    ob = lax.map(lambda qi: attend(qi, k, v), qb)
    return ob.transpose(1, 0, 2, 3, 4).reshape(B, L, H, v.shape[-1])

def spatial_gating_mixer(z, g_v, w_s, b_s):
    B, L, _ = z.shape
    z = jax.nn.gelu(z)
    u, v = jnp.split(z, 2, axis=-1)
    v = rms_norm(v.reshape(B, L, SGU_HEADS, SGU_HD), g_v)
    v = v.reshape(B, L // SGU_CHUNK, SGU_CHUNK, SGU_HEADS, SGU_HD)
    v = jnp.einsum('hpq,bnqhc->bnphc', w_s, v) + b_s.T[None, None, :, :, None]
    return u * v.reshape(B, L, GROUP_W)

def pooling_mixer(z, w_p, s_p):
    B, L, _ = z.shape
    zf = z.reshape(B, L, POOL_GROUPS, POOL_HD).astype(jnp.float32)
    cs = jnp.concatenate([jnp.zeros((B, 1, POOL_GROUPS, POOL_HD), jnp.float32), jnp.cumsum(zf, axis=1)], axis=1)
    t = jnp.arange(L)[:, None]
    w = jnp.array(POOL_WINDOWS, dtype=jnp.int32)[None, :]
    lo = jnp.clip(t - w // 2, 0, L)
    hi = jnp.clip(t - w // 2 + w, 0, L)
    gi = jnp.arange(POOL_GROUPS)[None, :]
    win_sum = cs[:, hi, gi] - cs[:, lo, gi]
    pooled = win_sum / (hi - lo).astype(jnp.float32)[None, :, :, None] - zf
    y = jnp.einsum('blgc,gcd->blgd', pooled.astype(z.dtype), w_p).reshape(B, L, GROUP_W)
    return y * s_p

def mix_heads(z, k, v, rope, w_fnet, g_q, w_uq, g_sgu, w_sgu, b_sgu, w_pool, s_pool):
    B, L, _ = z.shape
    q = mla_query(z[..., OFF_Q:OFF_KV], g_q, w_uq, rope)
    att = blocked_attention(q, k, v).reshape(B, L, GROUP_W)
    return jnp.concatenate([
        fourier_mixer(z[..., OFF_F:OFF_Q], w_fnet),
        att,
        spatial_gating_mixer(z[..., OFF_G:OFF_P], g_sgu, w_sgu, b_sgu),
        pooling_mixer(z[..., OFF_P:], w_pool, s_pool),
    ], axis=-1)

def second_inputs(seed: int = 0) -> dict:
    key = jax.random.key(seed)
    ks = iter(jax.random.split(key, 32))
    f32 = jnp.float32

    def nrm(shape, scale):
        return jax.random.normal(next(ks), shape, f32) * scale

    def gain(shape):
        return 1.0 + 0.1 * jax.random.normal(next(ks), shape, f32)

    n = DEPTH_2
    return {
        "x": nrm((BATCH, SEQ, D_MODEL), 1.0),
        "c": nrm((BATCH, D_MODEL), 1.0),
        "ctx": nrm((BATCH, CTX_LEN, D_MODEL), 1.0),
        "c_ctx": nrm((D_MODEL,), 1.0),
        "w_ada": nrm((n, D_MODEL, N_MOD * D_MODEL), 0.5 * D_MODEL ** -0.5),
        "b_ada": nrm((n, N_MOD * D_MODEL), 0.02),
        "g_ffn1": gain((n, D_MODEL)),
        "w13_ffn1": nrm((n, D_MODEL, 2 * D_FF_2), D_MODEL ** -0.5),
        "w2_ffn1": nrm((n, D_FF_2, D_MODEL), D_FF_2 ** -0.5),
        "g_mix": gain((n, D_MODEL)),
        "w_in": nrm((n, D_MODEL, IN_W), D_MODEL ** -0.5),
        "w_fnet": nrm((n, FNET_HEADS, FNET_HD, FNET_HD), FNET_HD ** -0.5),
        "g_q": gain((n, Q_RANK)),
        "w_uq": nrm((n, Q_RANK, MLA_HEADS * (QK_NOPE + QK_ROPE)), Q_RANK ** -0.5),
        "g_kv": gain((n, KV_RANK)),
        "w_ukv": nrm((n, KV_RANK, MLA_HEADS * (QK_NOPE + V_HD)), KV_RANK ** -0.5),
        "g_sgu": gain((n, SGU_HEADS, SGU_HD)),
        "w_sgu": nrm((n, SGU_HEADS, SGU_CHUNK, SGU_CHUNK), SGU_CHUNK ** -0.5),
        "b_sgu": gain((n, SGU_HEADS, SGU_CHUNK)),
        "w_pool": nrm((n, POOL_GROUPS, POOL_HD, POOL_HD), POOL_HD ** -0.5),
        "s_pool": gain((n, GROUP_W)),
        "w_out": nrm((n, MIX_W, D_MODEL), MIX_W ** -0.5),
        "g_ffn2": gain((n, D_MODEL)),
        "w13_ffn2": nrm((n, D_MODEL, 2 * D_FF_2), D_MODEL ** -0.5),
        "w2_ffn2": nrm((n, D_FF_2, D_MODEL), D_FF_2 ** -0.5),
        "g_final": gain((D_MODEL,)),
    }

def second_block(x, c, ctx, c_ctx, w_ada, b_ada, g_ffn1, w13_ffn1, w2_ffn1, g_mix, w_in, w_fnet,
              g_q, w_uq, g_kv, w_ukv, g_sgu, w_sgu, b_sgu, w_pool, s_pool, w_out,
              g_ffn2, w13_ffn2, w2_ffn2, g_final):
    B, L, _ = x.shape
    rope = axial_rope_tables(L)
    silu_c = jax.nn.silu(c)
    silu_cc = jax.nn.silu(c_ctx)[None]
    h, hc = x, ctx
    for i in range(DEPTH_2):
        last = i == DEPTH_2 - 1
        m = jnp.split((silu_c @ w_ada[i] + b_ada[i])[:, None, :], N_MOD, axis=-1)
        mc = jnp.split((silu_cc @ w_ada[i] + b_ada[i])[:, None, :], N_MOD, axis=-1)

        h = ffn_half_step(h, g_ffn1[i], m[0], m[1], m[2], w13_ffn1[i], w2_ffn1[i])
        hc = ffn_half_step(hc, g_ffn1[i], mc[0], mc[1], mc[2], w13_ffn1[i], w2_ffn1[i])

        n_lat = modulate(rms_norm(h, g_mix[i]), m[3], m[4])
        n_ctx = modulate(rms_norm(hc, g_mix[i]), mc[3], mc[4])
        z = n_lat @ w_in[i]
        zc = n_ctx @ (w_in[i][:, OFF_KV:OFF_G] if last else w_in[i])
        zc_kv = zc if last else zc[..., OFF_KV:OFF_G]
        kc, vc = mla_keys_values(zc_kv[..., :KV_RANK], zc_kv[..., KV_RANK:], g_kv[i], w_ukv[i], None)
        k, v = mla_keys_values(z[..., OFF_KV:OFF_KR], z[..., OFF_KR:OFF_G], g_kv[i], w_ukv[i], rope)
        mix_p = (w_fnet[i], g_q[i], w_uq[i], g_sgu[i], w_sgu[i], b_sgu[i], w_pool[i], s_pool[i])
        y = mix_heads(z, jnp.concatenate([k, kc], axis=1), jnp.concatenate([v, vc], axis=1), rope, *mix_p) @ w_out[i]
        h = h + m[5] * y

        h = ffn_half_step(h, g_ffn2[i], m[6], m[7], m[8], w13_ffn2[i], w2_ffn2[i])

        if not last:
            yc = mix_heads(zc, kc, vc, None, *mix_p) @ w_out[i]
            hc = hc + mc[5] * yc
            hc = ffn_half_step(hc, g_ffn2[i], mc[6], mc[7], mc[8], w13_ffn2[i], w2_ffn2[i])
    return rms_norm(h, g_final)


def setup_inputs(seed=0):
    out = dict(first_inputs(seed))
    for name, value in second_inputs(seed + 1).items():
        if name != "x":
            out[name + "_2"] = value
    return out


def reference(
    x, c, w_ada, b_ada, norm_attn_g, w_in, rel_bias, conv_w, a_log, dt_bias, delta_norm_g,
    w_out, norm_ffn_g, w_gate, w_up, w_down, final_norm_g, c_2, ctx_2, c_ctx_2, w_ada_2,
    b_ada_2, g_ffn1_2, w13_ffn1_2, w2_ffn1_2, g_mix_2, w_in_2, w_fnet_2, g_q_2, w_uq_2, g_kv_2,
    w_ukv_2, g_sgu_2, w_sgu_2, b_sgu_2, w_pool_2, s_pool_2, w_out_2, g_ffn2_2, w13_ffn2_2,
    w2_ffn2_2, g_final_2,
):
    x = first_block(
        x, c, w_ada, b_ada, norm_attn_g, w_in, rel_bias, conv_w, a_log, dt_bias, delta_norm_g,
        w_out, norm_ffn_g, w_gate, w_up, w_down, final_norm_g,
    )
    return second_block(
        x, c_2, ctx_2, c_ctx_2, w_ada_2, b_ada_2, g_ffn1_2, w13_ffn1_2, w2_ffn1_2, g_mix_2,
        w_in_2, w_fnet_2, g_q_2, w_uq_2, g_kv_2, w_ukv_2, g_sgu_2, w_sgu_2, b_sgu_2, w_pool_2,
        s_pool_2, w_out_2, g_ffn2_2, w13_ffn2_2, w2_ffn2_2, g_final_2,
    )


_drawn_inputs = setup_inputs


def setup_inputs(seed=0):
    import zlib

    import numpy as np

    out = dict(_drawn_inputs(seed))
    spreads = {}
    factors = {'norm_attn_g': 3.919,
     'rel_bias': 2.96,
     'delta_norm_g': 7.399,
     'norm_ffn_g': 4.03,
     'ctx_2': 8.0,
     'c_ctx_2': 2.881,
     'g_q_2': 8.0,
     'w_uq_2': 2.883,
     'g_kv_2': 8.0,
     'g_sgu_2': 3.536,
     'b_sgu_2': 3.76,
     's_pool_2': 2.739,
     'g_ffn2_2': 2.702}
    for name, (base, spread) in spreads.items():
        noise = np.random.default_rng([zlib.crc32(name.encode()), seed]).standard_normal(out[name].shape)
        drawn = base * np.exp(spread * noise) if base else spread * noise
        out[name] = jnp.asarray(drawn.astype(out[name].dtype))
    for name, factor in factors.items():
        out[name] = (out[name] * factor).astype(out[name].dtype)
    return out
```

```python
from contextlib import ExitStack
import math

import numpy as np

import concourse.bass as bass
from concourse import mybir

F32 = mybir.dt.float32
ALU = mybir.AluOpType
ACT = mybir.ActivationFunctionType
AX_X = mybir.AxisListType.X

P = 128
D = 1024
KT = D // P
SEQ = 512
CTX = 256
HD = 64
D_FF = 2816
FT = D_FF // P
CHUNK = 64
N_BUCKETS, MAX_DISTANCE = 32, 2048
EPS = 1e-6
MASKED = -1e30
COLS = 256
SLOTS = 5
HEADS1 = 8
HEADS2 = 4
Q_RANK, KV_RANK, ROPE = 192, 128, 32
GW = 256
N_MOD1, N_MOD2 = 6, 9
SKEW = 640


def shape_constants():
    c = {}
    eye = np.eye(P, dtype=np.float32)
    half = np.arange(P) // HD
    c["eye"] = eye
    c["head_ones"] = (half[:, None] == half[None, :]).astype(np.float32)
    e, t = np.arange(P)[:, None], np.arange(P)[None, :]
    same = e // CHUNK == t // CHUNK
    masks = [same & (e < t), same & (e <= t)]
    for level in range(6):
        n = 2 ** level
        masks.append((e // (2 * n) == t // (2 * n)) & (e // n % 2 == 1) & (t // n % 2 == 0))
    c["masks"] = np.stack(masks, 1).astype(np.float32)
    head_of_row = np.zeros((HEADS1, HEADS1 // 2, P), np.float32)
    for k in range(HEADS1 // 2):
        head_of_row[2 * k, k, :HD] = 1
        head_of_row[2 * k + 1, k, HD:] = 1
    c["pick_pair"] = head_of_row
    c["pick_head"] = np.repeat(np.eye(HEADS1, dtype=np.float32)[:, :, None], P, 2)
    d = 511 - np.arange(SKEW)
    dist = np.maximum(d, 0)
    exact = N_BUCKETS // 2
    f = np.maximum(dist, 1).astype(np.float32)
    large = exact + (np.log(f / exact) / math.log(MAX_DISTANCE / exact) * (N_BUCKETS - exact)).astype(np.int32)
    bucket = np.where(dist < exact, dist, np.minimum(large, N_BUCKETS - 1))
    count = (d <= 128).astype(int) + (d % 4 == 0) + (d % 16 == 0)
    seen = (d >= 0) & (count > 0) & (np.arange(SKEW) < 639)
    table = np.zeros((N_BUCKETS + 1, SKEW), np.float32)
    table[bucket[seen], np.arange(SKEW)[seen]] = 1
    table[N_BUCKETS] = np.where(seen, np.log(np.maximum(count, 1)), MASKED)
    c["distance"] = table
    a = 2 * np.pi / HD * (np.arange(HD)[:, None] * np.arange(HD)[None, :] % HD)
    c["head_dft"] = np.concatenate([np.tile(np.cos(a), (2, 1)), np.tile(-np.sin(a), (2, 1))], 1).astype(np.float32)
    for name, length in (("main", SEQ), ("ctx", CTX)):
        a = 2 * np.pi / length * (np.arange(length)[:, None] * np.arange(length)[None, :] % length)
        norm = 1 / math.sqrt(length * HD)
        both = np.stack([np.cos(a) * norm, np.sin(a) * norm], 1)
        both = both.reshape(length // P, P, 2, length).transpose(1, 2, 0, 3)
        c["token_dft_" + name] = both.astype(np.float32)
        t = np.arange(length)
        inv = []
        for w in (2, 4, 8, 16):
            lo, hi = np.clip(t - w // 2, 0, length), np.clip(t - w // 2 + w, 0, length)
            inv.append(np.tile((1 / (hi - lo)).astype(np.float32), (HD, 1)))
        c["pool_" + name] = np.stack([np.concatenate(inv[:2]), np.concatenate(inv[2:])], 1)
    inv = np.power(np.float32(10000.0), -np.arange(0, 16, 2, dtype=np.float32) / np.float32(16))
    t = np.arange(SEQ)
    pos = np.stack([t // 64, t % 64]).astype(np.float32)
    ang = (pos[:, :, None] * inv[None, None, :]).astype(np.float32)
    ang = np.broadcast_to(ang.transpose(0, 2, 1)[:, None], (2, 2, 8, SEQ)).reshape(ROPE, SEQ)
    c["rope"] = np.tile(np.stack([np.cos(ang), np.sin(ang)], 1), (4, 1, 1)).astype(np.float32)
    turn = np.zeros((P, P), np.float32)
    for m in range(P):
        if m // 8 % 2 == 0:
            turn[m + 8, m] = -1
        else:
            turn[m - 8, m] = 1
    c["turn"] = turn
    return c


class Lane:

    def __init__(self, sem):
        self.sem, self.count, self.steps = sem, 0, []

    def do(self, emit, after=()):
        self.count += 1
        self.steps.append((marks(after), emit, self.sem, 1))
        return (self.sem, self.count)

    def play(self, engine):
        seen = {}
        for waits, emit, sem, amount in self.steps:
            for s, value in waits:
                if seen.get(s.name, 0) < value:
                    engine.wait_ge(s, value)
                    seen[s.name] = value
            last = emit(engine)
            if last is not None:
                last.then_inc(sem, amount)


def marks(after):
    if after is None:
        return []
    if isinstance(after, tuple) and len(after) == 2 and isinstance(after[1], int):
        return [after]
    return [m for a in after for m in marks(a)]


class Counter:

    def __init__(self, sem):
        self.sem, self.count = sem, 0


class Bank:

    def __init__(self, ap):
        self.ap, self.free = ap, ()


class Turn:
    def __init__(self, banks):
        self.banks, self.n = banks, 0

    def next(self):
        b = self.banks[self.n % len(self.banks)]
        self.n += 1
        return b


class Part:

    def __init__(self, name, tokens, h, hn, col):
        self.name, self.T, self.h, self.hn, self.col = name, tokens, h, hn, col
        self.h_ready, self.hn_ready, self.hn_free = (), (), ()


class Program:
    def __init__(self, nc, ctx, inp, const, out):
        self.nc, self.inp, self.const, self.out = nc, inp, const, out
        self.ctx = ctx
        sem = lambda n: ctx.enter_context(nc.semaphore(n))
        self.pe, self.act, self.dve, self.pool, self.sp = (
            Lane(sem(n)) for n in ("pe_done", "act_done", "dve_done", "pool_done", "sp_unused"))
        self.slot_sems = [Counter(sem(f"slot{i}_landed")) for i in range(SLOTS)]
        self.misc_sems = [Counter(sem(f"misc{i}_landed")) for i in range(24)]
        self.misc_n = 0
        self.out_landed = Counter(sem("out_landed"))
        sb = lambda n, shape: ctx.enter_context(nc.sbuf_tensor(n, shape, F32))
        self.h_main = sb("h_main", [P, KT, SEQ])
        self.hn_main = sb("hn_main", [P, KT * SEQ])
        self.h_ctx = sb("h_ctx", [P, KT, CTX])
        self.arena = sb("arena", [P, 28672])
        self.ring = sb("ring", [P, SLOTS, KT * COLS])
        self.tmp = sb("tmp", [P, 4, SEQ])
        self.eye = sb("eye", [P, P])
        self.ones = sb("ones", [P, P])
        self.head_ones = sb("head_ones", [P, P])
        self.vec = sb("vec", [P, 3, P])
        self.mod1 = sb("mod1", [P, N_MOD1 * KT, 1])
        self.mod2 = sb("mod2", [P, N_MOD2 * KT, 2])
        self.cond = sb("cond", [P, KT, 3])
        self.gain = sb("gain", [P, KT, 3])
        self.small = sb("small", [P, 192])
        psum = ctx.enter_context(nc.psum_tensor("psum", [P, 8, 512], F32))
        self.ps = psum
        self.banks = Turn([Bank(psum[:, i, :]) for i in range(4)])
        self.mix = Turn([Bank(psum[:, i, :]) for i in range(4, 8)])
        self.slots = Turn([Bank(self.ring[:, i, :]) for i in range(SLOTS)])
        self.temps = Turn([Bank(self.tmp[:, i, :]) for i in range(4)])
        self.dram_writes = []
        self.w_free = ()
        self.skew = nc.dram_tensor("skew", (HEADS1, P * SKEW), F32, kind="Internal").ap()

    def everything(self):
        return [(l.sem, l.count) for l in (self.pe, self.act, self.dve, self.pool) if l.count] + \
            [(c.sem, c.count) for c in self.misc_sems if c.count]

    def dma(self, lane, out, in_, after=(), counter=None):
        if counter is None:
            counter = self.misc_sems[self.misc_n % len(self.misc_sems)]
            self.misc_n += 1
        before = [(counter.sem, counter.count)] if counter.count else []
        counter.count += 16
        lane.steps.append((marks([after, before]), lambda e: e.dma_start(out, in_), counter.sem, 16))
        return (counter.sem, counter.count)

    def mm(self, out, pairs, after=(), close=True, open_=True):
        def emit(e):
            for i, (a, b) in enumerate(pairs):
                last = e.matmul(out, a, b, start=open_ and i == 0, stop=close and i == len(pairs) - 1)
            return last
        return self.pe.do(emit, after)

    def transposes(self, triples, after=()):
        def emit(e):
            for out, in_, k in triples:
                last = e.transpose(out, in_, self.eye[0:k, 0:k])
            return last
        return self.pe.do(emit, after)

    def v(self, name, *args, after=(), lane=None, **kw):
        table = {
            "tt": lambda e: e.tensor_tensor(*args, **kw), "ts": lambda e: e.tensor_scalar(*args, **kw),
            "stt": lambda e: e.scalar_tensor_tensor(*args, **kw), "copy": lambda e: e.tensor_copy(*args),
            "recip": lambda e: e.reciprocal(*args), "max": lambda e: e.reduce_max(*args, AX_X),
            "sum": lambda e: e.reduce_sum(*args, AX_X), "set": lambda e: e.memset(*args),
            "ttr": lambda e: e.tensor_tensor_reduce(*args, **kw),
            "scan": lambda e: e.tensor_tensor_scan(*args, **kw)}
        return (lane or self.dve).do(table[name], after)

    def a(self, out, in_, func, after=(), **kw):
        return self.act.do(lambda e: e.activation(out, in_, func, **kw), after)

    def weights(self, w, k0, nk, c0, nc_, kp=P):
        slot = self.slots.next()
        counter = self.slot_sems[(self.slots.n - 1) % SLOTS]
        view = slot.ap[0:kp, 0:nk * nc_].rearrange("p (k n) -> p k n", k=nk)
        src = w[k0:k0 + nk * kp, c0:c0 + nc_].rearrange("(k p) n -> p k n", p=kp)
        landed = self.dma(self.sp, view, src, after=slot.free, counter=counter)
        return slot, view, landed

    def pieces(self, sources):
        slot = self.slots.next()
        counter = self.slot_sems[(self.slots.n - 1) % SLOTS]
        before = [(counter.sem, counter.count)] if counter.count else []
        views = []
        for at, kp, nk, cols, src in sources:
            view = slot.ap[0:kp, at:at + nk * cols].rearrange("p (k n) -> p k n", k=nk)
            dst = view if len(src.shape) == 3 else view.rearrange("p k (h n) -> p k h n", h=src.shape[2])
            for k in range(nk):
                counter.count += 16
                self.sp.steps.append((marks([slot.free, before]), lambda e, d=dst[:, k], s=src[:, k]: e.dma_start(d, s),
                                      counter.sem, 16))
            views.append(view)
        return slot, views, (counter.sem, counter.count)

    def linear(self, w, n_k, c0, width, parts, take, kp=P, tile=P):
        per = KT
        at = 0
        while at < width:
            cols = min(COLS, width - at)
            loads = [(k, min(per, n_k - k)) for k in range(0, n_k, per)]
            tiles = [(o, min(tile, cols - o)) for o in range(0, cols, tile)]
            held = {}
            for k, nk in loads:
                slot, view, landed = self.weights(w, k * kp, nk, c0 + at, cols, kp)
                for n, (x, T, x_ready) in enumerate(parts):
                    for o, m in tiles:
                        if k == 0:
                            held[n, o] = self.banks.next()
                        bank = held[n, o]
                        out = bank.ap[0:m, 0:T]
                        done = self.mm(out, [(view[:, i, o:o + m], x(k + i)) for i in range(nk)],
                                       [landed, x_ready, bank.free if k == 0 else ()],
                                       open_=k == 0, close=k + nk == n_k)
                        if k + nk == n_k:
                            take(n, (at + o) // tile, out, done, bank)
                slot.free = [done]
            at += cols

    def mean_square_root(self, tiles, T, ones, scale, after, rows=P):
        bank = self.mix.next()
        n = len(tiles)
        for i, x in enumerate(tiles):
            t = self.temps.next()
            sq = t.ap[0:rows, 0:T]
            m = self.v("tt", sq, x, x, ALU.mult, after=[after, t.free], lane=self.pool)
            done = self.pe.do(lambda e, i=i, sq=sq: e.matmul(bank.ap[:, 0:T], ones[0:rows, :], sq,
                                                             start=i == 0, stop=i == n - 1),
                              [m, bank.free if i == 0 else ()])
            t.free = [done]
        t = self.temps.next()
        root = t.ap[:, 0:T]
        m = self.v("ts", root, bank.ap[:, 0:T], scale, EPS, ALU.mult, ALU.add, after=[done, t.free])
        bank.free = [m]
        m = self.a(root, root, ACT.Sqrt, after=[m])
        m = self.v("recip", root, root, after=[m])
        return root, m, t

    def modulated_norm(self, part, gain, shift, after=()):
        T = part.T
        rinv, ready, t = self.mean_square_root([part.h[:, k, 0:T] for k in range(KT)], T, self.ones,
                                               1.0 / D, part.h_ready)
        for k in range(KT):
            m = self.v("tt", part.hn(k), part.h[:, k, 0:T], rinv, ALU.mult,
                       after=[ready, part.hn_free, part.h_ready, after])
            if shift is None:
                m = self.v("ts", part.hn(k), part.hn(k), gain[:, k, :], None, ALU.mult, after=[m])
            else:
                m = self.v("ts", part.hn(k), part.hn(k), gain[:, k, :], shift[:, k:k + 1], ALU.mult, ALU.add,
                           after=[m])
        t.free = [m]
        part.hn_ready = m
        return m

    def swiglu(self, parts, hidden, w_a, a0, w_b, b0, w_down, gate, after):
        gates = {}
        hid_ready = [None] * len(parts)
        at = 0
        while at < D_FF:
            cols = min(COLS, D_FF - at)
            slot_a, wa, landed_a = self.weights(w_a, 0, KT, a0 + at, cols)
            slot_b, wb, landed_b = self.weights(w_b, 0, KT, b0 + at, cols)
            for o in range(0, cols, P):
                for n, part in enumerate(parts):
                    T = part.T
                    bank_a, bank_b = self.banks.next(), self.banks.next()
                    ps_a, ps_b = bank_a.ap[:, 0:T], bank_b.ap[:, 0:T]
                    ma = self.mm(ps_a, [(wa[:, k, o:o + P], part.hn(k)) for k in range(KT)],
                                 [landed_a, part.hn_ready, bank_a.free])
                    mb = self.mm(ps_b, [(wb[:, k, o:o + P], part.hn(k)) for k in range(KT)],
                                 [landed_b, bank_b.free])
                    t = self.temps.next()
                    s = t.ap[:, 0:T]
                    m = self.a(s, ps_a, ACT.Sigmoid, after=[ma, t.free])
                    m = self.v("tt", s, s, ps_a, ALU.mult, after=[m])
                    bank_a.free = [m]
                    m = self.v("tt", hidden(n, (at + o) // P), s, ps_b, ALU.mult, after=[m, mb, after])
                    bank_b.free = t.free = [m]
                    hid_ready[n] = m
            slot_a.free = slot_b.free = [mb]
            at += cols
        for part in parts:
            part.hn_free = [mb]

        def take(n, f, ps, done, bank):
            part = parts[n]
            m = self.v("stt", part.h[:, f, 0:part.T], ps, gate(part)[:, f:f + 1], part.h[:, f, 0:part.T],
                       ALU.mult, ALU.add, after=[done, part.h_ready])
            bank.free = [m]
            gates[n] = m

        self.linear(w_down, FT, 0, D,
                    [(lambda k, n=n: hidden(n, k), part.T, hid_ready[n]) for n, part in enumerate(parts)], take)
        for n, part in enumerate(parts):
            part.h_ready = [gates[n]]

    def modulation(self, w, tiles, mod, rhs, ready, bias):
        width = rhs(0).shape[1]
        bank = self.mix.next()
        done = None
        for j0 in range(0, tiles, COLS // P):
            slot, view, landed = self.weights(w, 0, KT, j0 * P, COLS)
            for o in range(COLS // P):
                j = j0 + o
                done = self.mm(bank.ap[:, j * width:(j + 1) * width],
                               [(view[:, k, o * P:(o + 1) * P], rhs(k)) for k in range(KT)],
                               [landed, ready, bank.free if j == 0 else ()])
            slot.free = [done]
        ps = bank.ap[:, 0:tiles * width].rearrange("p (j w) -> p j w", w=width)
        for i in range(width):
            m = self.v("tt", mod[:, 0:tiles, i], ps[:, :, i], bias, ALU.add, after=[done])
        bank.free = [m]
        return m

    def sigmoid_times(self, out, x, after):
        t = self.temps.next()
        s = t.ap[:, 0:x.shape[1]]
        m = self.a(s, x, ACT.Sigmoid, after=[after, t.free])
        m = self.v("tt", out, x, s, ALU.mult, after=[m])
        t.free = [m]
        return m

    def setup(self):
        i = self.inp
        sp = self.sp
        rows = []
        self.col = {}
        stage = self.arena[:, 0:3 * P].rearrange("p (a n) -> p a n", a=3)

        def put(name, tile, row, ap):
            n = ap.shape[0]
            rows.append(self.dma(sp, stage[row:row + n, tile, :], ap))
            self.col[name] = (tile, row)

        def rows_of(ap):
            return ap.rearrange("(r p) -> r p", p=P)

        clear = self.v("set", stage, 0.0)
        rows.append(clear)

        def put_after(name, tile, row, ap):
            n = ap.shape[0]
            rows.append(self.dma(sp, stage[row:row + n, tile, 0:ap.shape[1]], ap, after=[clear]))
            self.col[name] = (tile, row)

        put = put_after
        put("norm_attn", 0, 0, rows_of(i["norm_attn_g"][0]))
        put("norm_ffn", 0, 8, rows_of(i["norm_ffn_g"][0]))
        put("final", 0, 16, rows_of(i["final_norm_g"]))
        put("b_ada", 0, 24, rows_of(i["b_ada"][0]))
        put("c", 0, 72, rows_of(i["c"][0]))
        put("conv", 0, 80, i["conv_w"][0].rearrange("j (r p) -> (j r) p", p=P))
        for l in range(2):
            t = 1 + l
            put(f"b_ada{l}", t, 0, rows_of(i["b_ada_2"][l]))
            put(f"g_ffn1{l}", t, 72, rows_of(i["g_ffn1_2"][l]))
            put(f"g_mix{l}", t, 80, rows_of(i["g_mix_2"][l]))
            put(f"g_ffn2{l}", t, 88, rows_of(i["g_ffn2_2"][l]))
            put(f"s_pool{l}", t, 96, rows_of(i["s_pool_2"][l]))
            put(f"g_sgu{l}", t, 98, i["g_sgu_2"][l].rearrange("(a b) d -> a (b d)", b=2))
            put(f"g_kv{l}", t, 100, rows_of(i["g_kv_2"][l]))
            put(f"g_q{l}", t, 101, i["g_q_2"][l].rearrange("(r p) -> r p", p=96))
        put("c2", 1, 103, rows_of(i["c_2"][0]))
        put("c_ctx", 1, 111, rows_of(i["c_ctx_2"]))
        put("final2", 1, 119, rows_of(i["g_final_2"]))
        eye = self.dma(sp, self.eye[:], self.const["eye"])
        hones = self.dma(sp, self.head_ones[:], self.const["head_ones"])
        ones = self.v("set", self.ones[:], 1.0)
        self.consts = [eye, hones, ones]
        bank = self.mix.next()
        m = self.transposes([(bank.ap[:, a * P:(a + 1) * P], stage[:, a, :], P) for a in range(3)],
                            [rows, eye, ones])
        m = self.v("copy", self.vec[:].rearrange("p a n -> p (a n)"), bank.ap[:, 0:3 * P], after=[m])
        bank.free = [m]
        self.vec_ready = m
        self.dt_bias, self.a_log = self.small[0:8, 0:1], self.small[0:8, 1:2]
        self.norm_g = self.small[:, 2:3]
        col = lambda ap: ap.rearrange("(n o) -> n o", o=1)
        self.small_ready = [self.dma(sp, self.dt_bias, col(i["dt_bias"][0])),
                            self.dma(sp, self.a_log, col(i["a_log"][0])),
                            self.dma(sp, self.norm_g[0:HD], col(i["delta_norm_g"][0])),
                            self.dma(sp, self.norm_g[HD:P], col(i["delta_norm_g"][0]))]
        for n, name in enumerate(("c", "c2", "c_ctx")):
            m = self.sigmoid_times(self.cond[:, :, n], self.column(name, KT), [self.vec_ready])
        self.cond_ready = m
        self.main = Part("main", SEQ, self.h_main, lambda k: self.hn_main[:, k * SEQ:(k + 1) * SEQ], 0)
        self.side = Part("ctx", CTX, self.h_ctx, None, 1)
        for part, src, at in ((self.main, i["x"][0], 1024), (self.side, i["ctx_2"][0], 1024 + 4096)):
            nt = part.T // P
            x = self.arena[:, at:at + nt * D].rearrange("p (a n) -> p a n", a=nt)
            landed = self.dma(sp, x, src.rearrange("(a p) n -> p a n", p=P))
            for k in range(KT):
                bank = self.mix.next()
                m = self.transposes([(bank.ap[:, a * P:(a + 1) * P], x[:, a, k * P:(k + 1) * P], P)
                                     for a in range(nt)], [landed, eye, bank.free])
                m = self.v("copy", part.h[:, k, :], bank.ap[:, 0:part.T], after=[m])
                bank.free = [m]
            part.h_ready = [m]

    def column(self, name, n, skip=0):
        tile, row = self.col[name]
        return self.vec[:, tile, row + skip:row + skip + n]

    def gains(self, slot, name, scale, after):
        return self.v("stt", self.gain[:, :, slot], scale, 1.0, self.column(name, KT), ALU.add, ALU.mult, after=after)

    def first_block(self):
        i, main = self.inp, self.main
        mod = self.mod1
        ready = self.modulation(i["w_ada"][0], N_MOD1 * KT, mod, lambda k: self.cond[:, k, 0:1],
                                [self.cond_ready], self.column("b_ada", N_MOD1 * KT))
        vec = lambda j: mod[:, j * KT:(j + 1) * KT, 0]
        g = self.gains(0, "norm_attn", vec(1), [ready])
        self.modulated_norm(main, self.gain[:, :, 0:1], vec(0), [g, ready])

        base = self.everything()
        A = self.arena
        off = [0]

        def take_region(n):
            off[0] += n
            return A[:, off[0] - n:off[0]]

        Y = take_region(8 * SEQ).rearrange("p (k t) -> p k t", k=8)
        DD = take_region(12 * SEQ).rearrange("p (k t) -> p k t", k=12)
        ZS = take_region(4 * SEQ).rearrange("p (k t) -> p k t", k=4)
        masks = take_region(8 * P).rearrange("p (m n) -> p m n", m=8)
        pick_pair = take_region(4 * P)[0:8].rearrange("p (m n) -> p m n", m=4)
        pick_head = take_region(8 * P)[0:8].rearrange("p (m n) -> p m n", m=8)
        spare = DD.rearrange("p k t -> p (k t)")
        table = spare[0:N_BUCKETS + 1, 2 * SKEW:3 * SKEW]
        shared = off[0]
        QA = take_region(4 * SEQ).rearrange("p (k t) -> p k t", k=4)
        KA = take_region(4 * SEQ).rearrange("p (k t) -> p k t", k=4)
        VA = take_region(4 * SEQ).rearrange("p (a n) -> p a n", a=4)
        PAD = SEQ + 3
        DX = take_region(12 * PAD).rearrange("p (k t) -> p k t", k=12)
        BT = take_region(SEQ)[0:8]
        AT = take_region(SEQ)[0:8]
        assert off[0] <= 28672, off[0]
        consts = [self.dma(self.sp, o, c, after=base) for o, c in (
            (masks, self.const["masks"]), (pick_pair, self.const["pick_pair"]),
            (pick_head, self.const["pick_head"]), (table, self.const["distance"]))]
        pads = self.v("set", DX[:, :, 0:3], 0.0, after=base)

        w = i["w_in"][0]
        hn = lambda k: main.hn(k)
        got = {}

        def take_qkz(n, f, ps, done, bank):
            if f < 4:
                m = self.a(QA[:, f, :], ps, ACT.Copy, after=[done, base], scale=HD ** -0.5)
            else:
                m = self.a(KA[:, f - 4, :], ps, ACT.Copy, after=[done, base])
            bank.free = got["qk"] = [m]

        self.linear(w, KT, 0, 1024, [(hn, SEQ, main.hn_ready)], take_qkz)
        for c in range(2):
            slot, view, landed = self.weights(w, 0, KT, 1024 + c * COLS, COLS)
            for a in range(4):
                bank = self.banks.next()
                done = self.mm(bank.ap[:, 0:COLS], [(hn(k)[:, a * P:(a + 1) * P], view[:, k, :]) for k in range(KT)],
                               [landed, main.hn_ready, bank.free])
                m = self.a(VA[:, a, c * COLS:(c + 1) * COLS], bank.ap[:, 0:COLS], ACT.Copy, after=[done, base])
                bank.free = got["v"] = [m]
            slot.free = [done]

        def take_conv(n, f, ps, done, bank):
            m = self.a(DX[:, f, 3:PAD], ps, ACT.Copy, after=[done, base])
            bank.free = got["conv"] = [m]

        self.linear(w, KT, 1536, 1536, [(hn, SEQ, main.hn_ready)], take_conv)

        def take_z(n, f, ps, done, bank):
            m = self.a(ZS[:, f, :], ps, ACT.Sigmoid, after=[done, base])
            m = self.v("tt", ZS[:, f, :], ZS[:, f, :], ps, ALU.mult, after=[m])
            bank.free = got["z"] = [m]

        self.linear(w, KT, 3072, 512, [(hn, SEQ, main.hn_ready)], take_z)

        def take_ba(n, f, ps, done, bank):
            if f == 0:
                m = self.a(BT, ps, ACT.Sigmoid, after=[done, base])
            else:
                m = self.a(AT, ps, ACT.Identity, after=[done, base, self.small_ready], bias=self.dt_bias)
            bank.free = [m]
            got["ba", f] = m

        self.linear(w, KT, 3584, 16, [(hn, SEQ, main.hn_ready)], take_ba, tile=8)

        after_proj = self.everything()
        E = self.hn_main[:].rearrange("p (h t) -> p h t", h=8)
        relb = DD[0:N_BUCKETS + 1, 6, 0:HEADS1]
        one = self.v("set", relb, 1.0, after=after_proj)
        rel = self.dma(self.sp, relb[0:N_BUCKETS], i["rel_bias"], after=[one])
        wide = DD[0:N_BUCKETS + 1, 4:6, :].rearrange("p a (h n) -> p (a h) n", n=P)
        wide_ready = self.v("copy", wide, relb.rearrange("p (h o) -> p h o", o=1).broadcast_to([N_BUCKETS + 1, HEADS1, P]),
                            after=[one, rel])
        Rb = [spare[:, b * SKEW:(b + 1) * SKEW] for b in range(2)]
        rb_free = [(), ()]
        skew_dram = self.skew
        e_ready = []
        for h in range(HEADS1):
            r = Rb[h % 2]
            for o, n in ((0, 512), (512, SKEW - 512)):
                bank = self.mix.next()
                done = self.mm(bank.ap[:, 0:n], [(wide[:, h, :], table[:, o:o + n])],
                               [wide_ready, consts, bank.free])
                m = self.v("copy", r[:, o:o + n], bank.ap[:, 0:n], after=[done, rb_free[h % 2], after_proj])
                bank.free = [m]
            wrote = self.dma(self.sp, skew_dram[h, :].rearrange("(p n) -> p n", p=P), r, after=[m])
            self.dram_writes.append(wrote)
            rb_free[h % 2] = [wrote]
            src = bass.AP(skew_dram.tensor, h * P * SKEW + 127, [[SKEW - 1, P], [1, SEQ]])
            e_ready.append(self.dma(self.sp, E[:, h, :], src, after=[wrote]))

        table_used = done
        PT = Turn([Bank(DD[:, 4 * b:4 * b + 4, :]) for b in (1, 2)])
        mx, sm = self.small[:, 32:64], self.small[:, 64:96]
        for h in range(HEADS1):
            k_, po = h // 2, HD * (h % 2)
            pt = PT.next()
            for qt in range(4):
                n = (qt + 1) * P
                bank = self.mix.next()
                done = self.mm(bank.ap[:, 0:n], [(QA[po:po + HD, k_, qt * P:(qt + 1) * P], KA[po:po + HD, k_, 0:n])],
                               [got["qk"], bank.free])
                s = self.temps.next()
                sc = s.ap[:, 0:n]
                c = 4 * h + qt
                m = self.v("ttr", sc, bank.ap[:, 0:n], E[:, h, (3 - qt) * P:SEQ], 1.0, -3e38, ALU.add, ALU.max,
                           mx[:, c:c + 1], after=[done, s.free, e_ready[h]])
                bank.free = [m]
                m = self.v("ts", mx[:, c:c + 1], mx[:, c:c + 1], -1.0, None, ALU.mult, after=[m])
                m = self.a(sc, sc, ACT.Exp, after=[m], bias=mx[:, c:c + 1], accum_out=sm[:, c:c + 1])
                m = self.v("recip", sm[:, c:c + 1], sm[:, c:c + 1], after=[m])
                m = self.v("ts", sc, sc, sm[:, c:c + 1], None, ALU.mult, after=[m])
                bank = self.mix.next()
                done = self.transposes([(bank.ap[:, a * P:(a + 1) * P], sc[:, a * P:(a + 1) * P], P)
                                        for a in range(qt + 1)], [m, bank.free])
                s.free = [done]
                m = self.a(pt.ap[:, 0:qt + 1, qt * P:(qt + 1) * P],
                           bank.ap[:, 0:n].rearrange("p (a q) -> p a q", q=P), ACT.Copy, after=[done, pt.free, table_used])
                bank.free = [m]
            bank = self.mix.next()

            def emit(e, pt=pt, bank=bank, h=h, po=po):
                for a in range(4):
                    last = e.matmul(bank.ap[po:po + HD, a * P:SEQ], VA[:, a, h * HD:(h + 1) * HD],
                                    pt.ap[:, a, a * P:SEQ], start=a == 0, stop=a == 3)
                return last
            done = self.pe.do(emit, [m, got["v"], bank.free])
            pt.free = [done]
            m = self.v("copy", Y[po:po + HD, k_, :], bank.ap[po:po + HD, :], after=[done, base])
            bank.free = [m]
        attn_done = m

        before = self.everything()
        cw = lambda j, f: self.column("conv", 1, skip=12 * j + f)
        for f in range(12):
            m = self.v("ts", DD[:, f, :], DX[:, f, 0:SEQ], cw(0, f), None, ALU.mult, after=[before, pads])
            for j in range(1, 4):
                m = self.v("stt", DD[:, f, :], DX[:, f, j:j + SEQ], cw(j, f), DD[:, f, :], ALU.mult, ALU.add, after=[m])
            t = self.temps.next()
            s = self.a(t.ap, DD[:, f, :], ACT.Sigmoid, after=[m, t.free, before])
            m = self.v("tt", DD[:, f, :], DD[:, f, :], t.ap, ALU.mult, after=[s])
            t.free = [m]
        conv_done = m
        for f in range(8):
            rinv, ready, t = self.mean_square_root([DD[:, f, :]], SEQ, self.head_ones, 1.0, [conv_done])
            m = self.v("stt", DD[:, f, :], DD[:, f, :], HD ** -0.5 if f < 4 else 1.0, rinv, ALU.mult, ALU.mult,
                       after=[ready])
            t.free = [m]
        unit = m

        space = shared
        region = {}

        def reuse(name, n):
            nonlocal space
            region[name] = A[:, space:space + n]
            space += n
            return region[name]

        QKT = reuse("QKT", 8 * SEQ).rearrange("p (h t) -> p h t", h=8)
        VB = reuse("VB", 4 * SEQ).rearrange("p (a n) -> p a n", a=4)
        KBE = reuse("KBE", 4 * SEQ).rearrange("p (a n) -> p a n", a=4)
        KD = reuse("KD", 4 * SEQ).rearrange("p (a n) -> p a n", a=4)
        rows = A[0:8, space:space + 4 * SEQ].rearrange("p (r t) -> p r t", r=4)
        assert space + 4 * SEQ <= off[0] - 2 * SEQ
        G, EG, KDr, BE = (rows[:, n, :] for n in range(4))
        X1, RS = KDr, BE
        reset = self.v("set", RS, 1.0, after=[conv_done])
        reset = self.v("set", RS.rearrange("p (n c) -> p n c", c=CHUNK)[:, :, 0:1], 0.0, after=[reset])
        m = self.a(X1, AT, ACT.Abs, after=[got["ba", 1], conv_done])
        m = self.a(X1, X1, ACT.Exp, after=[m], scale=-1.0)
        m = self.a(X1, X1, ACT.Ln, after=[m], bias=1.0)
        m = self.v("stt", X1, AT, 0.0, X1, ALU.max, ALU.add, after=[m])
        ea = self.a(self.a_log, self.a_log, ACT.Exp, after=[self.small_ready])
        m = self.v("ts", X1, X1, self.a_log, -1.0, ALU.mult, ALU.mult, after=[m, ea])
        m = self.v("scan", G, RS, X1, 0.0, ALU.mult, ALU.add, after=[m, reset])
        g_ready = m
        eg_ready = self.a(EG, G, ACT.Exp, after=[m])
        g3, x3 = (t.rearrange("p (n c) -> p n c", c=CHUNK) for t in (G, KDr))
        m = self.v("tt", x3, g3[:, :, CHUNK - 1:CHUNK].broadcast_to([8, 8, CHUNK]), g3, ALU.subtract, after=[m])
        kd_ready = self.a(KDr, KDr, ACT.Exp, after=[m])
        be_ready = self.v("tt", BE, BT, EG, ALU.mult, after=[eg_ready, got["ba", 0]])
        bank = self.mix.next()
        kinds = (G, BT, BE, KDr)
        done = self.transposes([(bank.ap[:, (a * 4 + n) * 8:(a * 4 + n + 1) * 8], r[:, a * P:(a + 1) * P], 8)
                                for a in range(4) for n, r in enumerate(kinds)],
                               [g_ready, kd_ready, be_ready, bank.free])
        TM = self.small[:, 32:160].rearrange("p (a k h) -> p a k h", a=4, k=4)
        tm_ready = self.v("copy", self.small[:, 32:160], bank.ap[:, 0:128], after=[done])
        bank.free = [tm_ready]

        after_conv = [unit]
        for a in range(4):
            for which in (4, 8):
                bank = self.mix.next()
                done = self.transposes([(bank.ap[:, f * P:(f + 1) * P], DD[:, which + f, a * P:(a + 1) * P], P)
                                        for f in range(4)], [after_conv, bank.free])
                src = bank.ap.rearrange("p (h d) -> p h d", h=8)
                outs = ((VB, 1),) if which == 8 else ((KBE, 2), (KD, 3))
                for dst, kind in outs:
                    m = self.v("tt", dst[:, a, :].rearrange("p (h d) -> p h d", h=8), src,
                               TM[:, a, kind, :].rearrange("p (h o) -> p h o", o=1).broadcast_to([P, 8, HD]),
                               ALU.mult, after=[done, tm_ready])
                bank.free = [m]
        tok_ready = m

        Ws = self.hn_main[:].rearrange("p (b t) -> p b t", b=8)
        EGL = self.small[:, 160:192].rearrange("p (k n) -> p k n", k=4)
        UU, WT = DD[:, 8:12, :], DD[:, 4:8, :]
        for pair in range(4):
            B_, U_, T_, W_ = (Ws[:, 2 * n:2 * n + 2, :] for n in range(4))
            bank = self.mix.next()
            done = self.mm(bank.ap, [(pick_pair[:, pair, :], BT)], [got["ba", 0], consts, bank.free])
            t = self.temps.next()
            kb = self.v("tt", t.ap, DD[:, 4 + pair, :], bank.ap, ALU.mult, after=[done, unit, t.free])
            bank.free = [kb]
            for o in range(2):
                h, po = 2 * pair + o, HD * o
                bank = self.mix.next()
                done = self.mm(bank.ap, [(pick_head[:, h, :], G)], [g_ready, bank.free])
                dec = W_[:, o, :]
                for a in range(4):
                    m = self.v("ts", dec[:, a * P:(a + 1) * P], bank.ap[:, a * P:(a + 1) * P],
                               TM[:, a, 0, h:h + 1], 0.0, ALU.subtract, ALU.min, after=[done, tm_ready, self.w_free])
                bank.free = [m]
                m = self.a(dec, dec, ACT.Exp, after=[m])
                for dst, rhs, mask in ((B_[:, o, :], t.ap, 0), (QKT[:, h, :], DD[:, pair, :], 1)):
                    bank = self.mix.next()

                    def emit(e, bank=bank, rhs=rhs, po=po, pair=pair):
                        for a in range(4):
                            last = e.matmul(bank.ap[:, a * P:(a + 1) * P], DD[po:po + HD, 4 + pair, a * P:(a + 1) * P],
                                            rhs[po:po + HD, a * P:(a + 1) * P], start=True, stop=True)
                        return last
                    done = self.pe.do(emit, [kb, unit, bank.free])
                    d = self.v("tt", dst, bank.ap, dec, ALU.mult, after=[done, m])
                    bank.free = [d]
                    d = self.v("tt", dst.rearrange("p (a c) -> p a c", a=4), dst.rearrange("p (a c) -> p a c", a=4),
                               masks[:, mask:mask + 1, :].broadcast_to([P, 4, P]), ALU.mult, after=[d], lane=self.pool)
                t_used = done
            t.free = [t_used]
            self.w_free = [d]
            four = lambda x: x.rearrange("p o (a c) -> p o a c", a=4)
            flat8 = lambda x: x.rearrange("p o (a c) -> p (o a) c", c=P)
            eye8 = self.eye[:].rearrange("p (o n) -> p o n", o=1).broadcast_to([P, 8, P])
            mu = self.v("copy", flat8(U_), eye8, after=[self.w_free], lane=self.pool)
            mt = self.v("copy", flat8(T_), eye8, after=[self.w_free], lane=self.pool)
            prev = [mu, mt, d]
            for level in range(6):
                def product(lhs, rhs, after):
                    out = []
                    for o in range(2):
                        bank = self.mix.next()

                        def emit(e, bank=bank, o=o):
                            for a in range(4):
                                c = slice(a * P, (a + 1) * P)
                                last = e.matmul(bank.ap[:, c], lhs[:, o, c], rhs[:, o, c], start=True, stop=True)
                            return last
                        out.append((bank, self.pe.do(emit, [after, bank.free])))
                    return out
                now = []
                for o, (bank, done) in enumerate(product(B_, T_, prev)):
                    m = self.v("tt", W_[:, o, :].rearrange("p (a c) -> p a c", a=4),
                               bank.ap.rearrange("p (a c) -> p a c", a=4),
                               masks[:, 2 + level:3 + level, :].broadcast_to([P, 4, P]), ALU.mult, after=[done, prev])
                    bank.free = [m]
                    now.append(m)
                u_new = product(W_, U_, now)
                t_new = product(U_, W_, now) if level < 5 else []
                prev = []
                for o, (bank, done) in enumerate(u_new):
                    m = self.v("tt", U_[:, o, :], U_[:, o, :], bank.ap, ALU.subtract,
                               after=[done, t_new[-1][1] if t_new else u_new[-1][1]])
                    bank.free = [m]
                    prev.append(m)
                for o, (bank, done) in enumerate(t_new):
                    m = self.v("tt", T_[:, o, :], T_[:, o, :], bank.ap, ALU.subtract, after=[done])
                    bank.free = [m]
                    prev.append(m)
            bank_u, bank_w = self.mix.next(), self.mix.next()

            def emit(e, bank=bank_u, U_=U_, pair=pair):
                for a in range(4):
                    for o in range(2):
                        last = e.matmul(bank.ap[:, (a * 2 + o) * HD:(a * 2 + o + 1) * HD], U_[:, o, a * P:(a + 1) * P],
                                        VB[:, a, (2 * pair + o) * HD:(2 * pair + o + 1) * HD], start=True, stop=True)
                return last
            done = self.pe.do(emit, [prev, tok_ready, bank_u.free])
            m1 = self.v("copy", UU[:, :, 2 * pair * HD:2 * (pair + 1) * HD], bank_u.ap.rearrange("p (a n) -> p a n", a=4),
                        after=[done])
            bank_u.free = [m1]

            def emit(e, bank=bank_w, U_=U_, pair=pair):
                for a in range(4):
                    for o in range(2):
                        last = e.matmul(bank.ap[HD * o:HD * (o + 1), a * P:(a + 1) * P],
                                        KBE[:, a, (2 * pair + o) * HD:(2 * pair + o + 1) * HD],
                                        U_[:, o, a * P:(a + 1) * P], start=True, stop=True)
                return last
            done = self.pe.do(emit, [bank_w.free])
            m2 = self.v("copy", WT[:, pair, :], bank_w.ap, after=[done])
            bank_w.free = [m2]
            bank = self.mix.next()
            done = self.mm(bank.ap, [(pick_pair[:, pair, :], EG)], [eg_ready, bank.free])
            m3 = self.v("tt", DD[:, pair, :], DD[:, pair, :], bank.ap, ALU.mult, after=[done, t_used])
            m4 = self.v("copy", EGL[:, pair, :], bank.ap.rearrange("p (n c) -> p n c", c=CHUNK)[:, :, CHUNK - 1],
                        after=[done, tm_ready])
            bank.free = [m4]
            self.w_free = [done]
        S = self.tmp[:, 0, 0:256].rearrange("p (k n) -> p k n", k=4)
        SG = self.tmp[:, 0, 256:512].rearrange("p (k n) -> p k n", k=4)
        VN = self.tmp[:, 1, :].rearrange("p (o k n) -> p o k n", o=2, k=4)
        s_ready = self.v("set", self.tmp[:, 0, :], 0.0, after=self.everything())
        vn_free = self.everything()
        self.scan_banks = [(self.banks.banks[0], self.banks.banks[1]), (self.banks.banks[2], self.banks.banks[3])]
        for n in range(SEQ // CHUNK):
            a, p0 = n // 2, CHUNK * (n % 2)
            c = slice(n * CHUNK, (n + 1) * CHUNK)
            bank_v = [self.mix.next(), self.mix.next()]
            bank_o, bank_s = self.scan_banks[n % 2]
            heads = [(h, h // 2, HD * (h % 2)) for h in range(8)]

            def emit(e, bank=bank_v, p0=p0, a=a, c=c, n=n):
                for h, k, po in heads:
                    last = e.matmul(bank[h % 2].ap[p0:p0 + CHUNK, k * HD:(k + 1) * HD], WT[po:po + HD, k, c],
                                    S[po:po + HD, k, :], start=True, stop=True)
                return last
            done_v = self.pe.do(emit, [s_ready, bank_v[0].free, bank_v[1].free, m4, m2])
            vn = []
            for o in range(2):
                u = UU[p0:p0 + CHUNK, a, :].rearrange("p (k o n) -> p o k n", o=2, n=HD)[:, o]
                vn.append(self.v("tt", VN[p0:p0 + CHUNK, o], u,
                                 bank_v[o].ap[p0:p0 + CHUNK, 0:256].rearrange("p (k n) -> p k n", k=4), ALU.subtract,
                                 after=[done_v, vn_free]))
                bank_v[o].free = [vn[-1]]
            sg = self.v("tt", SG, S, EGL[:, :, n:n + 1].broadcast_to([P, 4, HD]), ALU.mult, after=[s_ready, m4], lane=self.pool)

            def emit(e, bank=bank_s, p0=p0, a=a, c=c, n=n):
                for h, k, po in heads:
                    last = e.matmul(bank.ap[po:po + HD, k * HD:(k + 1) * HD], KD[p0:p0 + CHUNK, a, h * HD:(h + 1) * HD],
                                    VN[p0:p0 + CHUNK, h % 2, k, :], start=True, stop=True)
                return last
            done_s = self.pe.do(emit, [vn, bank_s.free])

            def emit(e, bank=bank_o, p0=p0, a=a, c=c, n=n):
                for h, k, po in heads:
                    last = e.matmul(bank.ap[po:po + HD, k * HD:(k + 1) * HD], S[po:po + HD, k, :], DD[po:po + HD, k, c],
                                    start=k == 0, stop=False, skip_group_check=True)
                return last
            done_q = self.pe.do(emit, [s_ready, m3, m4, bank_o.free])

            def emit(e, bank=bank_o, p0=p0, a=a, c=c, n=n):
                for h, k, po in heads:
                    last = e.matmul(bank.ap[po:po + HD, k * HD:(k + 1) * HD], VN[p0:p0 + CHUNK, h % 2, k, :],
                                    QKT[p0:p0 + CHUNK, h, n * CHUNK:(n + 1) * CHUNK], start=False, stop=True,
                                    skip_group_check=True)
                return last
            done_o = self.pe.do(emit, [vn, done_q])
            s_ready = self.v("tt", S, SG, bank_s.ap[:, 0:256].rearrange("p (k n) -> p k n", k=4), ALU.add,
                             after=[done_s, done_o, sg])
            bank_s.free = [s_ready]
            m = self.a(Y[:, 4:8, c], bank_o.ap[:, 0:256].rearrange("p (k n) -> p k n", k=4), ACT.Copy, after=[done_o, base])
            bank_o.free = [m]
            vn_free = [done_o]
        self.temps.banks[0].free = self.temps.banks[1].free = self.everything()
        o_ready = m
        for f in range(4):
            rinv, ready, t = self.mean_square_root([Y[:, 4 + f, :]], SEQ, self.head_ones, 1.0 / HD, [o_ready])
            m = self.v("tt", rinv, rinv, ZS[:, f, :], ALU.mult, after=[ready, got["z"]])
            m = self.v("stt", Y[:, 4 + f, :], Y[:, 4 + f, :], self.norm_g, rinv, ALU.mult, ALU.mult, after=[m, self.small_ready])
            t.free = [m]
        y_ready = [m, attn_done]

        def take_out(n, f, ps, done, bank):
            m = self.v("stt", main.h[:, f, :], ps, vec(2)[:, f:f + 1], main.h[:, f, :], ALU.mult, ALU.add, after=[done])
            bank.free = main_h[0] = [m]
        main_h = [()]
        self.linear(i["w_out"][0], KT, 0, D, [(lambda k: Y[:, k, :], SEQ, y_ready)], take_out)
        main.h_ready = main_h[0]

        g = self.gains(0, "norm_ffn", vec(4), [ready])
        main.hn_free = self.everything()
        self.modulated_norm(main, self.gain[:, :, 0:1], vec(3), [g])
        hidden = A[:, 0:FT * SEQ].rearrange("p (k t) -> p k t", k=FT)
        self.swiglu([main], lambda n, k: hidden[:, k, :], i["w_gate"][0], 0, i["w_up"][0], 0, i["w_down"][0],
                    lambda part: vec(5), self.everything())
        self.plain_norm(main, "final")

    def plain_norm(self, part, name):
        T = part.T
        rinv, ready, t = self.mean_square_root([part.h[:, k, 0:T] for k in range(KT)], T, self.ones, 1.0 / D, part.h_ready)
        for k in range(KT):
            m = self.v("stt", part.h[:, k, 0:T], part.h[:, k, 0:T], self.column(name, 1, skip=k), rinv, ALU.mult, ALU.mult,
                       after=[ready])
        t.free = [m]
        part.h_ready = [m]

    def half_step(self, parts, layer, names, first, hidden, mod_ready):
        mod = self.mod2
        rows = lambda j, c: mod[:, j * KT:(j + 1) * KT, c]
        for part in parts:
            g = self.gains(part.col, f"{names}{layer}", rows(first + 1, part.col), [mod_ready])
            self.modulated_norm(part, self.gain[:, :, part.col:part.col + 1], rows(first, part.col), [g])
        half = {}
        for part in parts:
            half[part.name] = self.small[:, part.col * KT:(part.col + 1) * KT]
            m = self.v("ts", half[part.name], rows(first + 2, part.col), 0.5, None, ALU.mult, after=[mod_ready])
            part.h_ready = [part.h_ready, m]
        w13, w2 = self.inp[f"w13_{names[2:]}_2"][layer], self.inp[f"w2_{names[2:]}_2"][layer]
        self.swiglu(parts, hidden, w13, 0, w13, D_FF, w2, lambda part: half[part.name], self.everything())

    def gelu(self, x, ready):
        t = self.temps.next()
        u = t.ap[:, 0:x.shape[1]]
        c = 2 * math.sqrt(2 / math.pi)
        m = self.v("tt", u, x, x, ALU.mult, after=[ready, t.free], lane=self.pool)
        m = self.v("ts", u, u, 0.044715 * c, c, ALU.mult, ALU.add, after=[m])
        m = self.v("tt", u, u, x, ALU.mult, after=[m], lane=self.pool)
        m = self.a(u, u, ACT.Sigmoid, after=[m])
        m = self.v("tt", x, x, u, ALU.mult, after=[m])
        t.free = [m]
        return m

    def pair_of_banks(self):
        if self.mix.n % 2:
            self.mix.next()
        first, second = self.mix.next(), self.mix.next()
        i = 4 + (self.mix.n - 2) % 4
        return first, second, self.ps[:, i:i + 2, :].rearrange("p a n -> p (a n)")

    def mixers(self, part, layer, kv_only, mod_ready):
        i, T, A, name = self.inp, part.T, self.arena, part.name
        nt = T // P
        w_in = i["w_in_2"][layer]
        mod = self.mod2
        rows = lambda j: mod[:, j * KT:(j + 1) * KT, part.col]
        g = self.gains(part.col, f"g_mix{layer}", rows(4), [mod_ready])
        self.modulated_norm(part, self.gain[:, :, part.col:part.col + 1], rows(3), [g])
        base = self.everything()
        off = [0]

        def take(n):
            off[0] += n
            assert off[0] <= 28672 - (2048 if part.col else 0), off[0]
            return A[:, off[0] - n:off[0]]

        keys = SEQ + CTX
        own = 0 if name == "main" else SEQ
        KN = take(2 * keys).rearrange("p (k t) -> p k t", k=2)
        KR = take(keys)
        VT = take(keys // P * GW).rearrange("p (a n) -> p a n", n=GW)
        CKV = take(T)
        if not kv_only:
            CQ = take(2 * T)[0:96].rearrange("p (k t) -> p k t", k=2)
            QN = take(2 * T).rearrange("p (k t) -> p k t", k=2)
            QR = take(T)
            F_ = take(2 * T).rearrange("p (k t) -> p k t", k=2)
            U_ = take(2 * T).rearrange("p (k t) -> p k t", k=2)
            V_ = take(nt * GW).rearrange("p (a n) -> p a n", n=GW)
            PZ = take(2 * (T + 16)).rearrange("p (k t) -> p k t", k=2)
            Y = take(8 * T).rearrange("p (k t) -> p k t", k=8)
            head_dft, turn = take(P), take(P)
            inv = take(2 * T).rearrange("p (k t) -> p k t", k=2)
            wf, wp = (take(2 * HD).rearrange("p (k n) -> p k n", k=2) for _ in range(2))
            R_ = take(2 * P).rearrange("p (k n) -> p k n", k=2)
            WST = take(HEADS2 * P).rearrange("p (h n) -> p h n", h=HEADS2)
            BB = take(2 * P).rearrange("p (k n) -> p k n", k=2)
            rope = take(2 * SEQ).rearrange("p (c t) -> p c t", c=2)
            scores = Turn([Bank(take(keys)) for _ in range(2)])
            spare = take(2 * 6 * T)
            PT = Turn([Bank(spare[:, n * 6 * T:(n + 1) * 6 * T].rearrange("p (a t) -> p a t", a=6)) for n in range(2)])
            raw_ws = spare[:, 0:HEADS2 * P].rearrange("p (h n) -> p h n", h=HEADS2)
            YT = spare[:, 512:512 + nt * 512].rearrange("p (a n) -> p a n", a=nt)
            sums = [spare[:, 512 * (1 + nt) + n * (T + 16):512 * (1 + nt) + (n + 1) * (T + 16)] for n in range(2)]
            assert 512 * (1 + nt) + 2 * (T + 16) <= 12 * T
        sp = self.sp

        def section(c0, width, tile, put):
            self.linear(w_in, KT, c0, width, [(part.hn, T, part.hn_ready)], put, tile=tile)

        got = {}

        def copy_to(dst, key):
            def put(n, f, ps, done, bank):
                m = self.a(dst(f), ps, ACT.Copy, after=[done, base])
                bank.free = [m]
                got[key] = m
            return put

        section(448, KV_RANK, P, copy_to(lambda f: CKV, "ckv"))
        src = w_in[:, 576:576 + ROPE].rearrange("(k p) (o n) -> p k o n", p=P, o=1)
        slot = self.slots.next()
        counter = self.slot_sems[(self.slots.n - 1) % SLOTS]
        before = [(counter.sem, counter.count)] if counter.count else []
        view = slot.ap[:, 0:KT * P].rearrange("p (k n) -> p k n", k=KT)
        by_copy = slot.ap[:, 0:KT * P].rearrange("p (k o n) -> p k o n", k=KT, o=HEADS2)
        for o in range(HEADS2):
            counter.count += 16
            self.sp.steps.append((marks([slot.free, before]),
                                  lambda e, d=by_copy[:, :, o], s=src[:, :, 0]: e.dma_start(d, s), counter.sem, 16))
        landed = (counter.sem, counter.count)
        bank = self.banks.next()
        done = self.mm(bank.ap[:, 0:T], [(view[:, k, :], part.hn(k)) for k in range(KT)],
                       [landed, part.hn_ready, bank.free])
        slot.free = [done]
        m = self.a(KR[:, own:own + T], bank.ap[:, 0:T], ACT.Copy, after=[done, base])
        bank.free = [m]
        kr_ready = m
        if not kv_only:
            loads = [self.dma(sp, o, c, after=base) for o, c in (
                (head_dft, self.const["head_dft"]), (turn, self.const["turn"]), (inv, self.const["pool_" + name]),
                (rope, self.const["rope"]),
                (raw_ws, i["w_sgu_2"][layer].rearrange("h p q -> p h q")))]
            for h in range(HEADS2):
                half = slice(HD * (h % 2), HD * (h % 2 + 1))
                loads.append(self.dma(sp, wf[half, h // 2, :], i["w_fnet_2"][layer, h], after=base))
                loads.append(self.dma(sp, wp[half, h // 2, :], i["w_pool_2"][layer, h], after=base))
                b = i["b_sgu_2"][layer, h]
                loads.append(self.dma(sp, BB[half, h // 2, :], bass.AP(b.tensor, b.offset, [[0, HD], [1, P]]), after=base))
            pads = self.v("set", PZ, 0.0, after=base, lane=self.pool)
            section(256, Q_RANK, 96, copy_to(lambda f: CQ[:, f, :], "cq"))
            section(0, GW, P, copy_to(lambda f: F_[:, f, :], "f"))

            def put_u(n, f, ps, done, bank):
                m = self.a(U_[:, f, :], ps, ACT.Copy, after=[done, base])
                bank.free = [m]
                got["u"] = self.gelu(U_[:, f, :], [m])
            section(608, GW, P, put_u)
            slot, view, landed = self.weights(w_in, 0, KT, 864, GW)
            for a in range(nt):
                bank = self.banks.next()
                done = self.mm(bank.ap[:, 0:GW], [(part.hn(k)[:, a * P:(a + 1) * P], view[:, k, :]) for k in range(KT)],
                               [landed, part.hn_ready, bank.free])
                m = self.a(V_[:, a, :], bank.ap[:, 0:GW], ACT.Copy, after=[done, base])
                bank.free = [m]
                got["v"] = self.gelu(V_[:, a, :], [m])
            slot.free = [done]

            def put_p(n, f, ps, done, bank):
                m = self.a(PZ[:, f, 8:8 + T], ps, ACT.Copy, after=[done, pads])
                bank.free = [m]
                got["p"] = m
            section(1120, GW, P, put_p)
            part.hn_free = [done, self.everything()]

        def rank_norm(tiles, rows_, gain, ready):
            rinv, m, t = self.mean_square_root(tiles, T, self.ones, 1.0 / (rows_ * len(tiles)), [ready], rows=rows_)
            for f, x in enumerate(tiles):
                last = self.v("stt", x, x, self.column(gain, 1, skip=f)[0:rows_], rinv[0:rows_], ALU.mult, ALU.mult, after=[m])
            t.free = [last]
            return last

        kv_ready = rank_norm([CKV], P, f"g_kv{layer}", got["ckv"])
        src = i["w_ukv_2"][layer].rearrange("(k p) (h n) -> p k h n", p=P, h=HEADS2)
        slot, (w_k, w_v), landed = self.pieces([(0, P, 1, GW, src[:, :, :, 0:HD]), (GW, P, 1, GW, src[:, :, :, HD:2 * HD])])
        for k in range(2):
            bank = self.mix.next()
            done = self.mm(bank.ap[:, 0:T], [(w_k[:, 0, k * P:(k + 1) * P], CKV)], [landed, kv_ready, bank.free])
            m = self.a(KN[:, k, own:own + T], bank.ap[:, 0:T], ACT.Copy, after=[done, base])
            bank.free = [m]
        kn_ready = m
        for a in range(nt):
            bank = self.mix.next()
            done = self.mm(bank.ap[:, 0:GW], [(CKV[:, a * P:(a + 1) * P], w_v[:, 0, :])], [bank.free])
            m = self.a(VT[:, own // P + a, :], bank.ap[:, 0:GW], ACT.Copy, after=[done, base])
            bank.free = [m]
        slot.free = [done]
        vt_ready = m
        if name == "main":
            kr_ready = self.turned(KR[:, 0:T], turn, rope, [kr_ready, loads])
        part.kv = [kn_ready, vt_ready, kr_ready]
        if kv_only:
            return
        q_ready = rank_norm([CQ[:, 0, :], CQ[:, 1, :]], 96, f"g_q{layer}", got["cq"])
        src = i["w_uq_2"][layer].rearrange("(k p) (h n) -> p k h n", p=96, h=HEADS2)
        slot, (w_nope, w_rope), landed = self.pieces([(0, 96, 2, GW, src[:, :, :, 0:HD]),
                                                      (2 * GW, 96, 2, P, src[:, :, :, HD:HD + ROPE])])
        for k in range(2):
            bank = self.mix.next()
            done = self.mm(bank.ap[:, 0:T], [(w_nope[:, n, k * P:(k + 1) * P], CQ[:, n, :]) for n in range(2)],
                           [landed, q_ready, bank.free])
            m = self.a(QN[:, k, :], bank.ap[:, 0:T], ACT.Copy, after=[done, base])
            bank.free = [m]
        qn_ready = m
        bank = self.mix.next()
        done = self.mm(bank.ap[:, 0:T], [(w_rope[:, n, :], CQ[:, n, :]) for n in range(2)], [bank.free])
        slot.free = [done]
        qr_ready = self.a(QR, bank.ap[:, 0:T], ACT.Copy, after=[done, base])
        bank.free = [qr_ready]
        if name == "main":
            qr_ready = self.turned(QR, turn, rope, [qr_ready, loads])

        dft = self.hn_main[:, 0:2 * nt * T].rearrange("p (c a t) -> p c a t", c=2, a=nt)
        dft_ready = self.dma(sp, dft, self.const["token_dft_" + name], after=self.everything())
        for h in range(HEADS2):
            po, k = HD * (h % 2), h // 2
            bank = self.mix.next()

            def emit(e, bank=bank, po=po, k=k):
                for c in range(2):
                    last = e.matmul(bank.ap[po:po + HD, c * HD:(c + 1) * HD], head_dft[po:po + HD, c * HD:(c + 1) * HD],
                                    wf[po:po + HD, k, :], start=True, stop=True)
                return last
            done = self.pe.do(emit, [loads, bank.free])
            m = self.v("copy", R_[po:po + HD, k, :], bank.ap[po:po + HD, 0:P], after=[done])
            bank.free = [m]
        for a in range(nt):
            bank = [self.mix.next(), self.mix.next()]

            def emit(e, bank=bank, a=a):
                for h in range(HEADS2):
                    po, k = HD * (h % 2), h // 2
                    last = e.matmul(bank[h % 2].ap[:, k * P:(k + 1) * P], F_[po:po + HD, k, a * P:(a + 1) * P],
                                    R_[po:po + HD, k, :], start=True, stop=True)
                return last
            done = self.pe.do(emit, [m, got["f"], bank[0].free, bank[1].free])
            m2 = []
            for o in range(2):
                dst = YT[:, a, :].rearrange("p (c k o n) -> p o c k n", k=2, o=2, c=2)[:, o]
                m2.append(self.v("copy", dst, bank[o].ap[:, 0:2 * P].rearrange("p (k c n) -> p c k n", k=2, c=2),
                                 after=[done, base]))
                bank[o].free = [m2[-1]]
        for k in range(2):
            bank = self.mix.next()
            pairs = [(YT[:, a, c * GW + k * P:c * GW + (k + 1) * P], dft[:, c, a, :])
                     for c in range(2) for a in range(nt)]
            done = self.mm(bank.ap[:, 0:T], pairs, [m2, dft_ready, bank.free])
            m = self.v("copy", Y[:, k, :], bank.ap[:, 0:T], after=[done])
            bank.free = [m]
        fourier_ready = m
        bank = self.mix.next()
        done = self.transposes([(bank.ap[:, h * P:(h + 1) * P], raw_ws[:, h, :], P) for h in range(HEADS2)], [loads, bank.free])
        ws_ready = self.v("copy", WST.rearrange("p h n -> p (h n)"), bank.ap, after=[done])
        bank.free = [ws_ready]
        for a in range(nt):
            t = self.temps.next()
            v3 = lambda x: x.rearrange("p (h d) -> p h d", h=HEADS2)
            sq, st = t.ap[:, 0:GW], t.ap[:, GW:GW + HEADS2]
            m = self.v("tt", sq, V_[:, a, :], V_[:, a, :], ALU.mult, after=[got["v"], t.free], lane=self.pool)
            m = self.v("sum", st, v3(sq), after=[m])
            m = self.v("ts", st, st, 1.0 / HD, EPS, ALU.mult, ALU.add, after=[m])
            m = self.a(st, st, ACT.Sqrt, after=[m])
            m = self.v("recip", st, st, after=[m])
            m = self.v("tt", v3(V_[:, a, :]), v3(V_[:, a, :]),
                       st.rearrange("p (h o) -> p h o", o=1).broadcast_to([P, HEADS2, HD]), ALU.mult, after=[m])
            t.free = [m]
        v_ready = m
        for k in range(2):
            bank = self.mix.next()

            def emit(e, bank=bank, k=k):
                for a in range(nt):
                    for o in range(2):
                        h = 2 * k + o
                        last = e.matmul(bank.ap[HD * o:HD * (o + 1), a * P:(a + 1) * P], V_[:, a, h * HD:(h + 1) * HD],
                                        WST[:, h, :], start=True, stop=True)
                return last
            done = self.pe.do(emit, [v_ready, ws_ready, bank.free])
            blocks = lambda x: x.rearrange("p (a n) -> p a n", n=P)
            m = self.v("stt", blocks(Y[:, 4 + k, :]), blocks(bank.ap[:, 0:T]), self.column(f"g_sgu{layer}", 1, skip=k),
                       BB[:, k:k + 1, :].broadcast_to([P, nt, P]), ALU.mult, ALU.add, after=[done])
            bank.free = [m]
            m = self.v("tt", Y[:, 4 + k, :], Y[:, 4 + k, :], U_[:, k, :], ALU.mult, after=[m, got["u"]])
        sgu_ready = m
        E = T + 16
        prev = [got["p"]]
        for k in range(2):
            z = PZ[:, k, :]
            s, w = z, 1
            for n in range(4 if k else 2):
                reach = 2 ** n // 2 if n else 0
                lo, hi = (1, E) if n == 0 else (2 ** n, E - 2 ** n + 1)
                a_, b_ = (-1, 0) if n == 0 else (-reach, reach)
                d = sums[n % 2]
                prev = [self.v("tt", d[:, lo:hi], s[:, lo + a_:hi + a_], s[:, lo + b_:hi + b_], ALU.add, after=[prev, base])]
                s = d
                if n // 2 == k:
                    half = slice(HD * (n % 2), HD * (n % 2 + 1))
                    dst = Y[half, 6 + k, :]
                    m = self.v("tt", dst, s[half, 8:8 + T], inv[half, k, :], ALU.mult, after=[prev, loads, base])
                    m = self.v("tt", dst, dst, z[half, 8:8 + T], ALU.subtract, after=[m])
                    prev = [m]
            bank = self.mix.next()

            def emit(e, bank=bank, k=k):
                for o in range(2):
                    half = slice(HD * o, HD * (o + 1))
                    last = e.matmul(bank.ap[half, 0:T], wp[half, k, :], Y[half, 6 + k, :], start=True, stop=True)
                return last
            done = self.pe.do(emit, [prev, bank.free])
            m = self.v("ts", Y[:, 6 + k, :], bank.ap[:, 0:T], self.column(f"s_pool{layer}", 1, skip=k), None, ALU.mult,
                       after=[done])
            bank.free = [m]
        pool_ready = m
        k_lo, k_hi = (0, keys) if name == "main" else (SEQ, keys)
        nk = k_hi - k_lo
        scale = (HD + ROPE) ** -0.5
        mx, sm = self.small[:, 32:48], self.small[:, 48:64]
        pt_first = self.everything()
        all_kv = [self.side.kv, part.kv]
        for h in range(HEADS2):
            po, k = HD * (h % 2), h // 2
            pt = PT.next()
            for qt in range(nt):
                first, second, wide = self.pair_of_banks()
                q = slice(qt * P, (qt + 1) * P)

                def emit(e, wide=wide, q=q, h=h, k=k, po=po):
                    for lo in range(0, nk, 512):
                        n = min(512, nk - lo)
                        key = slice(k_lo + lo, k_lo + lo + n)
                        e.matmul(wide[:, lo:lo + n], QN[po:po + HD, k, q], KN[po:po + HD, k, key], start=True, stop=False)
                        last = e.matmul(wide[:, lo:lo + n], QR[ROPE * h:ROPE * (h + 1), q], KR[ROPE * h:ROPE * (h + 1), key],
                                        start=False, stop=True, tile_position=(ROPE * h, 0))
                    return last
                done = self.pe.do(emit, [all_kv, qn_ready, qr_ready, first.free, second.free])
                c = slice(h * nt + qt, h * nt + qt + 1)
                s = scores.next()
                m = self.v("max", mx[:, c], wide[:, 0:nk], after=[done])
                m = self.v("ts", mx[:, c], mx[:, c], -scale, None, ALU.mult, after=[m])
                m = self.a(s.ap[:, 0:nk], wide[:, 0:nk], ACT.Exp, after=[m, s.free], bias=mx[:, c], scale=scale, accum_out=sm[:, c])
                first.free = second.free = [m]
                m = self.v("recip", sm[:, c], sm[:, c], after=[m])
                m = self.v("ts", s.ap[:, 0:nk], s.ap[:, 0:nk], sm[:, c], None, ALU.mult, after=[m])
                first, second, wide = self.pair_of_banks()
                done = self.transposes([(wide[:, a * P:(a + 1) * P], s.ap[:, a * P:(a + 1) * P], P) for a in range(nk // P)],
                                       [m, first.free, second.free])
                s.free = [done]
                m = self.a(pt.ap[:, 0:nk // P, q], wide[:, 0:nk].rearrange("p (a q) -> p a q", q=P), ACT.Copy,
                           after=[done, pt.free, pt_first])
                first.free = second.free = [m]
            bank = self.mix.next()
            done = self.mm(bank.ap[po:po + HD, 0:T], [(VT[:, k_lo // P + a, h * HD:(h + 1) * HD], pt.ap[:, a, 0:T])
                                                      for a in range(nk // P)], [m, bank.free])
            pt.free = [done]
            m = self.v("copy", Y[po:po + HD, 2 + k, :], bank.ap[po:po + HD, 0:T], after=[done])
            bank.free = [m]
        y_ready = [m, fourier_ready, sgu_ready, pool_ready]
        last = [()]

        def take_out(n, f, ps, done, bank):
            m = self.v("stt", part.h[:, f, 0:T], ps, rows(5)[:, f:f + 1], part.h[:, f, 0:T], ALU.mult, ALU.add, after=[done])
            bank.free = last[0] = [m]
        self.linear(i["w_out_2"][layer], KT, 0, D, [(lambda k: Y[:, k, :], T, y_ready)], take_out)
        part.h_ready = last[0]

    def turned(self, x, turn, rope, ready):
        bank, t = self.mix.next(), self.temps.next()
        done = self.mm(bank.ap, [(turn, x)], [ready, bank.free])
        m = self.v("tt", t.ap, bank.ap, rope[:, 1, :], ALU.mult, after=[done, t.free])
        bank.free = [m]
        m2 = self.v("tt", x, x, rope[:, 0, :], ALU.mult, after=[done])
        m = self.v("tt", x, x, t.ap, ALU.add, after=[m, m2])
        t.free = [m]
        return m

    def second_block(self):
        main, side = self.main, self.side
        side.hn = lambda k: self.arena[:, 28672 - 2048 + k * CTX:28672 - 2048 + (k + 1) * CTX]
        widths = {"main": SEQ, "ctx": CTX}
        start = {"main": 0, "ctx": FT * SEQ}

        def hidden_of(parts):
            return lambda n, k: self.arena[:, start[parts[n].name] + k * parts[n].T:start[parts[n].name] + (k + 1) * parts[n].T]

        for layer in range(2):
            free = self.everything()
            main.hn_free = side.hn_free = free
            ready = self.modulation(self.inp["w_ada_2"][layer], N_MOD2 * KT, self.mod2, lambda k: self.cond[:, k, 1:3],
                                    [self.cond_ready, free], self.column(f"b_ada{layer}", N_MOD2 * KT))
            both = [main, side]
            self.half_step(both, layer, "g_ffn1", 0, hidden_of(both), ready)
            main.hn_free = side.hn_free = self.everything()
            self.mixers(side, layer, layer == 1, ready)
            main.hn_free = self.everything()
            self.mixers(main, layer, False, ready)
            main.hn_free = side.hn_free = self.everything()
            parts = both if layer == 0 else [main]
            self.half_step(parts, layer, "g_ffn2", 6, hidden_of(parts), ready)
        self.plain_norm(main, "final2")
        stage = self.arena[:, 0:4 * D].rearrange("p (a n) -> p a n", a=4)
        free = self.everything()
        for a in range(4):
            for half in range(2):
                bank = self.mix.next()
                done = self.transposes([(bank.ap[:, k * P:(k + 1) * P], main.h[:, 4 * half + k, a * P:(a + 1) * P], P)
                                        for k in range(4)], [main.h_ready, bank.free])
                m = self.v("copy", stage[:, a, half * 512:(half + 1) * 512], bank.ap, after=[done, free])
                bank.free = [m]
            self.dram_writes.append(self.dma(self.sp, self.out[0, a * P:(a + 1) * P, :], stage[:, a, :], after=[m],
                                             counter=self.out_landed))
        self.sp.steps.append((marks(self.dram_writes), lambda e: None, None, 0))


def build(nc, inp, const, out):
    with ExitStack() as ctx:
        prog = Program(nc, ctx, inp, const, out)
        prog.setup()
        prog.first_block()
        prog.second_block()
        block = ctx.enter_context(nc.Block())
        block.sync(lambda e: prog.sp.play(e))
        block.gpsimd(lambda e: prog.pool.play(e))
        block.scalar(lambda e: prog.act.play(e))
        block.tensor(lambda e: prog.pe.play(e))
        block.vector(lambda e: prog.dve.play(e))


def kernel(**inputs):
    import concourse.bacc as bacc
    from concourse.bass_utils import run_bass_kernel_spmd

    nc = bacc.Bacc("TRN2", target_bir_lowering=False, num_devices=1)
    arrays, inp, const = {}, {}, {}
    for name, a in inputs.items():
        a = np.ascontiguousarray(a)
        arrays["in_" + name] = a
        inp[name] = nc.dram_tensor("in_" + name, a.shape, F32, kind="ExternalInput").ap()
    for name, a in shape_constants().items():
        arrays["const_" + name] = np.ascontiguousarray(a)
        const[name] = nc.dram_tensor("const_" + name, a.shape, F32, kind="ExternalInput").ap()
    out = nc.dram_tensor("out", (1, SEQ, D), F32, kind="ExternalOutput").ap()
    build(nc, inp, const, out)
    result = run_bass_kernel_spmd(nc, [arrays], core_ids=[0])
    return result.results[0]["out"]
```

```python
from contextlib import ExitStack
import math

import numpy as np

import concourse.bass as bass
from concourse import mybir

F32 = mybir.dt.float32
F32R = mybir.dt.float32r
ALU = mybir.AluOpType
ACT = mybir.ActivationFunctionType
AX_X = mybir.AxisListType.X

P = 128
D = 1024
KT = D // P
SEQ = 512
CTX = 256
HD = 64
D_FF = 2816
FT = D_FF // P
CHUNK = 64
N_BUCKETS, MAX_DISTANCE = 32, 2048
EPS = 1e-6
MASKED = -1e30
STAGES, SLOTS = 4, 3
GROUPS = ((0, 8), (8, 8), (16, 6))
HEADS1 = 8
HEADS2 = 4
Q_RANK, KV_RANK, ROPE = 192, 128, 32
GW = 256
N_MOD1, N_MOD2 = 6, 9
SBUF_END = 229344
SKEW = 640


def shape_constants():
    c = {}
    eye = np.eye(P, dtype=np.float32)
    half = np.arange(P) // HD
    c["eye"] = eye
    c["head_ones"] = (half[:, None] == half[None, :]).astype(np.float32)
    e, t = np.arange(P)[:, None], np.arange(P)[None, :]
    same = e // CHUNK == t // CHUNK
    masks = [same & (e < t), same & (e <= t)]
    for level in range(6):
        n = 2 ** level
        masks.append((e // (2 * n) == t // (2 * n)) & (e // n % 2 == 1) & (t // n % 2 == 0))
    c["masks"] = np.stack(masks, 1).astype(np.float32)
    head_of_row = np.zeros((HEADS1, HEADS1 // 2, P), np.float32)
    for k in range(HEADS1 // 2):
        head_of_row[2 * k, k, :HD] = 1
        head_of_row[2 * k + 1, k, HD:] = 1
    c["pick_pair"] = head_of_row
    c["sum_rows"] = np.zeros((P, 8, 16), np.float32)
    for f in range(8):
        for o in range(2):
            c["sum_rows"][HD * o:HD * (o + 1), f, 2 * f + o] = 1
    c["spread_rows"] = np.ascontiguousarray(c["sum_rows"].transpose(2, 1, 0))
    c["pick_head"] = np.repeat(np.eye(HEADS1, dtype=np.float32)[:, :, None], P, 2)
    d = 511 - np.arange(SKEW)
    dist = np.maximum(d, 0)
    exact = N_BUCKETS // 2
    f = np.maximum(dist, 1).astype(np.float32)
    large = exact + (np.log(f / exact) / math.log(MAX_DISTANCE / exact) * (N_BUCKETS - exact)).astype(np.int32)
    bucket = np.where(dist < exact, dist, np.minimum(large, N_BUCKETS - 1))
    count = (d <= 128).astype(int) + (d % 4 == 0) + (d % 16 == 0)
    seen = (d >= 0) & (count > 0) & (np.arange(SKEW) < 639)
    table = np.zeros((N_BUCKETS + 1, SKEW), np.float32)
    table[bucket[seen], np.arange(SKEW)[seen]] = 1
    table[N_BUCKETS] = np.where(seen, np.log(np.maximum(count, 1)), MASKED)
    c["distance"] = table
    a = 2 * np.pi / HD * (np.arange(HD)[:, None] * np.arange(HD)[None, :] % HD)
    c["head_dft"] = np.concatenate([np.tile(np.cos(a), (2, 1)), np.tile(-np.sin(a), (2, 1))], 1).astype(np.float32)
    for name, length in (("main", SEQ), ("ctx", CTX)):
        a = 2 * np.pi / length * (np.arange(length)[:, None] * np.arange(length)[None, :] % length)
        norm = 1 / math.sqrt(length * HD)
        both = np.stack([np.cos(a) * norm, np.sin(a) * norm], 1)
        both = both.reshape(length // P, P, 2, length).transpose(1, 2, 0, 3)
        c["token_dft_" + name] = both.astype(np.float32)
        t = np.arange(length)
        inv = []
        for w in (2, 4, 8, 16):
            lo, hi = np.clip(t - w // 2, 0, length), np.clip(t - w // 2 + w, 0, length)
            inv.append(np.tile((1 / (hi - lo)).astype(np.float32), (HD, 1)))
        c["pool_" + name] = np.stack([np.concatenate(inv[:2]), np.concatenate(inv[2:])], 1)
    inv = np.power(np.float32(10000.0), -np.arange(0, 16, 2, dtype=np.float32) / np.float32(16))
    t = np.arange(SEQ)
    pos = np.stack([t // 64, t % 64]).astype(np.float32)
    ang = (pos[:, :, None] * inv[None, None, :]).astype(np.float32)
    ang = np.broadcast_to(ang.transpose(0, 2, 1)[:, None], (2, 2, 8, SEQ)).reshape(ROPE, SEQ)
    c["rope"] = np.tile(np.stack([np.cos(ang), np.sin(ang)], 1), (4, 1, 1)).astype(np.float32)
    turn = np.zeros((P, P), np.float32)
    for m in range(P):
        if m // 8 % 2 == 0:
            turn[m + 8, m] = -1
        else:
            turn[m - 8, m] = 1
    c["turn"] = turn
    c["repeat"] = np.tile(np.eye(ROPE, dtype=np.float32), (1, HEADS2))
    return c


class Lane:

    def __init__(self, sem):
        self.sem, self.count, self.steps = sem, 0, []

    def do(self, emit, after=()):
        self.count += 1
        self.steps.append((marks(after), emit, self.sem, 1))
        return (self.sem, self.count)

    def play(self, engine):
        seen = {}
        for waits, emit, sem, amount in self.steps:
            for s, value in waits:
                if seen.get(s.name, 0) < value:
                    engine.wait_ge(s, value)
                    seen[s.name] = value
            last = emit(engine)
            if last is not None:
                last.then_inc(sem, amount)


def marks(after):
    if after is None:
        return []
    if isinstance(after, tuple) and len(after) == 2 and isinstance(after[1], int):
        return [after]
    return [m for a in after for m in marks(a)]


class Counter:

    def __init__(self, sem):
        self.sem, self.count = sem, 0


class Bank:

    def __init__(self, ap):
        self.ap, self.taken, self.last = ap, False, ()

    @property
    def free(self):
        return self.last

    @free.setter
    def free(self, after):
        self.last, self.taken = after, False


class Turn:
    def __init__(self, banks):
        self.banks, self.n = banks, 0

    def next(self):
        b = self.banks[self.n % len(self.banks)]
        self.n += 1
        assert not b.taken, "taken again before its readers were queued"
        b.taken = True
        return b


class Part:

    def __init__(self, name, tokens, h, hn, col):
        self.name, self.T, self.h, self.hn, self.col = name, tokens, h, hn, col
        self.h_ready, self.hn_ready, self.hn_free = (), (), ()


class Program:
    def __init__(self, nc, ctx, inp, const, out, plan):
        self.nc, self.inp, self.const, self.out = nc, inp, const, out
        self.ctx = ctx
        sem = lambda n: ctx.enter_context(nc.semaphore(n))
        self.pe, self.act, self.dve, self.pool, self.sp = (
            Lane(sem(n)) for n in ("pe_done", "act_done", "dve_done", "pool_done", "sp_unused"))
        self.stage_sems = [Counter(sem(f"stage{i}_landed")) for i in range(STAGES)]
        self.misc_sems = [Counter(sem(f"misc{i}_landed")) for i in range(24)]
        self.misc_n = 0
        self.out_landed = Counter(sem("out_landed"))
        self.at, self.names = 16512, 0
        sb = self.place
        self.h_main = sb("h_main", [P, KT, SEQ])
        self.h_ctx = sb("h_ctx", [P, KT, CTX])
        self.stage = sb("stage", [P, STAGES, KT * P])
        self.high = [sb(f"high{n}", [P, KT * P], F32R) for n in range(SLOTS)]
        self.low = [sb(f"low{n}", [P, KT * P], F32R) for n in range(SLOTS)]
        self.tmp = sb("tmp", [P, 4, SEQ])
        self.eye = sb("eye", [P, P])
        self.ones = sb("ones", [P, P])
        self.head_ones = sb("head_ones", [P, P])
        self.vec = sb("vec", [P, 3, P])
        self.mod1 = sb("mod1", [P, N_MOD1 * KT, 1])
        self.mod2 = [sb(f"mod2_{n}", [P, N_MOD2 * KT, 2]) for n in range(2)]
        self.cond = sb("cond", [P, KT, 3])
        self.gain = sb("gain", [P, KT, 3])
        self.small = sb("small", [P, 192])
        self.partial = sb("partial", [P, 2, 2, P])
        self.root = sb("root", [P, SEQ])
        self.token_gates = sb("token_gates", [P, P])
        self.small_consts, self.loaded = sb("small_consts", [P, P]), {}
        self.phase_base = self.at
        psum = ctx.enter_context(nc.psum_tensor("psum", [P, 8, 512], F32))
        self.ps = psum
        self.banks = Turn([Bank(psum[:, i, :]) for i in range(4)])
        self.mix = Turn([Bank(psum[:, i, :]) for i in range(4, 8)])
        self.stages = Turn([Bank(self.stage[:, i, :]) for i in range(STAGES)])
        self.slots = Turn([Bank((self.high[i], self.low[i])) for i in range(SLOTS)])
        self.partials = Turn([Bank(self.partial[:, i]) for i in range(2)])
        self.plan, self.asked, self.brought, self.ready_blocks = plan, [], 0, {}
        self.jobs, self.background, self.rate, self.unfinished = [], [], 1, None
        self.roots = Turn([Bank(self.root[:, :])])
        self.temps = Turn([Bank(self.tmp[:, i, :]) for i in range(4)])
        self.dram_writes = []
        self.skew = nc.dram_tensor("skew", (HEADS1, P * SKEW), F32, kind="Internal").ap()

    def place(self, name, shape, dtype=F32):
        size = 4 * int(np.prod(shape[1:]))
        assert self.at + size <= SBUF_END, (name, self.at + size - SBUF_END)
        self.names += 1
        t = self.nc.alloc_sbuf_tensor_at(f"{name}_{self.names}", shape, dtype, offset=self.at)
        self.at += (size + 31) // 32 * 32
        return t

    def area(self, name, n):
        return self.place(name, [P, n])[:, :]

    def halves(self, name, tiles, T):
        return [self.place(f"{name}_{part}", [P, tiles, T], F32R) for part in ("high", "low")]

    def everything(self):
        return [(l.sem, l.count) for l in (self.pe, self.act, self.dve, self.pool) if l.count] + \
            [(c.sem, c.count) for c in self.misc_sems if c.count]

    def dma(self, lane, out, in_, after=(), counter=None):
        if counter is None:
            counter = self.misc_sems[self.misc_n % len(self.misc_sems)]
            self.misc_n += 1
        before = [(counter.sem, counter.count)] if counter.count else []
        counter.count += 16
        lane.steps.append((marks([after, before]), lambda e: e.dma_start(out, in_), counter.sem, 16))
        return (counter.sem, counter.count)

    def mm(self, out, pairs, after=(), close=True, open_=True):
        def emit(e):
            for i, (a, b) in enumerate(pairs):
                last = e.matmul(out, a, b, start=open_ and i == 0, stop=close and i == len(pairs) - 1)
            return last
        return self.pe.do(emit, after)

    def transposes(self, triples, after=()):
        def emit(e):
            for out, in_, k in triples:
                last = e.transpose(out, in_, self.eye[0:k, 0:k])
            return last
        return self.pe.do(emit, after)

    def v(self, name, *args, after=(), lane=None, **kw):
        table = {
            "tt": lambda e: e.tensor_tensor(*args, **kw), "ts": lambda e: e.tensor_scalar(*args, **kw),
            "stt": lambda e: e.scalar_tensor_tensor(*args, **kw), "copy": lambda e: e.tensor_copy(*args),
            "recip": lambda e: e.reciprocal(*args), "max": lambda e: e.reduce_max(*args, AX_X),
            "sum": lambda e: e.reduce_sum(*args, AX_X), "set": lambda e: e.memset(*args),
            "ttr": lambda e: e.tensor_tensor_reduce(*args, **kw),
            "scan": lambda e: e.tensor_tensor_scan(*args, **kw)}
        return (lane or self.dve).do(table[name], after)

    def a(self, out, in_, func, after=(), **kw):
        return self.act.do(lambda e: e.activation(out, in_, func, **kw), after)

    def bring(self, n):
        w, k0, nk, c0, cols, split = self.plan[n]
        stage = self.stages.next()
        counter = self.stage_sems[(self.stages.n - 1) % STAGES]
        raw = stage.ap[:, 0:nk * cols]
        landed = self.dma(self.sp, raw.rearrange("p (k n) -> p k n", k=nk),
                          w[k0:k0 + nk * P, c0:c0 + cols].rearrange("(k p) n -> p k n", p=P),
                          after=stage.free, counter=counter)
        if not split:
            return stage, raw.rearrange("p (k n) -> p k n", k=nk), landed
        slot = self.slots.next()
        high, low = (part[:, 0:nk * cols] for part in slot.ap)
        m = self.a(high, raw, ACT.Copy, after=[landed, slot.free])
        m = self.v("tt", low, raw, high.bitcast(F32), ALU.subtract, after=[m])
        stage.free = [m]
        return slot, [part.rearrange("p (k n) -> p k n", k=nk) for part in (high, low)], m

    def weights(self, w, k0, nk, c0, cols=P, split=True):
        n = len(self.asked)
        self.asked.append((w, k0, nk, c0, cols, split))
        if self.plan is None:
            stub = Bank(None)
            part = self.high[0][:, 0:nk * cols].rearrange("p (k n) -> p k n", k=nk)
            return stub, [part, part] if split else self.stage[:, 0, 0:nk * cols].rearrange("p (k n) -> p k n", k=nk), ()
        target = n
        if split:
            later = [m for m in range(n + 1, min(n + 4, len(self.plan))) if self.plan[m][5]]
            target = later[0] if later else n
        while self.brought <= target:
            self.ready_blocks[self.brought] = self.bring(self.brought)
            self.brought += 1
        return self.ready_blocks.pop(n)

    def pieces(self, sources):
        stage = self.stages.next()
        counter = self.stage_sems[(self.stages.n - 1) % STAGES]
        before = [(counter.sem, counter.count)] if counter.count else []
        views = []
        for at, kp, nk, cols, src in sources:
            view = stage.ap[0:kp, at:at + nk * cols].rearrange("p (k n) -> p k n", k=nk)
            dst = view if len(src.shape) == 3 else view.rearrange("p k (h n) -> p k h n", h=src.shape[2])
            for k in range(nk):
                counter.count += 16
                self.sp.steps.append((marks([stage.free, before]), lambda e, d=dst[:, k], s=src[:, k]: e.dma_start(d, s),
                                      counter.sem, 16))
            views.append(view)
        return stage, views, (counter.sem, counter.count)

    def products(self, out, blocks, x, i0, after, first=True, last=True, cols=slice(None), each=None):
        high, low = blocks
        nk = high.shape[1]
        pairs = []
        for i in range(nk):
            xh, xl = x[0][:, i0 + i, :], x[1][:, i0 + i, :]
            pairs += [(high[:, i, cols], xh), (high[:, i, cols], xl), (low[:, i, cols], xh)]
            if each:
                done = self.mm(out, pairs, [after, each[i]], open_=first and i == 0, close=last and i == nk - 1)
                pairs = []
        return done if each else self.mm(out, pairs, after, open_=first, close=last)

    def split(self, x, high, low, after):
        m = self.a(high, x, ACT.Copy, after=after)
        return self.v("tt", low, x, high.bitcast(F32), ALU.subtract, after=[m])

    def linear(self, w, n_k, c0, width, parts, take, tile=P):
        for at in range(0, width, tile):
            cols = min(tile, width - at)
            held = {}
            for k in range(0, n_k, KT):
                nk = min(KT, n_k - k)
                slot, view, ready = self.weights(w, k * P, nk, c0 + at, cols)
                for n, (x, T, x_ready) in enumerate(parts):
                    if k == 0:
                        held[n] = self.banks.next()
                    bank = held[n]
                    by_tile = at == 0 and len(x_ready) == n_k
                    done = self.products(bank.ap[0:cols, 0:T], view, x, k,
                                         [ready, () if by_tile else x_ready, bank.free if k == 0 else ()],
                                         first=k == 0, last=k + nk == n_k, each=x_ready[k:k + nk] if by_tile else None)
                    slot.free = [done]
                    if k + nk == n_k:
                        take(n, at // tile, bank.ap[0:cols, 0:T], done, bank)
            self.pump()

    def pump(self, n=1):
        for _ in range(n):
            for queue in (self.jobs, self.background):
                if queue:
                    queue.pop(0)()

    def mean_square_root(self, tiles, T, ones, scale, after, rows=P):
        bank = self.mix.next()
        n = len(tiles)
        for i, x in enumerate(tiles):
            t = self.temps.next()
            sq = t.ap[0:rows, 0:T]
            m = self.a(sq, x, ACT.Square, after=[after, t.free])
            done = self.pe.do(lambda e, i=i, sq=sq: e.matmul(bank.ap[:, 0:T], ones[0:rows, :], sq,
                                                             start=i == 0, stop=i == n - 1),
                              [m, bank.free if i == 0 else ()])
            t.free = [done]
        t = self.roots.next()
        root = t.ap[:, 0:T]
        m = self.v("ts", root, bank.ap[:, 0:T], scale, EPS, ALU.mult, ALU.add, after=[done, t.free])
        bank.free = [m]
        m = self.a(root, root, ACT.Sqrt, after=[m])
        m = self.v("recip", root, root, after=[m])
        return root, m, t

    def modulated_norm(self, part, gain, shift, after=()):
        T = part.T
        rinv, ready, t = self.mean_square_root([part.h[:, k, 0:T] for k in range(KT)], T, self.ones,
                                               1.0 / D, part.h_ready)
        high, low = part.hn
        held, part.hn_ready = [], []
        for k in range(KT + 2):
            if k < KT:
                x = self.temps.next()
                xs = x.ap[:, 0:T]
                m = self.v("tt", xs, part.h[:, k, 0:T], rinv, ALU.mult, after=[ready, part.h_ready, x.free])
                m = self.a(xs, xs, ACT.Identity, after=[m, after], scale=gain[:, k, :], bias=shift[:, k:k + 1])
                m = self.a(high[:, k, :], xs, ACT.Copy, after=[m, part.hn_free])
                held.append((x, xs, m))
            if k >= 2:
                x, xs, m = held[k - 2]
                m = self.v("tt", low[:, k - 2, :], xs, high[:, k - 2, :].bitcast(F32), ALU.subtract, after=[m])
                x.free = [m]
                part.hn_ready.append(m)
        t.free = [m]

    def swiglu(self, parts, hidden, w_a, a0, w_b, b0, w_down, gate, hidden_free):
        for first, tiles in GROUPS:
            hid_ready = [[] for _ in parts]
            for f in range(tiles):
                slot_a, wa, ready_a = self.weights(w_a, 0, KT, a0 + (first + f) * P)
                slot_b, wb, ready_b = self.weights(w_b, 0, KT, b0 + (first + f) * P)
                for n, part in enumerate(parts):
                    T = part.T
                    bank_a, bank_b = self.banks.next(), self.banks.next()
                    ps_a, ps_b = bank_a.ap[:, 0:T], bank_b.ap[:, 0:T]
                    ma = self.products(ps_a, wa, part.hn, 0, [ready_a, bank_a.free],
                                       each=part.hn_ready if first + f == 0 else None)
                    mb = self.products(ps_b, wb, part.hn, 0, [ready_b, bank_b.free])
                    t = self.temps.next()
                    s = t.ap[:, 0:T]
                    m = self.a(s, ps_a, ACT.Sigmoid, after=[ma, t.free])
                    m = self.v("tt", s, s, ps_a, ALU.mult, after=[m])
                    bank_a.free = [m]
                    m = self.v("tt", s, s, ps_b, ALU.mult, after=[m, mb])
                    bank_b.free = [m]
                    high, low = hidden[n]
                    m = self.split(s, high[:, f, :], low[:, f, :], [m, hidden_free])
                    t.free = [m]
                    hid_ready[n].append(m)
                slot_a.free = slot_b.free = [mb]
                self.pump(self.rate)
            last = {}

            def take(n, f, ps, done, bank):
                part = parts[n]
                m = self.v("stt", part.h[:, f, 0:part.T], ps, gate(part)[:, f:f + 1], part.h[:, f, 0:part.T],
                           ALU.mult, ALU.add, after=[done, part.h_ready])
                bank.free = [m]
                last[n] = m

            for f in range(KT):
                slot, view, ready = self.weights(w_down, first * P, tiles, f * P)
                for n, part in enumerate(parts):
                    bank = self.banks.next()
                    done = self.products(bank.ap[:, 0:part.T], view, hidden[n], 0, [ready, bank.free],
                                         each=hid_ready[n] if f == 0 else None)
                    take(n, f, bank.ap[:, 0:part.T], done, bank)
                slot.free = [done]
                self.pump(self.rate)
            hidden_free = [done]
            for n, part in enumerate(parts):
                part.h_ready = [last[n]]
        for part in parts:
            part.hn_free = [mb]

    def modulation(self, w, j, mod, vectors, ready, bias):
        stage, view, landed = self.weights(w, 0, KT, j * P, split=False)
        part = self.partials.next()
        m = [(), ()]
        for k in range(KT):
            for i, c in enumerate(vectors):
                acc, by = part.ap[:, i, :], self.cond[:, k, c:c + 1]
                if k == 0:
                    m[i] = self.v("ts", acc, view[:, k, :], by, None, ALU.mult, after=[landed, ready, part.free])
                else:
                    m[i] = self.v("stt", acc, view[:, k, :], by, acc, ALU.mult, ALU.add, after=[m[i]])
        stage.free = m

        def finish():
            bank = self.mix.next()

            def emit(e, n=len(vectors)):
                for i in range(n):
                    last = e.matmul(bank.ap[:, i:i + 1], part.ap[:, i, :], self.ones[:, 0:1], start=True, stop=True)
                return last
            done = self.pe.do(emit, [m, bank.free])
            part.free = [done]
            self.mod_ready = self.v("ts", mod[:, j, :], bank.ap[:, 0:len(vectors)], bias[:, j:j + 1], None, ALU.add,
                                    after=[done])
            bank.free = [self.mod_ready]
        self.finish_modulation()
        self.unfinished = finish

    def finish_modulation(self):
        if self.unfinished:
            self.unfinished()
        self.unfinished = None

    def sigmoid_times(self, out, x, after):
        t = self.temps.next()
        s = t.ap[:, 0:x.shape[1]]
        m = self.a(s, x, ACT.Sigmoid, after=[after, t.free])
        m = self.v("tt", out, x, s, ALU.mult, after=[m])
        t.free = [m]
        return m

    def setup(self):
        i = self.inp
        sp = self.sp
        rows = []
        self.col = {}
        self.at = self.phase_base
        stage = self.area("vectors", 3 * P).rearrange("p (a n) -> p a n", a=3)

        def put(name, tile, row, ap):
            n = ap.shape[0]
            rows.append(self.dma(sp, stage[row:row + n, tile, :], ap))
            self.col[name] = (tile, row)

        def rows_of(ap):
            return ap.rearrange("(r p) -> r p", p=P)

        clear = self.v("set", stage, 0.0)
        rows.append(clear)

        def put_after(name, tile, row, ap):
            n = ap.shape[0]
            rows.append(self.dma(sp, stage[row:row + n, tile, 0:ap.shape[1]], ap, after=[clear]))
            self.col[name] = (tile, row)

        put = put_after
        put("norm_attn", 0, 0, rows_of(i["norm_attn_g"][0]))
        put("norm_ffn", 0, 8, rows_of(i["norm_ffn_g"][0]))
        put("final", 0, 16, rows_of(i["final_norm_g"]))
        put("b_ada", 0, 24, rows_of(i["b_ada"][0]))
        put("c", 0, 72, rows_of(i["c"][0]))
        put("conv", 0, 80, i["conv_w"][0].rearrange("j (r p) -> (j r) p", p=P))
        for l in range(2):
            t = 1 + l
            put(f"b_ada{l}", t, 0, rows_of(i["b_ada_2"][l]))
            put(f"g_ffn1{l}", t, 72, rows_of(i["g_ffn1_2"][l]))
            put(f"g_mix{l}", t, 80, rows_of(i["g_mix_2"][l]))
            put(f"g_ffn2{l}", t, 88, rows_of(i["g_ffn2_2"][l]))
            put(f"s_pool{l}", t, 96, rows_of(i["s_pool_2"][l]))
            put(f"g_sgu{l}", t, 98, i["g_sgu_2"][l].rearrange("(a b) d -> a (b d)", b=2))
            put(f"g_kv{l}", t, 100, rows_of(i["g_kv_2"][l]))
            put(f"g_q{l}", t, 101, i["g_q_2"][l].rearrange("(r p) -> r p", p=96))
        put("c2", 1, 103, rows_of(i["c_2"][0]))
        put("c_ctx", 1, 111, rows_of(i["c_ctx_2"]))
        put("final2", 1, 119, rows_of(i["g_final_2"]))
        eye = self.dma(sp, self.eye[:], self.const["eye"])
        hones = self.dma(sp, self.head_ones[:], self.const["head_ones"])
        ones = self.v("set", self.ones[:], 1.0)
        self.consts = [eye, hones, ones]
        bank = self.mix.next()
        m = self.transposes([(bank.ap[:, a * P:(a + 1) * P], stage[:, a, :], P) for a in range(3)],
                            [rows, eye, ones])
        m = self.v("copy", self.vec[:].rearrange("p a n -> p (a n)"), bank.ap[:, 0:3 * P], after=[m])
        bank.free = [m]
        self.vec_ready = m
        self.dt_bias, self.a_log = self.small[0:8, 0:1], self.small[0:8, 1:2]
        self.norm_g = self.small[:, 2:3]
        col = lambda ap: ap.rearrange("(n o) -> n o", o=1)
        self.small_ready = [self.dma(sp, self.dt_bias, col(i["dt_bias"][0])),
                            self.dma(sp, self.a_log, col(i["a_log"][0])),
                            self.dma(sp, self.norm_g[0:HD], col(i["delta_norm_g"][0])),
                            self.dma(sp, self.norm_g[HD:P], col(i["delta_norm_g"][0]))]
        for n, name in enumerate(("c", "c2", "c_ctx")):
            m = self.sigmoid_times(self.cond[:, :, n], self.column(name, KT), [self.vec_ready])
        self.cond_ready = m
        self.main = Part("main", SEQ, self.h_main, None, 0)
        self.side = Part("ctx", CTX, self.h_ctx, None, 1)
        for part, src in ((self.main, i["x"][0]), (self.side, i["ctx_2"][0])):
            nt = part.T // P
            x = self.area("tokens", nt * D).rearrange("p (a n) -> p a n", a=nt)
            landed = self.dma(sp, x, src.rearrange("(a p) n -> p a n", p=P))
            for k in range(KT):
                bank = self.mix.next()
                m = self.transposes([(bank.ap[:, a * P:(a + 1) * P], x[:, a, k * P:(k + 1) * P], P)
                                     for a in range(nt)], [landed, eye, bank.free])
                m = self.v("copy", part.h[:, k, :], bank.ap[:, 0:part.T], after=[m])
                bank.free = [m]
            part.h_ready = [m]
        self.end_of_setup = self.everything()

    def column(self, name, n, skip=0):
        tile, row = self.col[name]
        return self.vec[:, tile, row + skip:row + skip + n]

    def gains(self, slot, name, scale, after):
        return self.v("stt", self.gain[:, :, slot], scale, 1.0, self.column(name, KT), ALU.add, ALU.mult, after=after)

    def distance_bias(self):
        table = self.area("table", SKEW)[0:N_BUCKETS + 1]
        relb = self.area("rel_bias", HEADS1)[0:N_BUCKETS + 1]
        wide = self.area("rel_wide", HEADS1 * P)[0:N_BUCKETS + 1].rearrange("p (h n) -> p h n", n=P)
        rows = [self.area("distances", SKEW) for _ in range(2)]
        table_ready = self.dma(self.sp, table, self.const["distance"])
        one = self.v("set", relb, 1.0)
        rel = self.dma(self.sp, relb[0:N_BUCKETS], self.inp["rel_bias"], after=[one])
        wide_ready = self.v("copy", wide, relb.rearrange("p (h o) -> p h o", o=1).broadcast_to([N_BUCKETS + 1, HEADS1, P]),
                            after=[one, rel])
        free, self.skewed = [(), ()], []
        for h in range(HEADS1):
            r = rows[h % 2]
            for o, n in ((0, 512), (512, SKEW - 512)):
                bank = self.mix.next()
                done = self.mm(bank.ap[:, 0:n], [(wide[:, h, :], table[:, o:o + n])],
                               [wide_ready, table_ready, bank.free])
                m = self.a(r[:, o:o + n], bank.ap[:, 0:n], ACT.Copy, after=[done, free[h % 2]])
                bank.free = [m]
            wrote = self.dma(self.sp, self.skew[h, :].rearrange("(p n) -> p n", p=P), r, after=[m])
            self.dram_writes.append(wrote)
            self.skewed.append(wrote)
            free[h % 2] = [wrote]

    def dilated_attention(self, gates_read, QA, KA, VA, Y, ready):
        E = Turn([Bank(self.area("bias", SEQ)) for _ in range(2)])
        PT = Turn([Bank(self.area("weights_t", 4 * SEQ).rearrange("p (a q) -> p a q", a=4)) for _ in range(2)])
        for e in E.banks:
            e.free = gates_read
        mx, sm = self.small[:, 32:64], self.small[:, 64:96]
        state = {"late": None}

        def scores(h, qt):
            k, po, n, c = h // 2, HD * (h % 2), (qt + 1) * P, 4 * h + qt
            if qt == 0:
                e = E.next()
                src = bass.AP(self.skew.tensor, h * P * SKEW + 127, [[SKEW - 1, P], [1, SEQ]])
                state["bias"] = (e, self.dma(self.sp, e.ap, src, after=[self.skewed[h], e.free]))
                state["pt"] = PT.next()
            e, e_ready = state["bias"]
            bank, s = self.mix.next(), self.temps.next()
            sc = s.ap[:, 0:n]
            done = self.mm(bank.ap[:, 0:n], [(QA[po:po + HD, k, qt * P:(qt + 1) * P], KA[po:po + HD, k, 0:n])],
                           [ready(), bank.free])
            m = self.v("ttr", sc, bank.ap[:, 0:n], e.ap[:, (3 - qt) * P:SEQ], 1.0, -3e38, ALU.add, ALU.max,
                       mx[:, c:c + 1], after=[done, s.free, e_ready])
            bank.free = e.free = [m]
            m = self.v("ts", mx[:, c:c + 1], mx[:, c:c + 1], -1.0, None, ALU.mult, after=[m])
            m = self.a(sc, sc, ACT.Exp, after=[m], bias=mx[:, c:c + 1], accum_out=sm[:, c:c + 1])
            m = self.v("recip", sm[:, c:c + 1], sm[:, c:c + 1], after=[m])
            m = self.v("ts", sc, sc, sm[:, c:c + 1], None, ALU.mult, after=[m])
            return (h, qt, s, sc, m, state["pt"])

        def values(late):
            h, qt, s, sc, m, pt = late
            k, po, n = h // 2, HD * (h % 2), (qt + 1) * P
            bank = self.mix.next()
            done = self.transposes([(bank.ap[:, a * P:(a + 1) * P], sc[:, a * P:(a + 1) * P], P)
                                    for a in range(qt + 1)], [m, bank.free])
            s.free = [done]
            m = self.a(pt.ap[:, 0:qt + 1, qt * P:(qt + 1) * P], bank.ap[:, 0:n].rearrange("p (a q) -> p a q", q=P),
                       ACT.Copy, after=[done, pt.free])
            bank.free = [m]
            if qt < 3:
                return
            bank = self.mix.next()

            def emit(e):
                for a in range(4):
                    last = e.matmul(bank.ap[po:po + HD, a * P:SEQ], VA[:, a, h * HD:(h + 1) * HD],
                                    pt.ap[:, a, a * P:SEQ], start=a == 0, stop=a == 3)
                return last
            done = self.pe.do(emit, [m, bank.free])
            pt.free = [done]
            m = self.a(Y[po:po + HD, k, :], bank.ap[po:po + HD, :], ACT.Copy, after=[done])
            bank.free = [m]
            self.attention_done = m

        def job(h, qt):
            now = scores(h, qt) if h < HEADS1 else None
            if state["late"]:
                values(state["late"])
            state["late"] = now
        return [lambda h=h, qt=qt: job(h, qt) for h in range(HEADS1) for qt in range(4)] + [lambda: job(HEADS1, 0)]

    def head_norm(self, tiles, n, scale, eps, after, sum_rows, spread_rows, rows, finish):
        bank = self.mix.next()
        for f, x in enumerate(tiles):
            t = self.temps.next()
            m = self.a(t.ap, x, ACT.Square, after=[after, t.free])
            done = self.pe.do(lambda e, f=f, sq=t.ap: e.matmul(bank.ap[0:16, :], sum_rows[:, f, :], sq, start=f == 0,
                                                               stop=f == n - 1), [m, bank.free if f == 0 else ()])
            t.free = [done]
        m = self.v("ts", rows, bank.ap[0:16, :], scale, eps, ALU.mult, ALU.add, after=[done])
        bank.free = [m]
        m = self.a(rows, rows, ACT.Sqrt, after=[m])
        m = self.v("recip", rows, rows, after=[m])
        for f in range(n):
            bank = self.mix.next()
            done = self.mm(bank.ap, [(spread_rows[0:16, f, :], rows)], [m, bank.free])
            last = finish(f, bank.ap, done)
            bank.free = [last]
        return last

    def first_block(self):
        i, main, mod = self.inp, self.main, self.mod1
        self.at = self.phase_base + 4 * (3 * P + 6 * D)
        self.distance_bias()
        bias = self.column("b_ada", N_MOD1 * KT)
        for j in range(N_MOD1 * KT):
            self.modulation(i["w_ada"][0], j, mod, (0,), [self.cond_ready], bias)
            if j == 2 * KT - 1:
                self.finish_modulation()
                first_two = self.mod_ready
                break
        self.background = [lambda j=j: self.modulation(i["w_ada"][0], j, mod, (0,), [self.cond_ready], bias)
                           for j in range(2 * KT, N_MOD1 * KT)]
        vec = lambda j: mod[:, j * KT:(j + 1) * KT, 0]
        before = self.everything()
        self.at = self.phase_base
        YA = self.area("attention_out", 4 * SEQ).rearrange("p (k t) -> p k t", k=4)
        ZS = self.area("silu_z", 4 * SEQ).rearrange("p (k t) -> p k t", k=4)
        PAD = SEQ + 3
        DX = self.area("delta_qkv", 12 * PAD).rearrange("p (k t) -> p k t", k=12)
        G, EG, BT = (self.area("gate_rows", SEQ)[0:8] for _ in range(3))
        delta_base = self.at
        main.hn = self.halves("hn", KT, SEQ)
        QA, KA, VA = (self.area("qkv", 4 * SEQ).rearrange("p (k t) -> p k t", k=4) for _ in range(3))
        gate_work = self.at
        X1, BE, AT = (self.area("gate_work", SEQ)[0:8] for _ in range(3))
        g = self.gains(0, "norm_attn", vec(1), [first_two])
        main.hn_free = before
        self.modulated_norm(main, self.gain[:, :, 0:1], vec(0), [g, first_two])
        pads = self.v("set", DX[:, :, 0:3], 0.0, after=before)
        w = i["w_in"][0]
        got = {}
        part = [(main.hn, SEQ, main.hn_ready)]

        for n, dst in ((0, BT), (1, AT)):
            def take_gate(_, f, ps, done, bank, n=n, dst=dst):
                if n == 0:
                    m = self.a(dst, ps, ACT.Sigmoid, after=[done, before])
                else:
                    m = self.a(dst, ps, ACT.Identity, after=[done, before, self.small_ready], bias=self.dt_bias)
                bank.free = [m]
                got[n] = m
            self.linear(w, KT, 3584 + 8 * n, 8, part, take_gate)
        RS = BE
        reset = self.v("set", RS, 1.0, after=before)
        reset = self.v("set", RS.rearrange("p (n c) -> p n c", c=CHUNK)[:, :, 0:1], 0.0, after=[reset])
        m = self.a(X1, AT, ACT.Abs, after=[got[1]])
        m = self.a(X1, X1, ACT.Exp, after=[m], scale=-1.0)
        m = self.a(X1, X1, ACT.Ln, after=[m], bias=1.0)
        m = self.v("stt", X1, AT, 0.0, X1, ALU.max, ALU.add, after=[m])
        ea = self.a(self.a_log, self.a_log, ACT.Exp, after=[self.small_ready])
        m = self.v("ts", X1, X1, self.a_log, -1.0, ALU.mult, ALU.mult, after=[m, ea])
        m = self.v("scan", G, RS, X1, 0.0, ALU.mult, ALU.add, after=[m, reset])
        g_ready = m
        eg_ready = self.a(EG, G, ACT.Exp, after=[m])
        g3, x3 = (t.rearrange("p (n c) -> p n c", c=CHUNK) for t in (G, X1))
        m = self.v("tt", x3, g3[:, :, CHUNK - 1:CHUNK].broadcast_to([8, 8, CHUNK]), g3, ALU.subtract, after=[m])
        kd_ready = self.a(X1, X1, ACT.Exp, after=[m])
        be_ready = self.v("tt", BE, BT, EG, ALU.mult, after=[eg_ready, got[0]])
        bank = self.mix.next()
        kinds = (G, BT, BE, X1)
        done = self.transposes([(bank.ap[:, (a * 4 + n) * 8:(a * 4 + n + 1) * 8], r[:, a * P:(a + 1) * P], 8)
                                for a in range(4) for n, r in enumerate(kinds)],
                               [g_ready, kd_ready, be_ready, bank.free])
        TM = self.token_gates[:, :].rearrange("p (a k h) -> p a k h", a=4, k=4)
        tm_ready = self.v("copy", self.token_gates[:, :], bank.ap[:, 0:128], after=[done])
        bank.free = [tm_ready]

        def take_qk(n, f, ps, done, bank):
            dst, scale = (QA[:, f, :], HD ** -0.5) if f < 4 else (KA[:, f - 4, :], 1.0)
            m = self.a(dst, ps, ACT.Copy, after=[done, before], scale=scale)
            bank.free = got["qk"] = [m]

        self.linear(w, KT, 0, 1024, part, take_qk)

        def take_v(n, f, ps, done, bank):
            t = self.temps.next()
            m = self.a(t.ap, ps, ACT.Copy, after=[done, t.free])
            bank.free = [m]
            turned = self.mix.next()
            done = self.transposes([(turned.ap[:, a * P:(a + 1) * P], t.ap[:, a * P:(a + 1) * P], P) for a in range(4)],
                                   [m, turned.free])
            t.free = [done]
            m = self.a(VA[:, :, f * P:(f + 1) * P], turned.ap.rearrange("p (a n) -> p a n", a=4), ACT.Copy, after=[done, before])
            turned.free = got["v"] = [m]

        self.linear(w, KT, 1024, 512, part, take_v)
        self.at = gate_work
        self.jobs = self.dilated_attention(tm_ready, QA, KA, VA, YA, lambda: [got["qk"], got["v"]])
        cw = lambda j, f: self.column("conv", 1, skip=12 * j + f)
        conv_done = []

        def take_conv(f0):
            def take(n, f, ps, done, bank):
                f += f0
                x, y, acc = DX[:, f, 3:PAD], DX[:, f, 0:SEQ], self.temps.next()
                m = self.a(x, ps, ACT.Copy, after=[done, pads])
                bank.free = [m]
                m = self.a(acc.ap, y, ACT.Copy, after=[m, acc.free], scale=cw(0, f))
                for j in range(1, 4):
                    m = self.v("stt", acc.ap, DX[:, f, j:j + SEQ], cw(j, f), acc.ap, ALU.mult, ALU.add, after=[m])
                s = self.a(y, acc.ap, ACT.Sigmoid, after=[m])
                m = self.v("tt", y, y, acc.ap, ALU.mult, after=[s], lane=self.pool)
                acc.free = [m]
                conv_done.append(m)
                self.pump()
            return take
        DD = DX[:, :, 0:SEQ]
        self.linear(w, KT, 1536 + 512, 512, part, take_conv(4))
        self.linear(w, KT, 1536, 512, part, take_conv(0))
        self.linear(w, KT, 1536 + 1024, 512, part, take_conv(8))
        while self.jobs:
            self.jobs.pop(0)()

        def take_z(n, f, ps, done, bank):
            m = self.a(ZS[:, f, :], ps, ACT.Sigmoid, after=[done, before])
            m = self.v("tt", ZS[:, f, :], ZS[:, f, :], ps, ALU.mult, after=[m])
            bank.free = got["z"] = [m]
        self.linear(w, KT, 3072, 512, part, take_z)

        before = self.everything()
        self.at = delta_base
        masks = self.area("masks", 8 * P).rearrange("p (m n) -> p m n", m=8)
        pick_head = self.area("pick_head", 8 * P)[0:8].rearrange("p (m n) -> p m n", m=8)
        spread = self.area("spread", 8 * P)[0:16].rearrange("p (m n) -> p m n", m=8)
        sum_rows = self.area("sum_rows", 8 * 16).rearrange("p (m n) -> p m n", m=8)
        norm_rows = self.area("norm_rows", SEQ)[0:16]
        consts = [self.dma(self.sp, o, c, after=before) for o, c in (
            (masks, self.const["masks"]), (spread, self.const["spread_rows"]), (sum_rows, self.const["sum_rows"]),
            (pick_head, self.const["pick_head"]))]
        pick_pair = spread[0:8, 0:4, :]
        after_norms = self.at

        def unit(f, ps, done):
            return self.v("stt", DD[:, f, :], DD[:, f, :], HD ** -0.5 if f < 4 else 1.0, ps, ALU.mult, ALU.mult, after=[done])
        unit_done = self.head_norm([DD[:, f, :] for f in range(8)], 8, 1.0, EPS, [conv_done, consts], sum_rows, spread,
                                   norm_rows, unit)
        QKT = self.area("qk", 8 * SEQ).rearrange("p (h t) -> p h t", h=8)
        KD = self.area("k_decayed", 4 * SEQ).rearrange("p (a n) -> p a n", a=4)
        EGL = self.small[:, 160:192].rearrange("p (k n) -> p k n", k=4)
        two = lambda name, n: self.area(name, n)
        works = [dict(B=two("B", 1024), U=two("U", 1024), T=two("T", 1024), W=two("W", 1024), VB=two("vb", SEQ),
                      KBE=two("kbe", SEQ), free=[before]) for _ in range(2)]
        turns = [self.mix, self.banks]
        eye8 = self.eye[:].rearrange("p (o n) -> p o n", o=1).broadcast_to([P, 8, P])

        def within_chunks(pair, work, turn):
            B_, U_, T_, W_ = (work[n].rearrange("p (o t) -> p o t", o=2) for n in "BUTW")
            VB, KBE = (work[n].rearrange("p (a o n) -> p a o n", a=4, o=2) for n in ("VB", "KBE"))
            flat8 = lambda x: x.rearrange("p o (a c) -> p (o a) c", c=P)
            four = lambda x: x.rearrange("p (a c) -> p a c", a=4)
            free = [work["free"]]
            bank = turn.next()
            done = self.mm(bank.ap, [(pick_pair[:, pair, :], BT)], [got[0], consts, bank.free])
            t = self.temps.next()
            kb = self.v("tt", t.ap, DD[:, 4 + pair, :], bank.ap, ALU.mult, after=[done, unit_done, t.free])
            bank.free = [kb]
            ready = []
            for o in range(2):
                h, po = 2 * pair + o, HD * o
                bank = turn.next()
                done = self.mm(bank.ap, [(pick_head[:, h, :], G)], [g_ready, consts, bank.free])
                dec = W_[:, o, :]
                for a in range(4):
                    m = self.v("ts", dec[:, a * P:(a + 1) * P], bank.ap[:, a * P:(a + 1) * P],
                               TM[:, a, 0, h:h + 1], 0.0, ALU.subtract, ALU.min, after=[done, tm_ready, free])
                bank.free = [m]
                m = self.a(dec, dec, ACT.Exp, after=[m])
                for dst, rhs, mask in ((B_[:, o, :], t.ap, 0), (QKT[:, h, :], DD[:, pair, :], 1)):
                    bank = turn.next()

                    def emit(e, bank=bank, rhs=rhs, po=po):
                        for a in range(4):
                            c = slice(a * P, (a + 1) * P)
                            last = e.matmul(bank.ap[:, c], DD[po:po + HD, 4 + pair, c], rhs[po:po + HD, c], start=True, stop=True)
                        return last
                    done = self.pe.do(emit, [kb, unit_done, bank.free])
                    t_used = done
                    d = self.v("tt", dst, bank.ap, dec, ALU.mult, after=[done, m, free])
                    bank.free = [d]
                    d = self.v("tt", four(dst), four(dst), masks[:, mask:mask + 1, :].broadcast_to([P, 4, P]), ALU.mult,
                               after=[d], lane=self.pool)
                    ready.append(d)
                yield
            t.free = [t_used]
            for tile, outs in ((4 + pair, ((KBE, 2), (KD[:, :, 2 * pair * HD:2 * (pair + 1) * HD]
                                                      .rearrange("p a (o n) -> p a o n", o=2), 3))), (8 + pair, ((VB, 1),))):
                bank = turn.next()
                done = self.transposes([(bank.ap[:, a * P:(a + 1) * P], DD[:, tile, a * P:(a + 1) * P], P) for a in range(4)],
                                       [unit_done, conv_done, bank.free])
                src = bank.ap.rearrange("p (a o n) -> p a o n", a=4, o=2)
                for dst, kind in outs:
                    m = self.v("tt", dst, src, TM[:, :, kind, 2 * pair:2 * pair + 2]
                               .rearrange("p a (o n) -> p a o n", n=1).broadcast_to([P, 4, 2, HD]), ALU.mult,
                               after=[done, tm_ready, free])
                bank.free = [m]
            tok_ready = m
            yield
            level0 = masks[:, 0:1, :]
            first = self.v("tt", flat8(W_), flat8(B_), self.mask_below.rearrange("p (o n) -> p o n", o=1)
                           .broadcast_to([P, 8, P]), ALU.mult, after=[ready, self.below_ready])
            mu = self.v("tt", flat8(U_), eye8, flat8(W_), ALU.subtract, after=[first, free])
            prev = [mu]
            for o in range(2):
                bank = turn.next()
                done = self.transposes([(bank.ap[:, a * P:(a + 1) * P], U_[:, o, a * P:(a + 1) * P], P) for a in range(4)],
                                       [mu, bank.free])
                m = self.a(T_[:, o, :], bank.ap, ACT.Copy, after=[done, free])
                bank.free = [m]
                prev.append(m)
            yield

            def product(lhs, rhs, after):
                out = []
                for o in range(2):
                    bank = turn.next()

                    def emit(e, bank=bank, o=o):
                        for a in range(4):
                            c = slice(a * P, (a + 1) * P)
                            last = e.matmul(bank.ap[:, c], lhs[:, o, c], rhs[:, o, c], start=True, stop=True)
                        return last
                    out.append((bank, self.pe.do(emit, [after, bank.free])))
                return out

            for level in range(1, 6):
                now = []
                for o, (bank, done) in enumerate(product(B_, T_, prev)):
                    m = self.v("tt", four(W_[:, o, :]), four(bank.ap), masks[:, 2 + level:3 + level, :]
                               .broadcast_to([P, 4, P]), ALU.mult, after=[done, prev])
                    bank.free = [m]
                    now.append(m)
                yield
                u_new = product(W_, U_, now)
                t_new = product(U_, W_, now) if level < 5 else []
                prev = []
                for o, (bank, done) in enumerate(u_new):
                    m = self.v("tt", U_[:, o, :], U_[:, o, :], bank.ap, ALU.subtract,
                               after=[done, t_new[-1][1] if t_new else u_new[-1][1]])
                    bank.free = [m]
                    prev.append(m)
                for o, (bank, done) in enumerate(t_new):
                    m = self.v("tt", T_[:, o, :], T_[:, o, :], bank.ap, ALU.subtract, after=[done])
                    bank.free = [m]
                    prev.append(m)
                yield
            bank = turn.next()

            def emit(e, bank=bank):
                for a in range(4):
                    for o in range(2):
                        last = e.matmul(bank.ap[:, (a * 2 + o) * HD:(a * 2 + o + 1) * HD], U_[:, o, a * P:(a + 1) * P],
                                        VB[:, a, o, :], start=True, stop=True)
                return last
            done = self.pe.do(emit, [prev, tok_ready, bank.free])
            m1 = self.a(DD[:, 8 + pair, :], bank.ap, ACT.Copy, after=[done])
            bank.free = [m1]
            bank = turn.next()

            def emit(e, bank=bank):
                for a in range(4):
                    for o in range(2):
                        last = e.matmul(bank.ap[HD * o:HD * (o + 1), a * P:(a + 1) * P], KBE[:, a, o, :],
                                        U_[:, o, a * P:(a + 1) * P], start=True, stop=True)
                return last
            done_w = self.pe.do(emit, [bank.free])
            m2 = self.a(DD[:, 4 + pair, :], bank.ap, ACT.Copy, after=[done_w])
            bank.free = [m2]
            bank = turn.next()
            done = self.mm(bank.ap, [(pick_pair[:, pair, :], EG)], [eg_ready, bank.free])
            m3 = self.v("tt", DD[:, pair, :], DD[:, pair, :], bank.ap, ALU.mult, after=[done, t_used])
            m4 = self.v("copy", EGL[:, pair, :], bank.ap.rearrange("p (n c) -> p n c", c=CHUNK)[:, :, CHUNK - 1], after=[done])
            bank.free = [m4]
            work["free"] = [done_w, ready, m4]
            work["done"] = [work.get("done", ()), m1, m2, m3, m4, ready]

        self.mask_below = self.area("below", P)
        bank = self.mix.next()
        done = self.transposes([(bank.ap[:, 0:P], masks[:, 2, :], P)], [consts, bank.free])
        self.below_ready = self.v("copy", self.mask_below, bank.ap[:, 0:P], after=[done])
        bank.free = [self.below_ready]
        runs = [self.chain(within_chunks(n, works[n], turns[n]), within_chunks(n + 2, works[n], turns[n])) for n in range(2)]
        next(runs[1], None)
        while runs:
            runs = [r for r in runs if next(r, "end") != "end"]
        solved = [works[0]["done"], works[1]["done"]]
        self.at = after_norms
        Y = self.halves("mixed", KT, SEQ)
        YD = self.area("delta_out", 4 * SEQ).rearrange("p (k t) -> p k t", k=4)
        idle = self.everything()
        S = self.tmp[:, 0, 0:256].rearrange("p (k n) -> p k n", k=4)
        SG = self.tmp[:, 0, 256:512].rearrange("p (k n) -> p k n", k=4)
        VN = self.tmp[:, 1, :].rearrange("p (o k n) -> p o k n", o=2, k=4)
        s_ready = self.v("set", self.tmp[:, 0, :], 0.0, after=idle)
        vn_free = idle
        heads = [(h, h // 2, HD * (h % 2)) for h in range(8)]
        pairs_of_banks = [(self.banks.banks[0], self.banks.banks[1]), (self.banks.banks[2], self.banks.banks[3])]
        quarter = lambda ap: ap.rearrange("p (k n) -> p k n", k=4)
        for n in range(SEQ // CHUNK):
            a, p0 = n // 2, CHUNK * (n % 2)
            c = slice(n * CHUNK, (n + 1) * CHUNK)
            bank_v = [self.mix.next(), self.mix.next()]
            bank_o, bank_s = pairs_of_banks[n % 2]

            def emit(e, bank=bank_v, p0=p0, c=c):
                for h, k, po in heads:
                    last = e.matmul(bank[h % 2].ap[p0:p0 + CHUNK, k * HD:(k + 1) * HD], DD[po:po + HD, 4 + k, c],
                                    S[po:po + HD, k, :], start=True, stop=True)
                return last
            done_v = self.pe.do(emit, [s_ready, bank_v[0].free, bank_v[1].free, solved])

            def emit(e, bank=bank_o, c=c):
                for h, k, po in heads:
                    last = e.matmul(bank.ap[po:po + HD, k * HD:(k + 1) * HD], S[po:po + HD, k, :], DD[po:po + HD, k, c],
                                    start=k == 0, stop=False, skip_group_check=True)
                return last
            done_q = self.pe.do(emit, [bank_o.free])
            vn = []
            for o in range(2):
                u = DD[p0:p0 + CHUNK, 8:12, (2 * a + o) * HD:(2 * a + o + 1) * HD]
                vn.append(self.v("tt", VN[p0:p0 + CHUNK, o], u, quarter(bank_v[o].ap[p0:p0 + CHUNK, 0:256]), ALU.subtract,
                                 after=[done_v, vn_free]))
                bank_v[o].free = [vn[-1]]
            sg = self.v("tt", SG, S, EGL[:, :, n:n + 1].broadcast_to([P, 4, HD]), ALU.mult, after=[s_ready, solved],
                        lane=self.pool)

            def emit(e, bank=bank_s, p0=p0, a=a):
                for h, k, po in heads:
                    last = e.matmul(bank.ap[po:po + HD, k * HD:(k + 1) * HD], KD[p0:p0 + CHUNK, a, h * HD:(h + 1) * HD],
                                    VN[p0:p0 + CHUNK, h % 2, k, :], start=True, stop=True)
                return last
            done_s = self.pe.do(emit, [vn, bank_s.free])

            def emit(e, bank=bank_o, p0=p0, n=n):
                for h, k, po in heads:
                    last = e.matmul(bank.ap[po:po + HD, k * HD:(k + 1) * HD], VN[p0:p0 + CHUNK, h % 2, k, :],
                                    QKT[p0:p0 + CHUNK, h, n * CHUNK:(n + 1) * CHUNK], start=False, stop=True,
                                    skip_group_check=True)
                return last
            done_o = self.pe.do(emit, [done_q])
            s_ready = self.v("tt", S, SG, quarter(bank_s.ap[:, 0:256]), ALU.add, after=[done_s, done_q, sg])
            bank_s.free = [s_ready]
            m = self.a(YD[:, :, c], quarter(bank_o.ap[:, 0:256]), ACT.Copy, after=[done_o, before])
            bank_o.free = [m]
            vn_free = [done_o]
        idle = self.everything()
        self.temps.banks[0].free = self.temps.banks[1].free = idle
        parts_ready = [self.split(YA[:, k, :], Y[0][:, k, :], Y[1][:, k, :], [self.attention_done, idle]) for k in range(4)]

        def gated(f, ps, done):
            m = self.v("tt", ZS[:, f, :], ZS[:, f, :], ps, ALU.mult, after=[done, got["z"]])
            m = self.v("stt", YD[:, f, :], YD[:, f, :], self.norm_g, ZS[:, f, :], ALU.mult, ALU.mult, after=[m, self.small_ready])
            parts_ready.append(self.split(YD[:, f, :], Y[0][:, 4 + f, :], Y[1][:, 4 + f, :], [m, idle]))
            return parts_ready[-1]
        self.head_norm([YD[:, f, :] for f in range(4)], 4, 1.0 / HD, EPS, [m], sum_rows, spread, norm_rows, gated)
        self.pump(max(0, len(self.background) - KT * 3))
        self.finish_modulation()
        m_g1 = self.mod_ready
        main_h = [()]

        def take_out(n, f, ps, done, bank):
            m = self.v("stt", main.h[:, f, :], ps, vec(2)[:, f:f + 1], main.h[:, f, :], ALU.mult, ALU.add, after=[done, m_g1])
            bank.free = main_h[0] = [m]
        self.linear(i["w_out"][0], KT, 0, D, [(Y, SEQ, parts_ready)], take_out)
        self.pump(len(self.background))
        self.finish_modulation()
        main.h_ready = main_h[0]

        before = self.everything()
        self.at = self.phase_base
        main.hn = self.halves("hn", KT, SEQ)
        hidden = self.halves("hidden", GROUPS[0][1], SEQ)
        main.hn_free = before
        g = self.gains(0, "norm_ffn", vec(4), [self.mod_ready])
        self.modulated_norm(main, self.gain[:, :, 0:1], vec(3), [g])
        self.background, self.rate = self.modulation_jobs(0), 2
        self.swiglu([main], [hidden], i["w_gate"][0], 0, i["w_up"][0], 0, i["w_down"][0], lambda part: vec(5), before)
        self.pump(len(self.background))
        self.finish_modulation()
        self.rate = 1
        self.plain_norm(main, "final")

    def chain(self, *generators):
        for g in generators:
            yield from g

    def modulation_jobs(self, layer):
        bias = self.column(f"b_ada{layer}", N_MOD2 * KT)
        return [lambda j=j: self.modulation(self.inp["w_ada_2"][layer], j, self.mod2[layer], (1, 2), [self.cond_ready], bias)
                for j in range(N_MOD2 * KT)]

    def plain_norm(self, part, name):
        T = part.T
        rinv, ready, t = self.mean_square_root([part.h[:, k, 0:T] for k in range(KT)], T, self.ones, 1.0 / D, part.h_ready)
        for k in range(KT):
            m = self.v("stt", part.h[:, k, 0:T], part.h[:, k, 0:T], self.column(name, 1, skip=k), rinv, ALU.mult, ALU.mult,
                       after=[ready])
        t.free = [m]
        part.h_ready = [m]

    def half_step(self, parts, layer, names, first):
        mod, mod_ready = self.mod2[layer], self.mod_ready
        rows = lambda j, c: mod[:, j * KT:(j + 1) * KT, c]
        before, hidden = self.everything(), []
        self.at = self.phase_base
        for part in parts:
            part.hn = self.halves("hn", KT, part.T)
            hidden.append(self.halves("hidden", GROUPS[0][1], part.T))
            part.hn_free = before
        for part in parts:
            g = self.gains(part.col, f"{names}{layer}", rows(first + 1, part.col), [mod_ready])
            self.modulated_norm(part, self.gain[:, :, part.col:part.col + 1], rows(first, part.col), [g])
        half = {}
        for part in parts:
            half[part.name] = self.small[:, 96 + part.col * KT:96 + (part.col + 1) * KT]
            m = self.v("ts", half[part.name], rows(first + 2, part.col), 0.5, None, ALU.mult, after=[mod_ready])
            part.h_ready = [part.h_ready, m]
        w13, w2 = self.inp[f"w13_{names[2:]}_2"][layer], self.inp[f"w2_{names[2:]}_2"][layer]
        self.swiglu(parts, hidden, w13, 0, w13, D_FF, w2, lambda part: half[part.name], before)

    def gelu(self, x, ready):
        t = self.temps.next()
        u = t.ap[:, 0:x.shape[1]]
        c = 2 * math.sqrt(2 / math.pi)
        m = self.v("tt", u, x, x, ALU.mult, after=[ready, t.free], lane=self.pool)
        m = self.v("ts", u, u, 0.044715 * c, c, ALU.mult, ALU.add, after=[m])
        m = self.v("tt", u, u, x, ALU.mult, after=[m], lane=self.pool)
        m = self.a(u, u, ACT.Sigmoid, after=[m])
        m = self.v("tt", x, x, u, ALU.mult, after=[m])
        t.free = [m]
        return m

    def mixers(self, part, layer, kv_only):
        i, T, name = self.inp, part.T, part.name
        nt = T // P
        w_in = i["w_in_2"][layer]
        mod = self.mod2[layer]
        rows = lambda j: mod[:, j * KT:(j + 1) * KT, part.col]
        base = self.everything()
        keys = SEQ + CTX
        own = 0 if name == "main" else SEQ
        tiled = lambda name, k, n: self.area(name, k * n).rearrange("p (k n) -> p k n", k=k)
        self.at = self.phase_base
        if part is self.side:
            self.kv = tiled("k_nope", 2, keys), self.area("k_rope", keys), tiled("values", keys // P, GW)
            self.kv_end = self.at
        KN, KR, VT = self.kv
        self.at = self.kv_end
        CKV = self.area("kv_rank", T)
        after_kv = self.at
        if kv_only:
            part.hn = self.halves("hn", KT, T)
        else:
            CQ = tiled("q_rank", 2, T)[0:96]
            QN, QR = tiled("q_nope", 2, T), self.area("q_rope", T)
            F_, U_, V_, PZ = tiled("fourier", 2, T), tiled("sgu_u", 2, T), tiled("sgu_v", nt, GW), tiled("pool", 2, T + 16)
            head_dft, turn = self.area("head_dft", P), self.area("turn", P)
            inv = tiled("inverse", 2, T)
            wf, wp, R_ = tiled("w_fnet", 2, HD), tiled("w_pool", 2, HD), tiled("rows", 2, P)
            WST, BB = tiled("w_sgu", HEADS2, P), tiled("b_sgu", 2, P)
            rope = tiled("rope", 2, SEQ)
            dft_area, pt_area = self.area("token_dft", 8 * SEQ), self.area("weights_t", max(6 * T, (nt + 1) * 512))
            score_area = self.area("scores", 2 * keys)
            dft = dft_area[:, 0:2 * nt * T].rearrange("p (c a t) -> p c a t", c=2, a=nt)
            self.at -= 4 * 2 * keys
            sums = [self.area("sums", T + 16) for _ in range(2)]
            self.at += 4 * (2 * keys - 2 * (T + 16))
            scores = Turn([Bank(score_area[:, n * keys:(n + 1) * keys]) for n in range(2)])
            PT = Turn([Bank(a[:, 0:6 * T].rearrange("p (a t) -> p a t", a=6)) for a in (pt_area, dft_area)])
            raw_ws = pt_area[:, nt * 512:nt * 512 + HEADS2 * P].rearrange("p (h n) -> p h n", h=HEADS2)
            YT = pt_area[:, 0:nt * 512].rearrange("p (a n) -> p a n", a=nt)
            hn_at = self.at
            part.hn = self.halves("hn", KT, T)
            self.at = hn_at
            YS = self.halves("mixed", KT, T)
        g = self.gains(part.col, f"g_mix{layer}", rows(4), [self.mod_ready])
        part.hn_free = base
        self.modulated_norm(part, self.gain[:, :, part.col:part.col + 1], rows(3), [g])
        sp = self.sp

        def section(c0, width, tile, put):
            self.linear(w_in, KT, c0, width, [(part.hn, T, part.hn_ready)], put, tile=tile)

        def mixed(k, x, after, rows_=slice(None)):
            return self.split(x, YS[0][rows_, k, :], YS[1][rows_, k, :], [after, hn_read])

        got = {}

        def copy_to(dst, key):
            def put(n, f, ps, done, bank):
                m = self.a(dst(f), ps, ACT.Copy, after=[done, base])
                bank.free = [m]
                got[key] = m
            return put

        section(448, KV_RANK, P, copy_to(lambda f: CKV, "ckv"))
        repeat = self.small_const("repeat", self.const["repeat"])

        def put_kr(n, f, ps, done, bank):
            t = self.temps.next()
            m = self.a(t.ap[0:ROPE, 0:T], ps, ACT.Copy, after=[done, t.free])
            bank.free = [m]
            wide = self.mix.next()
            done = self.mm(wide.ap[:, 0:T], [(repeat[0][0:ROPE], t.ap[0:ROPE, 0:T])], [m, repeat[1], wide.free])
            t.free = [done]
            m = self.a(KR[:, own:own + T], wide.ap[:, 0:T], ACT.Copy, after=[done, base])
            wide.free = [m]
            got["kr"] = m
        section(576, ROPE, ROPE, put_kr)
        kr_ready = got["kr"]
        if not kv_only:
            loads = [self.dma(sp, o, c, after=base) for o, c in (
                (head_dft, self.const["head_dft"]), (turn, self.const["turn"]), (inv, self.const["pool_" + name]),
                (rope, self.const["rope"]), (dft, self.const["token_dft_" + name]),
                (raw_ws, i["w_sgu_2"][layer].rearrange("h p q -> p h q")))]
            for h in range(HEADS2):
                half = slice(HD * (h % 2), HD * (h % 2 + 1))
                loads.append(self.dma(sp, wf[half, h // 2, :], i["w_fnet_2"][layer, h], after=base))
                loads.append(self.dma(sp, wp[half, h // 2, :], i["w_pool_2"][layer, h], after=base))
                b = i["b_sgu_2"][layer, h]
                loads.append(self.dma(sp, BB[half, h // 2, :], bass.AP(b.tensor, b.offset, [[0, HD], [1, P]]), after=base))
            pads = self.v("set", PZ, 0.0, after=base, lane=self.pool)
            section(256, Q_RANK, 96, copy_to(lambda f: CQ[:, f, :], "cq"))
            section(0, GW, P, copy_to(lambda f: F_[:, f, :], "f"))

            def put_u(n, f, ps, done, bank):
                m = self.a(U_[:, f, :], ps, ACT.Copy, after=[done, base])
                bank.free = [m]
                got["u"] = self.gelu(U_[:, f, :], [m])
            section(608, GW, P, put_u)

            def put_v(n, f, ps, done, bank):
                t = self.temps.next()
                x = t.ap[:, 0:T]
                m = self.a(x, ps, ACT.Copy, after=[done, t.free])
                bank.free = [m]
                m = self.gelu(x, [m])
                turned = self.mix.next()
                done = self.transposes([(turned.ap[:, a * P:(a + 1) * P], x[:, a * P:(a + 1) * P], P) for a in range(nt)],
                                       [m, turned.free])
                t.free = [done]
                m = self.a(V_[:, :, f * P:(f + 1) * P], turned.ap[:, 0:T].rearrange("p (a n) -> p a n", a=nt), ACT.Copy,
                           after=[done, base])
                turned.free = [m]
                got["v"] = m
            section(864, GW, P, put_v)

            def put_p(n, f, ps, done, bank):
                m = self.a(PZ[:, f, 8:8 + T], ps, ACT.Copy, after=[done, pads])
                bank.free = [m]
                got["p"] = m
            section(1120, GW, P, put_p)
            hn_read = [(self.pe.sem, self.pe.count)]

        def rank_norm(tiles, rows_, gain, ready):
            rinv, m, t = self.mean_square_root(tiles, T, self.ones, 1.0 / (rows_ * len(tiles)), [ready], rows=rows_)
            for f, x in enumerate(tiles):
                last = self.v("stt", x, x, self.column(gain, 1, skip=f)[0:rows_], rinv[0:rows_], ALU.mult, ALU.mult, after=[m])
            t.free = [last]
            return last

        kv_ready = rank_norm([CKV], P, f"g_kv{layer}", got["ckv"])
        src = i["w_ukv_2"][layer].rearrange("(k p) (h n) -> p k h n", p=P, h=HEADS2)
        slot, (w_k, w_v), landed = self.pieces([(0, P, 1, GW, src[:, :, :, 0:HD]), (GW, P, 1, GW, src[:, :, :, HD:2 * HD])])
        for k in range(2):
            bank = self.mix.next()
            done = self.mm(bank.ap[:, 0:T], [(w_k[:, 0, k * P:(k + 1) * P], CKV)], [landed, kv_ready, bank.free])
            m = self.a(KN[:, k, own:own + T], bank.ap[:, 0:T], ACT.Copy, after=[done, base])
            bank.free = [m]
        kn_ready = m
        for a in range(nt):
            bank = self.mix.next()
            done = self.mm(bank.ap[:, 0:GW], [(CKV[:, a * P:(a + 1) * P], w_v[:, 0, :])], [bank.free])
            m = self.a(VT[:, own // P + a, :], bank.ap[:, 0:GW], ACT.Copy, after=[done, base])
            bank.free = [m]
        slot.free = [done]
        vt_ready = m
        if name == "main":
            kr_ready = self.turned(KR[:, 0:T], turn, rope, [kr_ready, loads])
        part.kv = [kn_ready, vt_ready, kr_ready]
        if kv_only:
            return
        q_ready = rank_norm([CQ[:, 0, :], CQ[:, 1, :]], 96, f"g_q{layer}", got["cq"])
        src = i["w_uq_2"][layer].rearrange("(k p) (h n) -> p k h n", p=96, h=HEADS2)
        slot, (w_nope, w_rope), landed = self.pieces([(0, 96, 2, GW, src[:, :, :, 0:HD]),
                                                      (2 * GW, 96, 2, P, src[:, :, :, HD:HD + ROPE])])
        for k in range(2):
            bank = self.mix.next()
            done = self.mm(bank.ap[:, 0:T], [(w_nope[:, n, k * P:(k + 1) * P], CQ[:, n, :]) for n in range(2)],
                           [landed, q_ready, bank.free])
            m = self.a(QN[:, k, :], bank.ap[:, 0:T], ACT.Copy, after=[done, base])
            bank.free = [m]
        qn_ready = m
        bank = self.mix.next()
        done = self.mm(bank.ap[:, 0:T], [(w_rope[:, n, :], CQ[:, n, :]) for n in range(2)], [bank.free])
        slot.free = [done]
        qr_ready = self.a(QR, bank.ap[:, 0:T], ACT.Copy, after=[done, base])
        bank.free = [qr_ready]
        if name == "main":
            qr_ready = self.turned(QR, turn, rope, [qr_ready, loads])

        for h in range(HEADS2):
            po, k = HD * (h % 2), h // 2
            bank = self.mix.next()

            def emit(e, bank=bank, po=po, k=k):
                for c in range(2):
                    last = e.matmul(bank.ap[po:po + HD, c * HD:(c + 1) * HD], head_dft[po:po + HD, c * HD:(c + 1) * HD],
                                    wf[po:po + HD, k, :], start=True, stop=True)
                return last
            done = self.pe.do(emit, [loads, bank.free])
            m = self.v("copy", R_[po:po + HD, k, :], bank.ap[po:po + HD, 0:P], after=[done])
            bank.free = [m]
        for a in range(nt):
            bank = [self.mix.next(), self.mix.next()]

            def emit(e, bank=bank, a=a):
                for h in range(HEADS2):
                    po, k = HD * (h % 2), h // 2
                    last = e.matmul(bank[h % 2].ap[:, k * P:(k + 1) * P], F_[po:po + HD, k, a * P:(a + 1) * P],
                                    R_[po:po + HD, k, :], start=True, stop=True)
                return last
            done = self.pe.do(emit, [m, got["f"], bank[0].free, bank[1].free])
            m2 = []
            for o in range(2):
                dst = YT[:, a, :].rearrange("p (c k o n) -> p o c k n", k=2, o=2, c=2)[:, o]
                m2.append(self.v("copy", dst, bank[o].ap[:, 0:2 * P].rearrange("p (k c n) -> p c k n", k=2, c=2),
                                 after=[done, base]))
                bank[o].free = [m2[-1]]
        for k in range(2):
            bank = self.mix.next()
            pairs = [(YT[:, a, c * GW + k * P:c * GW + (k + 1) * P], dft[:, c, a, :])
                     for c in range(2) for a in range(nt)]
            done = self.mm(bank.ap[:, 0:T], pairs, [m2, bank.free])
            m = mixed(k, bank.ap[:, 0:T], [done])
            bank.free = [m]
        fourier_ready = m
        bank = self.mix.next()
        done = self.transposes([(bank.ap[:, h * P:(h + 1) * P], raw_ws[:, h, :], P) for h in range(HEADS2)], [loads, bank.free])
        ws_ready = self.v("copy", WST.rearrange("p h n -> p (h n)"), bank.ap, after=[done])
        bank.free = [ws_ready]
        for a in range(nt):
            t = self.temps.next()
            v3 = lambda x: x.rearrange("p (h d) -> p h d", h=HEADS2)
            sq, st = t.ap[:, 0:GW], t.ap[:, GW:GW + HEADS2]
            m = self.v("tt", sq, V_[:, a, :], V_[:, a, :], ALU.mult, after=[got["v"], t.free], lane=self.pool)
            m = self.v("sum", st, v3(sq), after=[m])
            m = self.v("ts", st, st, 1.0 / HD, EPS, ALU.mult, ALU.add, after=[m])
            m = self.a(st, st, ACT.Sqrt, after=[m])
            m = self.v("recip", st, st, after=[m])
            m = self.v("tt", v3(V_[:, a, :]), v3(V_[:, a, :]),
                       st.rearrange("p (h o) -> p h o", o=1).broadcast_to([P, HEADS2, HD]), ALU.mult, after=[m])
            t.free = [m]
        v_ready = m
        for k in range(2):
            bank = self.mix.next()

            def emit(e, bank=bank, k=k):
                for a in range(nt):
                    for o in range(2):
                        h = 2 * k + o
                        last = e.matmul(bank.ap[HD * o:HD * (o + 1), a * P:(a + 1) * P], V_[:, a, h * HD:(h + 1) * HD],
                                        WST[:, h, :], start=True, stop=True)
                return last
            done = self.pe.do(emit, [v_ready, ws_ready, bank.free])
            blocks = lambda x: x.rearrange("p (a n) -> p a n", n=P)
            t = self.temps.next()
            y = t.ap[:, 0:T]
            m = self.v("stt", blocks(y), blocks(bank.ap[:, 0:T]), self.column(f"g_sgu{layer}", 1, skip=k),
                       BB[:, k:k + 1, :].broadcast_to([P, nt, P]), ALU.mult, ALU.add, after=[done, t.free])
            bank.free = [m]
            m = self.v("tt", y, y, U_[:, k, :], ALU.mult, after=[m, got["u"]])
            m = mixed(4 + k, y, [m])
            t.free = [m]
        sgu_ready = m
        E = T + 16
        prev = [got["p"]]
        for k in range(2):
            z = PZ[:, k, :]
            held = self.temps.next()
            pooled = held.ap[:, 0:T]
            prev = [prev, held.free]
            s, w = z, 1
            for n in range(4 if k else 2):
                reach = 2 ** n // 2 if n else 0
                lo, hi = (1, E) if n == 0 else (2 ** n, E - 2 ** n + 1)
                a_, b_ = (-1, 0) if n == 0 else (-reach, reach)
                d = sums[n % 2]
                prev = [self.v("tt", d[:, lo:hi], s[:, lo + a_:hi + a_], s[:, lo + b_:hi + b_], ALU.add, after=[prev, base])]
                s = d
                if n // 2 == k:
                    half = slice(HD * (n % 2), HD * (n % 2 + 1))
                    dst = pooled[half]
                    m = self.v("tt", dst, s[half, 8:8 + T], inv[half, k, :], ALU.mult, after=[prev, loads, base])
                    m = self.v("tt", dst, dst, z[half, 8:8 + T], ALU.subtract, after=[m])
                    prev = [m]
            bank = self.mix.next()

            def emit(e, bank=bank, k=k, pooled=pooled):
                for o in range(2):
                    half = slice(HD * o, HD * (o + 1))
                    last = e.matmul(bank.ap[half, 0:T], wp[half, k, :], pooled[half], start=True, stop=True)
                return last
            done = self.pe.do(emit, [prev, bank.free])
            m = self.v("ts", pooled, bank.ap[:, 0:T], self.column(f"s_pool{layer}", 1, skip=k), None, ALU.mult,
                       after=[done])
            bank.free = [m]
            m = mixed(6 + k, pooled, [m])
            held.free = [m]
        pool_ready = m
        k_lo, k_hi = (0, keys) if name == "main" else (SEQ, keys)
        nk = k_hi - k_lo
        scale = (HD + ROPE) ** -0.5
        mx, sm = self.small[:, 32:48], self.small[:, 48:64]
        pt_first = [(self.pe.sem, self.pe.count), (self.dve.sem, self.dve.count)]
        all_kv = [self.side.kv, part.kv]
        four = self.banks.banks + self.mix.banks
        assert not any(b.taken for b in four)
        pairs = Turn([Bank((self.ps[:, n:n + 2, :].rearrange("p a n -> p (a n)"), n)) for n in range(0, 8, 2)])
        for n, b in enumerate(pairs.banks):
            b.free = [four[2 * n].free, four[2 * n + 1].free]

        def rows_of_scores(h, qt):
            po, k = HD * (h % 2), h // 2
            bank = pairs.next()
            wide = bank.ap[0]
            q = slice(qt * P, (qt + 1) * P)

            def emit(e):
                for lo in range(0, nk, 512):
                    n = min(512, nk - lo)
                    key = slice(k_lo + lo, k_lo + lo + n)
                    e.matmul(wide[:, lo:lo + n], QN[po:po + HD, k, q], KN[po:po + HD, k, key], start=True, stop=False)
                    last = e.matmul(wide[:, lo:lo + n], QR[ROPE * h:ROPE * (h + 1), q], KR[ROPE * h:ROPE * (h + 1), key],
                                    start=False, stop=True, tile_position=(ROPE * h, 0))
                return last
            done = self.pe.do(emit, [all_kv, qn_ready, qr_ready, bank.free])
            c = slice(h * nt + qt, h * nt + qt + 1)
            s = scores.next()
            m = self.v("max", mx[:, c], wide[:, 0:nk], after=[done])
            m = self.v("ts", mx[:, c], mx[:, c], -scale, None, ALU.mult, after=[m])
            m = self.a(s.ap[:, 0:nk], wide[:, 0:nk], ACT.Exp, after=[m, s.free, pt_first], bias=mx[:, c], scale=scale,
                       accum_out=sm[:, c])
            bank.free = [m]
            m = self.v("recip", sm[:, c], sm[:, c], after=[m])
            m = self.v("ts", s.ap[:, 0:nk], s.ap[:, 0:nk], sm[:, c], None, ALU.mult, after=[m])
            return h, qt, s, m

        def weigh_values(h, qt, s, m):
            po, k = HD * (h % 2), h // 2
            q = slice(qt * P, (qt + 1) * P)
            if qt == 0:
                got["pt"] = PT.next()
            pt = got["pt"]
            bank = pairs.next()
            wide = bank.ap[0]
            done = self.transposes([(wide[:, a * P:(a + 1) * P], s.ap[:, a * P:(a + 1) * P], P) for a in range(nk // P)],
                                   [m, bank.free])
            s.free = [done]
            m = self.a(pt.ap[:, 0:nk // P, q], wide[:, 0:nk].rearrange("p (a q) -> p a q", q=P), ACT.Copy,
                       after=[done, pt.free, pt_first])
            bank.free = [m]
            if qt < nt - 1:
                return None
            bank = pairs.next()
            out = bank.ap[0][po:po + HD, 0:T]
            done = self.mm(out, [(VT[:, k_lo // P + a, h * HD:(h + 1) * HD], pt.ap[:, a, 0:T]) for a in range(nk // P)],
                           [m, bank.free])
            pt.free = [done]
            m = mixed(2 + k, out, [done], slice(po, po + HD))
            bank.free = [m]
            return m
        late = None
        for h in range(HEADS2):
            for qt in range(nt):
                now = rows_of_scores(h, qt)
                if late:
                    weigh_values(*late)
                late = now
        m = weigh_values(*late)
        for n, b in enumerate(pairs.banks):
            four[2 * n].free = four[2 * n + 1].free = b.free
        y_ready = [m, fourier_ready, sgu_ready, pool_ready]
        last = [()]

        def take_out(n, f, ps, done, bank):
            m = self.v("stt", part.h[:, f, 0:T], ps, rows(5)[:, f:f + 1], part.h[:, f, 0:T], ALU.mult, ALU.add, after=[done])
            bank.free = last[0] = [m]
        self.linear(i["w_out_2"][layer], KT, 0, D, [(YS, T, y_ready)], take_out)
        part.h_ready = last[0]

    def turned(self, x, turn, rope, ready):
        bank, t = self.mix.next(), self.temps.next()
        done = self.mm(bank.ap, [(turn, x)], [ready, bank.free])
        m = self.v("tt", t.ap, bank.ap, rope[:, 1, :], ALU.mult, after=[done, t.free])
        bank.free = [m]
        m2 = self.v("tt", x, x, rope[:, 0, :], ALU.mult, after=[done])
        m = self.v("tt", x, x, t.ap, ALU.add, after=[m, m2])
        t.free = [m]
        return m

    def small_const(self, name, src):
        if name not in self.loaded:
            n = len(self.loaded)
            view = self.small_consts[0:src.shape[0], n * P:n * P + src.shape[1]]
            self.loaded[name] = (view, self.dma(self.sp, view, src))
        return self.loaded[name]

    def second_block(self):
        main, side = self.main, self.side
        both = [main, side]
        for layer in range(2):
            self.background = self.modulation_jobs(1) if layer == 0 else []
            self.half_step(both, layer, "g_ffn1", 0)
            self.mixers(side, layer, layer == 1)
            self.mixers(main, layer, False)
            self.half_step(both if layer == 0 else [main], layer, "g_ffn2", 6)
            self.pump(len(self.background))
            self.finish_modulation()
        self.plain_norm(main, "final2")
        free = self.everything()
        self.at = self.phase_base
        stage = self.area("tokens_out", 4 * D).rearrange("p (a n) -> p a n", a=4)
        for a in range(4):
            for half in range(2):
                bank = self.mix.next()
                done = self.transposes([(bank.ap[:, k * P:(k + 1) * P], main.h[:, 4 * half + k, a * P:(a + 1) * P], P)
                                        for k in range(4)], [main.h_ready, bank.free])
                m = self.v("copy", stage[:, a, half * 512:(half + 1) * 512], bank.ap, after=[done, free])
                bank.free = [m]
            self.dram_writes.append(self.dma(self.sp, self.out[0, a * P:(a + 1) * P, :], stage[:, a, :], after=[m],
                                             counter=self.out_landed))
        self.sp.steps.append((marks(self.dram_writes), lambda e: None, None, 0))


def build(nc, scratch, inp, const, out):
    plan = None
    for target in (scratch, nc):
        with ExitStack() as ctx:
            prog = Program(target, ctx, inp, const, out, plan)
            prog.setup()
            prog.first_block()
            prog.second_block()
            plan = prog.asked
            if target is scratch:
                continue
            block = ctx.enter_context(nc.Block())
            block.sync(lambda e: prog.sp.play(e))
            block.gpsimd(lambda e: prog.pool.play(e))
            block.scalar(lambda e: prog.act.play(e))
            block.tensor(lambda e: prog.pe.play(e))
            block.vector(lambda e: prog.dve.play(e))


def kernel(**inputs):
    import concourse.bacc as bacc
    from concourse.bass_utils import run_bass_kernel_spmd

    nc = bacc.Bacc("TRN2", target_bir_lowering=False, num_devices=1)
    arrays, inp, const = {}, {}, {}
    for name, a in inputs.items():
        a = np.ascontiguousarray(a)
        arrays["in_" + name] = a
        inp[name] = nc.dram_tensor("in_" + name, a.shape, F32, kind="ExternalInput").ap()
    for name, a in shape_constants().items():
        arrays["const_" + name] = np.ascontiguousarray(a)
        const[name] = nc.dram_tensor("const_" + name, a.shape, F32, kind="ExternalInput").ap()
    out = nc.dram_tensor("out", (1, SEQ, D), F32, kind="ExternalOutput").ap()
    scratch = bacc.Bacc("TRN2", target_bir_lowering=False, num_devices=1)
    build(nc, scratch, inp, const, out)
    result = run_bass_kernel_spmd(nc, [arrays], core_ids=[0])
    return result.results[0]["out"]
```

```python
from contextlib import ExitStack
import math

import numpy as np

import concourse.bass as bass
from concourse import mybir

F32 = mybir.dt.float32
F32R = mybir.dt.float32r
ALU = mybir.AluOpType
ACT = mybir.ActivationFunctionType
AX_X = mybir.AxisListType.X

P = 128
D = 1024
KT = D // P
SEQ = 512
CTX = 256
HD = 64
D_FF = 2816
FT = D_FF // P
CHUNK = 64
N_BUCKETS, MAX_DISTANCE = 32, 2048
EPS = 1e-6
MASKED = -1e30
STAGES, SLOTS = 4, 3
GROUPS = ((0, 8), (8, 8), (16, 6))
HEADS1 = 8
HEADS2 = 4
Q_RANK, KV_RANK, ROPE = 192, 128, 32
GW = 256
N_MOD1, N_MOD2 = 6, 9
SBUF_END = 229344
SKEW = 640


def shape_constants():
    c = {}
    eye = np.eye(P, dtype=np.float32)
    half = np.arange(P) // HD
    c["eye"] = eye
    c["head_ones"] = (half[:, None] == half[None, :]).astype(np.float32)
    e, t = np.arange(P)[:, None], np.arange(P)[None, :]
    same = e // CHUNK == t // CHUNK
    masks = [same & (e < t), same & (e <= t)]
    for level in range(6):
        n = 2 ** level
        masks.append((e // (2 * n) == t // (2 * n)) & (e // n % 2 == 1) & (t // n % 2 == 0))
    c["masks"] = np.stack(masks, 1).astype(np.float32)
    head_of_row = np.zeros((HEADS1, HEADS1 // 2, P), np.float32)
    for k in range(HEADS1 // 2):
        head_of_row[2 * k, k, :HD] = 1
        head_of_row[2 * k + 1, k, HD:] = 1
    c["pick_pair"] = head_of_row
    c["sum_rows"] = np.zeros((P, 8, 16), np.float32)
    for f in range(8):
        for o in range(2):
            c["sum_rows"][HD * o:HD * (o + 1), f, 2 * f + o] = 1
    c["spread_rows"] = np.ascontiguousarray(c["sum_rows"].transpose(2, 1, 0))
    c["pick_head"] = np.repeat(np.eye(HEADS1, dtype=np.float32)[:, :, None], P, 2)
    d = 511 - np.arange(SKEW)
    dist = np.maximum(d, 0)
    exact = N_BUCKETS // 2
    f = np.maximum(dist, 1).astype(np.float32)
    large = exact + (np.log(f / exact) / math.log(MAX_DISTANCE / exact) * (N_BUCKETS - exact)).astype(np.int32)
    bucket = np.where(dist < exact, dist, np.minimum(large, N_BUCKETS - 1))
    count = (d <= 128).astype(int) + (d % 4 == 0) + (d % 16 == 0)
    seen = (d >= 0) & (count > 0) & (np.arange(SKEW) < 639)
    table = np.zeros((N_BUCKETS + 1, SKEW), np.float32)
    table[bucket[seen], np.arange(SKEW)[seen]] = 1
    table[N_BUCKETS] = np.where(seen, np.log(np.maximum(count, 1)), MASKED)
    c["distance"] = table
    a = 2 * np.pi / HD * (np.arange(HD)[:, None] * np.arange(HD)[None, :] % HD)
    c["head_dft"] = np.concatenate([np.tile(np.cos(a), (2, 1)), np.tile(-np.sin(a), (2, 1))], 1).astype(np.float32)
    for name, length in (("main", SEQ), ("ctx", CTX)):
        a = 2 * np.pi / length * (np.arange(length)[:, None] * np.arange(length)[None, :] % length)
        norm = 1 / math.sqrt(length * HD)
        both = np.stack([np.cos(a) * norm, np.sin(a) * norm], 1)
        both = both.reshape(length // P, P, 2, length).transpose(1, 2, 0, 3)
        c["token_dft_" + name] = both.astype(np.float32)
        t = np.arange(length)
        inv = []
        for w in (2, 4, 8, 16):
            lo, hi = np.clip(t - w // 2, 0, length), np.clip(t - w // 2 + w, 0, length)
            inv.append(np.tile((1 / (hi - lo)).astype(np.float32), (HD, 1)))
        c["pool_" + name] = np.stack([np.concatenate(inv[:2]), np.concatenate(inv[2:])], 1)
    inv = np.power(np.float32(10000.0), -np.arange(0, 16, 2, dtype=np.float32) / np.float32(16))
    t = np.arange(SEQ)
    pos = np.stack([t // 64, t % 64]).astype(np.float32)
    ang = (pos[:, :, None] * inv[None, None, :]).astype(np.float32)
    ang = np.broadcast_to(ang.transpose(0, 2, 1)[:, None], (2, 2, 8, SEQ)).reshape(ROPE, SEQ)
    c["rope"] = np.tile(np.stack([np.cos(ang), np.sin(ang)], 1), (4, 1, 1)).astype(np.float32)
    turn = np.zeros((P, P), np.float32)
    for m in range(P):
        if m // 8 % 2 == 0:
            turn[m + 8, m] = -1
        else:
            turn[m - 8, m] = 1
    c["turn"] = turn
    c["repeat"] = np.tile(np.eye(ROPE, dtype=np.float32), (1, HEADS2))
    return c


class Lane:

    def __init__(self, sem):
        self.sem, self.count, self.steps = sem, 0, []

    def do(self, emit, after=()):
        self.count += 1
        self.steps.append((marks(after), emit, self.sem, 1))
        return (self.sem, self.count)

    def play(self, engine):
        seen = {}
        for waits, emit, sem, amount in self.steps:
            for s, value in waits:
                if seen.get(s.name, 0) < value:
                    engine.wait_ge(s, value)
                    seen[s.name] = value
            last = emit(engine)
            if last is not None:
                last.then_inc(sem, amount)


def marks(after):
    if after is None:
        return []
    if isinstance(after, tuple) and len(after) == 2 and isinstance(after[1], int):
        return [after]
    return [m for a in after for m in marks(a)]


class Counter:

    def __init__(self, sem):
        self.sem, self.count = sem, 0


class Bank:

    def __init__(self, ap):
        self.ap, self.taken, self.last = ap, False, ()

    @property
    def free(self):
        return self.last

    @free.setter
    def free(self, after):
        self.last, self.taken = after, False


class Turn:
    def __init__(self, banks, skip=False):
        self.banks, self.n, self.skip = banks, 0, skip

    def next(self):
        b = self.banks[self.n % len(self.banks)]
        self.n += 1
        while self.skip and b.taken and any(not x.taken for x in self.banks):
            b = self.banks[self.n % len(self.banks)]
            self.n += 1
        assert not b.taken, "taken again before its readers were queued"
        b.taken = True
        return b


class Part:

    def __init__(self, name, tokens, h, hn, col):
        self.name, self.T, self.h, self.hn, self.col = name, tokens, h, hn, col
        self.h_ready, self.hn_ready, self.hn_free = (), (), ()
        self.unfinished, self.squares, self.mean_ready, self.mean, self.mean_free = False, (), None, None, ()


class Program:
    def __init__(self, nc, ctx, inp, const, out, plan):
        self.nc, self.inp, self.const, self.out = nc, inp, const, out
        self.ctx = ctx
        sem = lambda n: ctx.enter_context(nc.semaphore(n))
        self.pe, self.act, self.dve, self.pool, self.sp = (
            Lane(sem(n)) for n in ("pe_done", "act_done", "dve_done", "pool_done", "sp_unused"))
        self.stage_sems = [Counter(sem(f"stage{i}_landed")) for i in range(STAGES)]
        self.misc_sems = [Counter(sem(f"misc{i}_landed")) for i in range(24)]
        self.misc_n = 0
        self.out_landed = Counter(sem("out_landed"))
        self.at, self.names = 16512, 0
        sb = self.place
        self.h_main = sb("h_main", [P, KT, SEQ])
        self.h_ctx = sb("h_ctx", [P, KT, CTX])
        self.stage = sb("stage", [P, STAGES, KT * P])
        self.high = [sb(f"high{n}", [P, KT * P], F32R) for n in range(SLOTS)]
        self.low = [sb(f"low{n}", [P, KT * P], F32R) for n in range(SLOTS)]
        self.tmp = sb("tmp", [P, 4, SEQ])
        self.eye = sb("eye", [P, P])
        self.ones = sb("ones", [P, P])
        self.head_ones = sb("head_ones", [P, P])
        self.vec = sb("vec", [P, 3, P])
        self.mod1 = sb("mod1", [P, N_MOD1 * KT, 1])
        self.mod2 = [sb(f"mod2_{n}", [P, N_MOD2 * KT, 2]) for n in range(2)]
        self.cond = sb("cond", [P, KT, 3])
        self.gain = sb("gain", [P, KT, 3])
        self.small = sb("small", [P, 144])
        self.partial = sb("partial", [P, 2, 2, P])
        self.root = sb("root", [P, SEQ])
        self.mean_main, self.mean_ctx = sb("mean_main", [P, SEQ]), sb("mean_ctx", [P, CTX])
        self.token_gates = sb("token_gates", [P, P])
        self.small_consts, self.loaded = sb("small_consts", [P, 2 * P]), {}
        self.phase_base = self.at
        psum = ctx.enter_context(nc.psum_tensor("psum", [P, 8, 512], F32))
        self.ps = psum
        self.banks = Turn([Bank(psum[:, i, :]) for i in range(4)])
        self.mix = Turn([Bank(psum[:, i, :]) for i in range(4, 8)], skip=True)
        self.stages = Turn([Bank(self.stage[:, i, :]) for i in range(STAGES)])
        self.slots = Turn([Bank((self.high[i], self.low[i])) for i in range(SLOTS)])
        self.partials = Turn([Bank(self.partial[:, i]) for i in range(2)])
        self.plan, self.asked, self.brought, self.ready_blocks = plan, [], 0, {}
        self.jobs, self.background, self.unfinished = [], [], None
        self.roots = Turn([Bank(self.root[:, :])])
        self.temps = Turn([Bank(self.tmp[:, i, :]) for i in range(4)], skip=True)
        self.dram_writes = []
        self.skew = nc.dram_tensor("skew", (HEADS1, P * SKEW), F32, kind="Internal").ap()

    def place(self, name, shape, dtype=F32):
        size = 4 * int(np.prod(shape[1:]))
        assert self.at + size <= SBUF_END, (name, self.at + size - SBUF_END)
        self.names += 1
        t = self.nc.alloc_sbuf_tensor_at(f"{name}_{self.names}", shape, dtype, offset=self.at)
        self.at += (size + 31) // 32 * 32
        return t

    def area(self, name, n):
        return self.place(name, [P, n])[:, :]

    def halves(self, name, tiles, T):
        return [self.place(f"{name}_{part}", [P, tiles, T], F32R) for part in ("high", "low")]

    def everything(self):
        return [(l.sem, l.count) for l in (self.pe, self.act, self.dve, self.pool) if l.count] + \
            [(c.sem, c.count) for c in self.misc_sems if c.count]

    def dma(self, lane, out, in_, after=(), counter=None):
        if counter is None:
            counter = self.misc_sems[self.misc_n % len(self.misc_sems)]
            self.misc_n += 1
        before = [(counter.sem, counter.count)] if counter.count else []
        counter.count += 16
        lane.steps.append((marks([after, before]), lambda e: e.dma_start(out, in_), counter.sem, 16))
        return (counter.sem, counter.count)

    def mm(self, out, pairs, after=(), close=True, open_=True):
        def emit(e):
            for i, (a, b) in enumerate(pairs):
                last = e.matmul(out, a, b, start=open_ and i == 0, stop=close and i == len(pairs) - 1)
            return last
        return self.pe.do(emit, after)

    def transposes(self, triples, after=()):
        def emit(e):
            for out, in_, k in triples:
                last = e.transpose(out, in_, self.eye[0:k, 0:k])
            return last
        return self.pe.do(emit, after)

    def v(self, name, *args, after=(), lane=None, **kw):
        table = {
            "tt": lambda e: e.tensor_tensor(*args, **kw), "ts": lambda e: e.tensor_scalar(*args, **kw),
            "stt": lambda e: e.scalar_tensor_tensor(*args, **kw), "copy": lambda e: e.tensor_copy(*args),
            "recip": lambda e: e.reciprocal(*args), "max": lambda e: e.reduce_max(*args, AX_X),
            "sum": lambda e: e.reduce_sum(*args, AX_X), "set": lambda e: e.memset(*args),
            "ttr": lambda e: e.tensor_tensor_reduce(*args, **kw),
            "scan": lambda e: e.tensor_tensor_scan(*args, **kw)}
        return (lane or self.dve).do(table[name], after)

    def a(self, out, in_, func, after=(), **kw):
        return self.act.do(lambda e: e.activation(out, in_, func, **kw), after)

    def bring(self, n):
        w, k0, nk, c0, cols, split = self.plan[n]
        stage = self.stages.next()
        counter = self.stage_sems[(self.stages.n - 1) % STAGES]
        raw = stage.ap[:, 0:nk * cols]
        landed = self.dma(self.sp, raw.rearrange("p (k n) -> p k n", k=nk),
                          w[k0:k0 + nk * P, c0:c0 + cols].rearrange("(k p) n -> p k n", p=P),
                          after=stage.free, counter=counter)
        if not split:
            return stage, raw.rearrange("p (k n) -> p k n", k=nk), landed
        slot = self.slots.next()
        high, low = (part[:, 0:nk * cols] for part in slot.ap)
        m = self.a(high, raw, ACT.Copy, after=[landed, slot.free])
        m = self.v("tt", low, raw, high.bitcast(F32), ALU.subtract, after=[m], lane=self.pool if n % 2 else None)
        stage.free = [m]
        return slot, [part.rearrange("p (k n) -> p k n", k=nk) for part in (high, low)], m

    def weights(self, w, k0, nk, c0, cols=P, split=True):
        n = len(self.asked)
        self.asked.append((w, k0, nk, c0, cols, split))
        if self.plan is None:
            stub = Bank(None)
            part = self.high[0][:, 0:nk * cols].rearrange("p (k n) -> p k n", k=nk)
            return stub, [part, part] if split else self.stage[:, 0, 0:nk * cols].rearrange("p (k n) -> p k n", k=nk), ()
        target = n
        if split:
            later = [m for m in range(n + 1, min(n + 4, len(self.plan))) if self.plan[m][5]]
            target = later[0] if later else n
        self.bring_to(target)
        return self.ready_blocks.pop(n)

    def bring_to(self, target):
        while self.brought <= target:
            self.ready_blocks[self.brought] = self.bring(self.brought)
            self.brought += 1

    def bring_two(self):
        n = len(self.asked)
        if self.plan is not None:
            later = [m for m in range(n, min(n + 4, len(self.plan))) if self.plan[m][5]]
            self.bring_to(later[1] if len(later) > 1 else n - 1)

    def pieces(self, sources):
        stage = self.stages.next()
        counter = self.stage_sems[(self.stages.n - 1) % STAGES]
        before = [(counter.sem, counter.count)] if counter.count else []
        views = []
        for at, kp, nk, cols, src in sources:
            view = stage.ap[0:kp, at:at + nk * cols].rearrange("p (k n) -> p k n", k=nk)
            dst = view if len(src.shape) == 3 else view.rearrange("p k (h n) -> p k h n", h=src.shape[2])
            for k in range(nk):
                counter.count += 16
                self.sp.steps.append((marks([stage.free, before]), lambda e, d=dst[:, k], s=src[:, k]: e.dma_start(d, s),
                                      counter.sem, 16))
            views.append(view)
        return stage, views, (counter.sem, counter.count)

    def products(self, out, blocks, x, i0, after, first=True, last=True, cols=slice(None), each=None):
        high, low = blocks
        nk = high.shape[1]
        pairs = []
        for i in range(nk):
            xh, xl = x[0][:, i0 + i, :], x[1][:, i0 + i, :]
            pairs += [(high[:, i, cols], xh), (high[:, i, cols], xl), (low[:, i, cols], xh)]
            if each:
                done = self.mm(out, pairs, [after, each[i]], open_=first and i == 0, close=last and i == nk - 1)
                pairs = []
        return done if each else self.mm(out, pairs, after, open_=first, close=last)

    def split(self, x, high, low, after):
        m = self.a(high, x, ACT.Copy, after=after)
        return self.v("tt", low, x, high.bitcast(F32), ALU.subtract, after=[m])

    def linear(self, w, n_k, c0, width, parts, take, tile=P, background=True, middle=False):
        for at in range(0, width, tile):
            cols = min(tile, width - at)
            held = {}
            for k in range(0, n_k, KT):
                nk = min(KT, n_k - k)
                slot, view, ready = self.weights(w, k * P, nk, c0 + at, cols)
                for n, (x, T, x_ready) in enumerate(parts):
                    if k == 0:
                        held[n] = self.banks.next()
                    bank = held[n]
                    by_tile = at == 0 and len(x_ready) == n_k
                    after = [ready, () if by_tile else x_ready, bank.free if k == 0 else ()]
                    if middle:
                        for lo, hi in ((0, 3), (3, 6), (6, nk)):
                            if lo:
                                self.pump()
                            done = self.products(bank.ap[0:cols, 0:T], [v[:, lo:hi] for v in view], x, k + lo, after,
                                                 first=k + lo == 0, last=k + hi == n_k)
                    else:
                        done = self.products(bank.ap[0:cols, 0:T], view, x, k, after, first=k == 0, last=k + nk == n_k,
                                             each=x_ready[k:k + nk] if by_tile else None)
                    slot.free = [done]
                    if k + nk == n_k:
                        if n == len(parts) - 1:
                            self.pump()
                            if background:
                                self.pump_background()
                        take(n, at // tile, bank.ap[0:cols, 0:T], done, bank)

    def pump(self):
        if self.jobs:
            self.jobs.pop(0)()

    def pump_background(self):
        if self.background:
            self.background.pop(0)()

    def flush(self):
        while self.jobs:
            self.jobs.pop(0)()

    def mean_square_root(self, tiles, T, ones, scale, after, rows=P):
        bank = self.mix.next()
        n = len(tiles)
        for i, x in enumerate(tiles):
            t = self.temps.next()
            sq = t.ap[0:rows, 0:T]
            m = self.a(sq, x, ACT.Square, after=[after, t.free])
            done = self.pe.do(lambda e, i=i, sq=sq: e.matmul(bank.ap[:, 0:T], ones[0:rows, :], sq,
                                                             start=i == 0, stop=i == n - 1),
                              [m, bank.free if i == 0 else ()])
            t.free = [done]
        return self.inverse_root(bank, T, scale, done)

    def square(self, part, k, ready, total=None):
        T = part.T
        if k == 0:
            part.mean = part.own_mean if total is None else total
        total = part.mean[:, 0:T]
        if k == 0:
            part.squares = self.a(total, part.h[:, k, 0:T], ACT.Square, after=[ready, part.mean_free])
            return
        t = self.temps.next()
        sq = t.ap[:, 0:T]
        m = self.a(sq, part.h[:, k, 0:T], ACT.Square, after=[ready, t.free])
        m = self.v("tt", total, total, sq, ALU.add, after=[m, part.squares], lane=self.pool)
        t.free = [m]
        part.squares = m
        if k == KT - 1:
            part.unfinished = True

    def finish_square(self, part):
        if not part.unfinished:
            return
        part.unfinished = False
        bank = self.mix.next()
        total = part.mean[:, 0:part.T]
        done = self.mm(bank.ap[:, 0:part.T], [(self.ones[:], total)], [part.squares, bank.free])
        part.mean_ready = self.v("ts", total, bank.ap[:, 0:part.T], 1.0 / D, EPS, ALU.mult, ALU.add, after=[done])
        bank.free = [part.mean_ready]

    def residual_root(self, part):
        self.finish_square(part)
        if part.mean_ready is None:
            return self.mean_square_root([part.h[:, k, 0:part.T] for k in range(KT)], part.T, self.ones, 1.0 / D,
                                         part.h_ready)
        ready, part.mean_ready = part.mean_ready, None
        t = Bank(part.mean)
        root = part.mean[:, 0:part.T]
        m = self.a(root, root, ACT.Sqrt, after=[ready])
        return root, self.v("recip", root, root, after=[m]), t

    def inverse_root(self, bank, T, scale, done):
        t = self.roots.next()
        root = t.ap[:, 0:T]
        m = self.v("ts", root, bank.ap[:, 0:T], scale, EPS, ALU.mult, ALU.add, after=[done, t.free])
        bank.free = [m]
        m = self.a(root, root, ACT.Sqrt, after=[m])
        m = self.v("recip", root, root, after=[m])
        return root, m, t

    def modulated_norm(self, part, gain, shift, after=()):
        T = part.T
        self.bring_two()
        rinv, ready, t = self.residual_root(part)
        high, low = part.hn
        held, part.hn_ready = [], []
        for k in range(KT + 2):
            if k < KT:
                x = self.temps.next()
                xs = x.ap[:, 0:T]
                m = self.v("tt", xs, part.h[:, k, 0:T], rinv, ALU.mult, after=[ready, part.h_ready, x.free])
                if k % 2:
                    m = self.v("ts", xs, xs, gain[:, k, :], shift[:, k:k + 1], ALU.mult, ALU.add, after=[m, after],
                               lane=self.pool)
                else:
                    m = self.a(xs, xs, ACT.Identity, after=[m, after], scale=gain[:, k, :], bias=shift[:, k:k + 1])
                m = self.a(high[:, k, :], xs, ACT.Copy, after=[m, part.hn_free])
                held.append((x, xs, m))
            if k >= 2:
                x, xs, m = held[k - 2]
                m = self.v("tt", low[:, k - 2, :], xs, high[:, k - 2, :].bitcast(F32), ALU.subtract, after=[m],
                           lane=self.pool if k % 2 else None)
                x.free = [m]
                part.hn_ready.append(m)
        t.free = [m]

    def swiglu(self, parts, hidden, w_a, a0, w_b, b0, w_down, gate, hidden_free, meanwhile=None):
        for first, tiles in GROUPS:
            hid_ready = [[] for _ in parts]
            for f in range(tiles):
                slot_a, wa, ready_a = self.weights(w_a, 0, KT, a0 + (first + f) * P)
                slot_b, wb, ready_b = self.weights(w_b, 0, KT, b0 + (first + f) * P)
                if first + f:
                    self.pump_background()
                numbered = list(enumerate(parts))
                for n, part in numbered if first + f else numbered[::-1]:
                    T = part.T
                    bank_a, bank_b = self.banks.next(), self.banks.next()
                    ps_a, ps_b = bank_a.ap[:, 0:T], bank_b.ap[:, 0:T]
                    ma = self.products(ps_a, wa, part.hn, 0, [ready_a, bank_a.free],
                                       each=part.hn_ready if first + f == 0 else None)
                    mb = self.products(ps_b, wb, part.hn, 0, [ready_b, bank_b.free])
                    t = self.temps.next()
                    s = t.ap[:, 0:T]
                    m = self.a(s, ps_a, ACT.Sigmoid, after=[ma, t.free])
                    m = self.v("tt", s, s, ps_a, ALU.mult, after=[m])
                    bank_a.free = [m]
                    m = self.v("tt", s, s, ps_b, ALU.mult, after=[m, mb])
                    bank_b.free = [m]
                    high, low = hidden[n]
                    m = self.split(s, high[:, f, :], low[:, f, :], [m, hidden_free])
                    t.free = [m]
                    hid_ready[n].append(m)
                slot_a.free = slot_b.free = [mb]
            last = {}
            if meanwhile and first + tiles == FT:
                meanwhile()

            def take(n, f, ps, done, bank):
                part = parts[n]
                m = self.v("stt", part.h[:, f, 0:part.T], ps, gate(part)[:, f:f + 1], part.h[:, f, 0:part.T],
                           ALU.mult, ALU.add, after=[done, part.h_ready])
                bank.free = [m]
                last[n] = m
                if first + tiles == FT:
                    self.square(part, f, [m])

            for f in range(KT):
                slot, view, ready = self.weights(w_down, first * P, tiles, f * P)
                if len(parts) > 1:
                    self.pump_background()
                for n, part in enumerate(parts):
                    bank = self.banks.next()
                    done = self.products(bank.ap[:, 0:part.T], view, hidden[n], 0, [ready, bank.free],
                                         each=hid_ready[n] if f == 0 else None)
                    take(n, f, bank.ap[:, 0:part.T], done, bank)
                slot.free = [done]
            hidden_free = [done]
            for n, part in enumerate(parts):
                part.h_ready = [last[n]]
        for part in parts:
            part.hn_free = [mb]
            self.finish_square(part)

    def modulation(self, w, j, mod, vectors, ready, bias):
        stage, view, landed = self.weights(w, 0, KT, j * P, split=False)
        part = self.partials.next()
        m = [(), ()]
        both = len(vectors) == 2
        for k in range(KT):
            for i, c in enumerate(vectors):
                n = i if both else k % 2
                acc, by = part.ap[:, n, :], self.cond[:, k, c:c + 1]
                if k < (1 if both else 2):
                    m[n] = self.v("ts", acc, view[:, k, :], by, None, ALU.mult, after=[landed, ready, part.free])
                else:
                    m[n] = self.v("stt", acc, view[:, k, :], by, acc, ALU.mult, ALU.add, after=[m[n]])
        stage.free = m

        def finish():
            bank = self.mix.next()

            def emit(e):
                for n in range(2):
                    at = n if both else 0
                    last = e.matmul(bank.ap[:, at:at + 1], part.ap[:, n, :], self.ones[:, 0:1], start=both or n == 0,
                                    stop=both or n == 1)
                return last
            done = self.pe.do(emit, [m, bank.free])
            part.free = [done]
            self.mod_ready = self.v("ts", mod[:, j, :], bank.ap[:, 0:len(vectors)], bias[:, j:j + 1], None, ALU.add,
                                    after=[done])
            bank.free = [self.mod_ready]
        self.finish_modulation()
        self.unfinished = finish

    def have_vectors(self, n):
        while self.n_background - len(self.background) < n:
            self.background.pop(0)()
        self.finish_modulation()

    def finish_modulation(self):
        if self.unfinished:
            self.unfinished()
        self.unfinished = None

    def sigmoid_times(self, out, x, after):
        t = self.temps.next()
        s = t.ap[:, 0:x.shape[1]]
        m = self.a(s, x, ACT.Sigmoid, after=[after, t.free])
        m = self.v("tt", out, x, s, ALU.mult, after=[m])
        t.free = [m]
        return m

    def setup(self):
        i = self.inp
        sp = self.sp
        rows = []
        self.col = {}
        self.at = self.phase_base
        stage = self.area("vectors", 3 * P).rearrange("p (a n) -> p a n", a=3)

        def rows_of(ap):
            return ap.rearrange("(r p) -> r p", p=P)

        clear = self.v("set", stage, 0.0)
        rows.append(clear)

        def put(name, tile, row, ap):
            n = ap.shape[0]
            rows.append(self.dma(sp, stage[row:row + n, tile, 0:ap.shape[1]], ap, after=[clear]))
            self.col[name] = (tile, row)

        put("norm_attn", 0, 0, rows_of(i["norm_attn_g"][0]))
        put("norm_ffn", 0, 8, rows_of(i["norm_ffn_g"][0]))
        put("final", 0, 16, rows_of(i["final_norm_g"]))
        put("b_ada", 0, 24, rows_of(i["b_ada"][0]))
        put("c", 0, 72, rows_of(i["c"][0]))
        put("conv", 0, 80, i["conv_w"][0].rearrange("j (r p) -> (j r) p", p=P))
        for l in range(2):
            t = 1 + l
            put(f"b_ada{l}", t, 0, rows_of(i["b_ada_2"][l]))
            put(f"g_ffn1{l}", t, 72, rows_of(i["g_ffn1_2"][l]))
            put(f"g_mix{l}", t, 80, rows_of(i["g_mix_2"][l]))
            put(f"g_ffn2{l}", t, 88, rows_of(i["g_ffn2_2"][l]))
            put(f"s_pool{l}", t, 96, rows_of(i["s_pool_2"][l]))
            put(f"g_sgu{l}", t, 98, i["g_sgu_2"][l].rearrange("(a b) d -> a (b d)", b=2))
            put(f"g_kv{l}", t, 100, rows_of(i["g_kv_2"][l]))
            put(f"g_q{l}", t, 101, i["g_q_2"][l].rearrange("(r p) -> r p", p=96))
        put("c2", 1, 103, rows_of(i["c_2"][0]))
        put("c_ctx", 1, 111, rows_of(i["c_ctx_2"]))
        put("final2", 1, 119, rows_of(i["g_final_2"]))
        eye = self.dma(sp, self.eye[:], self.const["eye"])
        hones = self.dma(sp, self.head_ones[:], self.const["head_ones"])
        ones = self.v("set", self.ones[:], 1.0)
        self.consts = [eye, hones, ones]
        bank = self.mix.next()
        m = self.transposes([(bank.ap[:, a * P:(a + 1) * P], stage[:, a, :], P) for a in range(3)],
                            [rows, eye, ones])
        m = self.v("copy", self.vec[:].rearrange("p a n -> p (a n)"), bank.ap[:, 0:3 * P], after=[m])
        bank.free = [m]
        self.vec_ready = m
        self.dt_bias, self.a_log = self.small[0:8, 0:1], self.small[0:8, 1:2]
        self.norm_g = self.small[:, 2:3]
        col = lambda ap: ap.rearrange("(n o) -> n o", o=1)
        self.small_ready = [self.dma(sp, self.dt_bias, col(i["dt_bias"][0])),
                            self.dma(sp, self.a_log, col(i["a_log"][0])),
                            self.dma(sp, self.norm_g[0:HD], col(i["delta_norm_g"][0])),
                            self.dma(sp, self.norm_g[HD:P], col(i["delta_norm_g"][0]))]
        for n, name in enumerate(("c", "c2", "c_ctx")):
            m = self.sigmoid_times(self.cond[:, :, n], self.column(name, KT), [self.vec_ready])
        self.cond_ready = m
        self.token_jobs = []
        self.main = Part("main", SEQ, self.h_main, None, 0)
        self.side = Part("ctx", CTX, self.h_ctx, None, 1)
        self.main.own_mean, self.side.own_mean = self.mean_main, self.mean_ctx
        for part, src in ((self.main, i["x"][0]), (self.side, i["ctx_2"][0])):
            nt = part.T // P
            x = self.area("tokens", nt * D).rearrange("p (a n) -> p a n", a=nt)
            landed = self.dma(sp, x, src.rearrange("(a p) n -> p a n", p=P))

            def turn_tile(k, part=part, nt=nt, x=x, landed=landed):
                bank = self.mix.next()
                m = self.transposes([(bank.ap[:, a * P:(a + 1) * P], x[:, a, k * P:(k + 1) * P], P)
                                     for a in range(nt)], [landed, eye, bank.free])
                m = self.a(part.h[:, k, :], bank.ap[:, 0:part.T], ACT.Copy, after=[m])
                bank.free = [m]
                if part is self.main:
                    self.square(part, k, [m])
                    if k == KT - 1:
                        self.finish_square(part)
                part.h_ready = [m]
            self.token_jobs += [lambda k=k, turn_tile=turn_tile: turn_tile(k) for k in range(KT)]

    def column(self, name, n, skip=0):
        tile, row = self.col[name]
        return self.vec[:, tile, row + skip:row + skip + n]

    def gains(self, slot, name, scale, after):
        return self.v("stt", self.gain[:, :, slot], scale, 1.0, self.column(name, KT), ALU.add, ALU.mult, after=after)

    def distance_bias(self):
        table = self.area("table", SKEW)[0:N_BUCKETS + 1]
        relb = self.area("rel_bias", HEADS1)[0:N_BUCKETS + 1]
        wide = self.area("rel_wide", HEADS1 * P)[0:N_BUCKETS + 1].rearrange("p (h n) -> p h n", n=P)
        rows = [self.area("distances", SKEW) for _ in range(2)]
        table_ready = self.dma(self.sp, table, self.const["distance"])
        one = self.v("set", relb, 1.0, lane=self.pool)
        rel = self.dma(self.sp, relb[0:N_BUCKETS], self.inp["rel_bias"], after=[one])
        wide_ready = self.v("copy", wide, relb.rearrange("p (h o) -> p h o", o=1).broadcast_to([N_BUCKETS + 1, HEADS1, P]),
                            after=[one, rel], lane=self.pool)
        free, self.skewed = [(), ()], []
        for h in range(HEADS1):
            r = rows[h % 2]
            for o, n in ((0, 512), (512, SKEW - 512)):
                bank = self.mix.next()
                done = self.mm(bank.ap[:, 0:n], [(wide[:, h, :], table[:, o:o + n])],
                               [wide_ready, table_ready, bank.free])
                m = self.a(r[:, o:o + n], bank.ap[:, 0:n], ACT.Copy, after=[done, free[h % 2]])
                bank.free = [m]
            wrote = self.dma(self.act, self.skew[h, :].rearrange("(p n) -> p n", p=P), r, after=[m])
            self.dram_writes.append(wrote)
            self.skewed.append(wrote)
            free[h % 2] = [wrote]
            yield

    def dilated_attention(self, gates_read, QA, KA, VA, Y, ready):
        E = Turn([Bank(self.area("bias", SEQ)) for _ in range(2)])
        PT = Turn([Bank(self.area("weights_t", 4 * SEQ).rearrange("p (a q) -> p a q", a=4)) for _ in range(2)])
        for e in E.banks:
            e.free = gates_read
        mx, sm = self.small[:, 32:64], self.small[:, 64:96]
        state = {"late": []}

        def scores(h, qt):
            k, po, n, c = h // 2, HD * (h % 2), (qt + 1) * P, 4 * h + qt
            if qt == 0:
                e = E.next()
                src = bass.AP(self.skew.tensor, h * P * SKEW + 127, [[SKEW - 1, P], [1, SEQ]])
                state["bias"] = (e, self.dma(self.sp, e.ap, src, after=[self.skewed[h], e.free]))
                state["pt"] = PT.next()
            e, e_ready = state["bias"]
            bank, s = self.mix.next(), self.temps.next()
            sc = s.ap[:, 0:n]
            done = self.mm(bank.ap[:, 0:n], [(QA[po:po + HD, k, qt * P:(qt + 1) * P], KA[po:po + HD, k, 0:n])],
                           [ready(), bank.free])
            m = self.v("ttr", sc, bank.ap[:, 0:n], e.ap[:, (3 - qt) * P:SEQ], 1.0, -3e38, ALU.add, ALU.max,
                       mx[:, c:c + 1], after=[done, s.free, e_ready])
            bank.free = e.free = [m]
            m = self.v("ts", mx[:, c:c + 1], mx[:, c:c + 1], -1.0, None, ALU.mult, after=[m])
            m = self.a(sc, sc, ACT.Exp, after=[m], bias=mx[:, c:c + 1], accum_out=sm[:, c:c + 1])
            return [h, qt, s, sc, m, state["pt"]]

        def normalise(item):
            h, qt, s, sc, m, pt = item
            c = 4 * h + qt
            m = self.v("recip", sm[:, c:c + 1], sm[:, c:c + 1], after=[m])
            item[4] = self.a(sc, sc, ACT.Copy, after=[m], scale=sm[:, c:c + 1])

        def values(late):
            h, qt, s, sc, m, pt = late
            k, po, n = h // 2, HD * (h % 2), (qt + 1) * P
            bank = self.mix.next()
            done = self.transposes([(bank.ap[:, a * P:(a + 1) * P], sc[:, a * P:(a + 1) * P], P)
                                    for a in range(qt + 1)], [m, bank.free])
            s.free = [done]
            m = self.a(pt.ap[:, 0:qt + 1, qt * P:(qt + 1) * P], bank.ap[:, 0:n].rearrange("p (a q) -> p a q", q=P),
                       ACT.Copy, after=[done, pt.free])
            bank.free = [m]
            if qt < 3:
                return
            bank = self.mix.next()

            def emit(e):
                for a in range(4):
                    last = e.matmul(bank.ap[po:po + HD, a * P:SEQ], VA[:, a, h * HD:(h + 1) * HD],
                                    pt.ap[:, a, a * P:SEQ], start=a == 0, stop=a == 3)
                return last
            done = self.pe.do(emit, [m, bank.free])
            pt.free = [done]
            m = self.a(Y[po:po + HD, k, :], bank.ap[po:po + HD, :], ACT.Copy, after=[done])
            bank.free = [m]
            self.attention_done = m

        def job(h, qt):
            if len(state["late"]) == 2 or h > HEADS1:
                values(state["late"].pop(0))
            if state["late"]:
                normalise(state["late"][-1])
            if h < HEADS1:
                state["late"].append(scores(h, qt))
        steps = [(h, qt) for h in range(HEADS1) for qt in range(4)] + [(HEADS1, 0), (HEADS1 + 1, 0)]
        return [lambda h=h, qt=qt: job(h, qt) for h, qt in steps]

    def head_norm(self, tiles, n, scale, eps, after, sum_rows, spread_rows, rows, finish):
        bank = self.mix.next()
        for f, x in enumerate(tiles):
            t = self.temps.next()
            m = self.a(t.ap, x, ACT.Square, after=[after, t.free])
            done = self.pe.do(lambda e, f=f, sq=t.ap: e.matmul(bank.ap[0:16, :], sum_rows[:, f, :], sq, start=f == 0,
                                                               stop=f == n - 1), [m, bank.free if f == 0 else ()])
            t.free = [done]
        m = self.v("ts", rows, bank.ap[0:16, :], scale, eps, ALU.mult, ALU.add, after=[done])
        bank.free = [m]
        m = self.a(rows, rows, ACT.Sqrt, after=[m])
        m = self.v("recip", rows, rows, after=[m])
        for f in range(n):
            bank = self.mix.next()
            done = self.mm(bank.ap, [(spread_rows[0:16, f, :], rows)], [m, bank.free])
            last = finish(f, bank.ap, done)
            bank.free = [last]
        return last

    def first_block(self):
        i, main, mod = self.inp, self.main, self.mod1
        self.at = self.phase_base + 4 * (3 * P + 6 * D)
        bias = self.column("b_ada", N_MOD1 * KT)
        for j in range(N_MOD1 * KT):
            self.modulation(i["w_ada"][0], j, mod, (0,), [self.cond_ready], bias)
            self.token_jobs[j]()
            if j == KT:
                distances = self.distance_bias()
            if j >= KT:
                next(distances)
            if j == 2 * KT - 1:
                self.finish_modulation()
                first_two = self.mod_ready
                break
        self.background = [lambda j=j: self.modulation(i["w_ada"][0], j, mod, (0,), [self.cond_ready], bias)
                           for j in range(2 * KT, N_MOD1 * KT)] + self.modulation_jobs(0) + self.modulation_jobs(1)
        self.n_background = len(self.background)
        vec = lambda j: mod[:, j * KT:(j + 1) * KT, 0]
        before = self.everything()
        self.at = self.phase_base
        YA = self.area("attention_out", 4 * SEQ).rearrange("p (k t) -> p k t", k=4)
        ZS = self.area("silu_z", 4 * SEQ).rearrange("p (k t) -> p k t", k=4)
        PAD = SEQ + 3
        DX = self.area("delta_qkv", 12 * PAD).rearrange("p (k t) -> p k t", k=12)
        G, EG, BT = (self.area("gate_rows", SEQ)[0:8] for _ in range(3))
        delta_base = self.at
        main.hn = self.halves("hn", KT, SEQ)
        QA, KA, VA = (self.area("qkv", 4 * SEQ).rearrange("p (k t) -> p k t", k=4) for _ in range(3))
        gate_work = self.at
        X1, BE, AT = (self.area("gate_work", SEQ)[0:8] for _ in range(3))
        g = self.gains(0, "norm_attn", vec(1), [first_two])
        main.hn_free = before
        self.modulated_norm(main, self.gain[:, :, 0:1], vec(0), [g, first_two])
        pads = self.v("set", DX[:, :, 0:3], 0.0, after=before)
        w = i["w_in"][0]
        got = {}
        part = [(main.hn, SEQ, main.hn_ready)]

        for n, dst in ((0, BT), (1, AT)):
            def take_gate(_, f, ps, done, bank, n=n, dst=dst):
                if n == 0:
                    m = self.a(dst, ps, ACT.Sigmoid, after=[done, before])
                else:
                    m = self.a(dst, ps, ACT.Identity, after=[done, before, self.small_ready], bias=self.dt_bias)
                bank.free = [m]
                got[n] = m
            self.linear(w, KT, 3584 + 8 * n, 8, part, take_gate)
        RS = BE
        reset = self.v("set", RS, 1.0, after=before)
        reset = self.v("set", RS.rearrange("p (n c) -> p n c", c=CHUNK)[:, :, 0:1], 0.0, after=[reset])
        m = self.a(X1, AT, ACT.Abs, after=[got[1]])
        m = self.a(X1, X1, ACT.Exp, after=[m], scale=-1.0)
        m = self.a(X1, X1, ACT.Ln, after=[m], bias=1.0)
        m = self.v("stt", X1, AT, 0.0, X1, ALU.max, ALU.add, after=[m])
        ea = self.a(self.a_log, self.a_log, ACT.Exp, after=[self.small_ready])
        m = self.v("ts", X1, X1, self.a_log, -1.0, ALU.mult, ALU.mult, after=[m, ea])
        m = self.v("scan", G, RS, X1, 0.0, ALU.mult, ALU.add, after=[m, reset])
        g_ready = m
        eg_ready = self.a(EG, G, ACT.Exp, after=[m])
        g3, x3 = (t.rearrange("p (n c) -> p n c", c=CHUNK) for t in (G, X1))
        m = self.v("tt", x3, g3[:, :, CHUNK - 1:CHUNK].broadcast_to([8, 8, CHUNK]), g3, ALU.subtract, after=[m])
        kd_ready = self.a(X1, X1, ACT.Exp, after=[m])
        be_ready = self.v("tt", BE, BT, EG, ALU.mult, after=[eg_ready, got[0]])
        bank = self.mix.next()
        kinds = (G, BT, BE, X1)
        done = self.transposes([(bank.ap[:, (a * 4 + n) * 8:(a * 4 + n + 1) * 8], r[:, a * P:(a + 1) * P], 8)
                                for a in range(4) for n, r in enumerate(kinds)],
                               [g_ready, kd_ready, be_ready, bank.free])
        TM = self.token_gates[:, :].rearrange("p (a k h) -> p a k h", a=4, k=4)
        tm_ready = self.v("copy", self.token_gates[:, :], bank.ap[:, 0:128], after=[done])
        bank.free = [tm_ready]

        def take_qk(n, f, ps, done, bank):
            dst, scale = (QA[:, f, :], HD ** -0.5) if f < 4 else (KA[:, f - 4, :], 1.0)
            m = self.a(dst, ps, ACT.Copy, after=[done, before], scale=scale)
            bank.free = got["qk"] = [m]

        self.linear(w, KT, 0, 1024, part, take_qk)

        def take_v(n, f, ps, done, bank):
            t = self.temps.next()
            m = self.a(t.ap, ps, ACT.Copy, after=[done, t.free])
            bank.free = [m]

            def turn():
                turned = self.mix.next()
                done = self.transposes([(turned.ap[:, a * P:(a + 1) * P], t.ap[:, a * P:(a + 1) * P], P) for a in range(4)],
                                       [m, turned.free])
                t.free = [done]
                turned.free = got["v"] = [self.a(VA[:, :, f * P:(f + 1) * P], turned.ap.rearrange("p (a n) -> p a n", a=4),
                                                 ACT.Copy, after=[done, before])]
            self.jobs.append(turn)

        self.linear(w, KT, 1024, 512, part, take_v)
        self.flush()
        self.at = gate_work
        self.jobs = self.dilated_attention(tm_ready, QA, KA, VA, YA, lambda: [got["qk"], got["v"]])
        cw = lambda j, f: self.column("conv", 1, skip=12 * j + f)
        conv_done, silus = [], []

        def take_conv(f0):
            def take(n, f, ps, done, bank):
                f += f0
                x, y, acc = DX[:, f, 3:PAD], DX[:, f, 0:SEQ], self.temps.next()
                m = self.a(x, ps, ACT.Copy, after=[done, pads])
                bank.free = [m]
                m = self.a(acc.ap, y, ACT.Copy, after=[m, acc.free], scale=cw(0, f))
                for j in range(1, 4):
                    m = self.v("stt", acc.ap, DX[:, f, j:j + SEQ], cw(j, f), acc.ap, ALU.mult, ALU.add, after=[m])
                m = self.v("copy", y, acc.ap, after=[m], lane=self.pool)
                acc.free = [m]

                def silu():
                    t = self.temps.next()
                    s = self.a(t.ap, y, ACT.Sigmoid, after=[m, t.free])
                    t.free = [self.v("tt", y, y, t.ap, ALU.mult, after=[s], lane=self.pool)]
                    conv_done.append(t.free[0])
                silus.append(silu)
            return take
        DD = DX[:, :, 0:SEQ]
        for f0, c0 in ((4, 1536 + 512), (0, 1536), (8, 1536 + 1024)):
            self.linear(w, KT, c0, 512, part, take_conv(f0), middle=True)
        self.flush()
        self.jobs = silus

        def take_z(n, f, ps, done, bank):
            m = self.a(ZS[:, f, :], ps, ACT.Sigmoid, after=[done, before])
            m = self.v("tt", ZS[:, f, :], ZS[:, f, :], ps, ALU.mult, after=[m])
            bank.free = got["z"] = [m]
        self.linear(w, KT, 3072, 512, part, take_z, background=False, middle=True)
        self.flush()

        before = self.everything()
        self.at = delta_base
        masks = self.area("masks", 8 * P).rearrange("p (m n) -> p m n", m=8)
        pick_head = self.area("pick_head", 8 * P)[0:8].rearrange("p (m n) -> p m n", m=8)
        spread = self.area("spread", 8 * P)[0:16].rearrange("p (m n) -> p m n", m=8)
        sum_rows, sum_rows_ready = self.small_const("sum_rows", self.const["sum_rows"].rearrange("p m n -> p (m n)"))
        sum_rows = sum_rows.rearrange("p (m n) -> p m n", m=8)
        norm_rows = self.root[0:16]
        consts = [self.dma(self.sp, o, c, after=before) for o, c in (
            (masks, self.const["masks"]), (spread, self.const["spread_rows"]),
            (pick_head, self.const["pick_head"]))] + [sum_rows_ready]
        pick_pair = spread[0:8, 0:4, :]
        after_norms = self.at

        def unit(f, ps, done):
            return self.v("stt", DD[:, f, :], DD[:, f, :], HD ** -0.5 if f < 4 else 1.0, ps, ALU.mult, ALU.mult, after=[done])
        unit_done = self.head_norm([DD[:, f, :] for f in range(8)], 8, 1.0, EPS, [conv_done, consts], sum_rows, spread,
                                   norm_rows, unit)
        QKT = self.area("qk", 8 * SEQ).rearrange("p (h t) -> p h t", h=8)
        KD = self.area("k_decayed", 4 * SEQ).rearrange("p (a n) -> p a n", a=4)
        EGL = self.small[:, 112:144].rearrange("p (k n) -> p k n", k=4)
        two = lambda name, n: self.area(name, n)
        works = [dict(B=two("B", 1024), U=two("U", 1024), T=two("T", 1024), W=two("W", 1024), VB=two("vb", SEQ),
                      KBE=two("kbe", SEQ), free=[before]) for _ in range(2)]
        turns = [self.mix, self.banks]
        eye8 = self.eye[:].rearrange("p (o n) -> p o n", o=1).broadcast_to([P, 8, P])

        def within_chunks(pair, work, turn):
            B_, U_, T_, W_ = (work[n].rearrange("p (o t) -> p o t", o=2) for n in "BUTW")
            VB, KBE = (work[n].rearrange("p (a o n) -> p a o n", a=4, o=2) for n in ("VB", "KBE"))
            flat8 = lambda x: x.rearrange("p o (a c) -> p (o a) c", c=P)
            four = lambda x: x.rearrange("p (a c) -> p a c", a=4)
            free = [work["free"]]
            bank = turn.next()
            done = self.mm(bank.ap, [(pick_pair[:, pair, :], BT)], [got[0], consts, bank.free])
            t = self.temps.next()
            kb = self.v("tt", t.ap, DD[:, 4 + pair, :], bank.ap, ALU.mult, after=[done, unit_done, t.free])
            bank.free = [kb]
            ready = []
            for o in range(2):
                h, po = 2 * pair + o, HD * o
                bank = turn.next()
                done = self.mm(bank.ap, [(pick_head[:, h, :], G)], [g_ready, consts, bank.free])
                dec = W_[:, o, :]
                for a in range(4):
                    m = self.v("ts", dec[:, a * P:(a + 1) * P], bank.ap[:, a * P:(a + 1) * P],
                               TM[:, a, 0, h:h + 1], 0.0, ALU.subtract, ALU.min, after=[done, tm_ready, free])
                bank.free = [m]
                m = self.a(dec, dec, ACT.Exp, after=[m])
                for dst, rhs, mask in ((B_[:, o, :], t.ap, 0), (QKT[:, h, :], DD[:, pair, :], 1)):
                    bank = turn.next()

                    def emit(e, bank=bank, rhs=rhs, po=po):
                        for a in range(4):
                            c = slice(a * P, (a + 1) * P)
                            last = e.matmul(bank.ap[:, c], DD[po:po + HD, 4 + pair, c], rhs[po:po + HD, c], start=True, stop=True)
                        return last
                    done = self.pe.do(emit, [kb, unit_done, bank.free])
                    t_used = done
                    d = self.v("tt", dst, bank.ap, dec, ALU.mult, after=[done, m, free])
                    bank.free = [d]
                    d = self.v("tt", four(dst), four(dst), masks[:, mask:mask + 1, :].broadcast_to([P, 4, P]), ALU.mult,
                               after=[d], lane=self.pool)
                    ready.append(d)
                yield
            t.free = [t_used]
            for tile, outs in ((4 + pair, ((KBE, 2), (KD[:, :, 2 * pair * HD:2 * (pair + 1) * HD]
                                                      .rearrange("p a (o n) -> p a o n", o=2), 3))), (8 + pair, ((VB, 1),))):
                bank = turn.next()
                done = self.transposes([(bank.ap[:, a * P:(a + 1) * P], DD[:, tile, a * P:(a + 1) * P], P) for a in range(4)],
                                       [unit_done, conv_done, bank.free])
                src = bank.ap.rearrange("p (a o n) -> p a o n", a=4, o=2)
                for dst, kind in outs:
                    m = self.v("tt", dst, src, TM[:, :, kind, 2 * pair:2 * pair + 2]
                               .rearrange("p a (o n) -> p a o n", n=1).broadcast_to([P, 4, 2, HD]), ALU.mult,
                               after=[done, tm_ready, free])
                bank.free = [m]
            tok_ready = m
            yield
            first = self.v("tt", flat8(W_), flat8(B_), self.mask_below.rearrange("p (o n) -> p o n", o=1)
                           .broadcast_to([P, 8, P]), ALU.mult, after=[ready, self.below_ready])
            mu = self.v("tt", flat8(U_), eye8, flat8(W_), ALU.subtract, after=[first, free])
            prev = [mu]
            for o in range(2):
                bank = turn.next()
                done = self.transposes([(bank.ap[:, a * P:(a + 1) * P], U_[:, o, a * P:(a + 1) * P], P) for a in range(4)],
                                       [mu, bank.free])
                m = self.a(T_[:, o, :], bank.ap, ACT.Copy, after=[done, free])
                bank.free = [m]
                prev.append(m)
            yield

            def product(lhs, rhs, after):
                out = []
                for o in range(2):
                    bank = turn.next()

                    def emit(e, bank=bank, o=o):
                        for a in range(4):
                            c = slice(a * P, (a + 1) * P)
                            last = e.matmul(bank.ap[:, c], lhs[:, o, c], rhs[:, o, c], start=True, stop=True)
                        return last
                    out.append((bank, self.pe.do(emit, [after, bank.free])))
                return out

            for level in range(1, 6):
                now = []
                for o, (bank, done) in enumerate(product(B_, T_, prev)):
                    m = self.v("tt", four(W_[:, o, :]), four(bank.ap), masks[:, 2 + level:3 + level, :]
                               .broadcast_to([P, 4, P]), ALU.mult, after=[done, prev])
                    bank.free = [m]
                    now.append(m)
                yield
                u_new = product(W_, U_, now)
                t_new = product(U_, W_, now) if level < 5 else []
                prev = []
                for o, (bank, done) in enumerate(u_new):
                    m = self.v("tt", U_[:, o, :], U_[:, o, :], bank.ap, ALU.subtract,
                               after=[done, t_new[-1][1] if t_new else u_new[-1][1]])
                    bank.free = [m]
                    prev.append(m)
                for o, (bank, done) in enumerate(t_new):
                    m = self.v("tt", T_[:, o, :], T_[:, o, :], bank.ap, ALU.subtract, after=[done])
                    bank.free = [m]
                    prev.append(m)
                yield
            bank = turn.next()

            def emit(e, bank=bank):
                for a in range(4):
                    for o in range(2):
                        last = e.matmul(bank.ap[:, (a * 2 + o) * HD:(a * 2 + o + 1) * HD], U_[:, o, a * P:(a + 1) * P],
                                        VB[:, a, o, :], start=True, stop=True)
                return last
            done = self.pe.do(emit, [prev, tok_ready, bank.free])
            m1 = self.a(DD[:, 8 + pair, :], bank.ap, ACT.Copy, after=[done])
            bank.free = [m1]
            bank = turn.next()

            def emit(e, bank=bank):
                for a in range(4):
                    for o in range(2):
                        last = e.matmul(bank.ap[HD * o:HD * (o + 1), a * P:(a + 1) * P], KBE[:, a, o, :],
                                        U_[:, o, a * P:(a + 1) * P], start=True, stop=True)
                return last
            done_w = self.pe.do(emit, [bank.free])
            m2 = self.a(DD[:, 4 + pair, :], bank.ap, ACT.Copy, after=[done_w])
            bank.free = [m2]
            bank = turn.next()
            done = self.mm(bank.ap, [(pick_pair[:, pair, :], EG)], [eg_ready, bank.free])
            m3 = self.v("tt", DD[:, pair, :], DD[:, pair, :], bank.ap, ALU.mult, after=[done, t_used])
            m4 = self.v("copy", EGL[:, pair, :], bank.ap.rearrange("p (n c) -> p n c", c=CHUNK)[:, :, CHUNK - 1], after=[done])
            bank.free = [m4]
            work["free"] = [done_w, ready, m4]
            work["done"] = [work.get("done", ()), m1, m2, m3, m4, ready]

        self.mask_below = self.mean_ctx[:, 0:P]
        bank = self.mix.next()
        done = self.transposes([(bank.ap[:, 0:P], masks[:, 2, :], P)], [consts, bank.free])
        self.below_ready = self.v("copy", self.mask_below, bank.ap[:, 0:P], after=[done])
        bank.free = [self.below_ready]
        runs = [self.chain(within_chunks(n, works[n], turns[n]), within_chunks(n + 2, works[n], turns[n])) for n in range(2)]
        next(runs[1], None)
        while runs:
            runs = [r for r in runs if next(r, "end") != "end"]
        solved = [works[0]["done"], works[1]["done"]]
        self.at = after_norms
        Y = self.halves("mixed", KT, SEQ)
        YD = self.area("delta_out", 4 * SEQ).rearrange("p (k t) -> p k t", k=4)
        idle = self.everything()
        S = self.tmp[:, 0, 0:256].rearrange("p (k n) -> p k n", k=4)
        SG = self.tmp[:, 0, 256:512].rearrange("p (k n) -> p k n", k=4)
        VN = self.tmp[:, 1, :].rearrange("p (o k n) -> p o k n", o=2, k=4)
        s_ready = self.v("set", self.tmp[:, 0, :], 0.0, after=idle)
        vn_free = idle
        heads = [(h, h // 2, HD * (h % 2)) for h in range(8)]
        pairs_of_banks = [(self.banks.banks[0], self.banks.banks[1]), (self.banks.banks[2], self.banks.banks[3])]
        quarter = lambda ap: ap.rearrange("p (k n) -> p k n", k=4)
        for n in range(SEQ // CHUNK):
            a, p0 = n // 2, CHUNK * (n % 2)
            c = slice(n * CHUNK, (n + 1) * CHUNK)
            bank_v = [self.mix.next(), self.mix.next()]
            bank_o, bank_s = pairs_of_banks[n % 2]

            def emit(e, bank=bank_v, p0=p0, c=c):
                for h, k, po in heads:
                    last = e.matmul(bank[h % 2].ap[p0:p0 + CHUNK, k * HD:(k + 1) * HD], DD[po:po + HD, 4 + k, c],
                                    S[po:po + HD, k, :], start=True, stop=True)
                return last
            done_v = self.pe.do(emit, [s_ready, bank_v[0].free, bank_v[1].free, solved])

            def emit(e, bank=bank_o, c=c):
                for h, k, po in heads:
                    last = e.matmul(bank.ap[po:po + HD, k * HD:(k + 1) * HD], S[po:po + HD, k, :], DD[po:po + HD, k, c],
                                    start=k == 0, stop=False, skip_group_check=True)
                return last
            done_q = self.pe.do(emit, [bank_o.free])
            vn = []
            for o in range(2):
                u = DD[p0:p0 + CHUNK, 8:12, (2 * a + o) * HD:(2 * a + o + 1) * HD]
                vn.append(self.v("tt", VN[p0:p0 + CHUNK, o], u, quarter(bank_v[o].ap[p0:p0 + CHUNK, 0:256]), ALU.subtract,
                                 after=[done_v, vn_free]))
                bank_v[o].free = [vn[-1]]
            sg = self.v("tt", SG, S, EGL[:, :, n:n + 1].broadcast_to([P, 4, HD]), ALU.mult, after=[s_ready, solved],
                        lane=self.pool)

            def emit(e, bank=bank_s, p0=p0, a=a):
                for h, k, po in heads:
                    last = e.matmul(bank.ap[po:po + HD, k * HD:(k + 1) * HD], KD[p0:p0 + CHUNK, a, h * HD:(h + 1) * HD],
                                    VN[p0:p0 + CHUNK, h % 2, k, :], start=True, stop=True)
                return last
            done_s = self.pe.do(emit, [vn, bank_s.free])

            def emit(e, bank=bank_o, p0=p0, n=n):
                for h, k, po in heads:
                    last = e.matmul(bank.ap[po:po + HD, k * HD:(k + 1) * HD], VN[p0:p0 + CHUNK, h % 2, k, :],
                                    QKT[p0:p0 + CHUNK, h, n * CHUNK:(n + 1) * CHUNK], start=False, stop=True,
                                    skip_group_check=True)
                return last
            done_o = self.pe.do(emit, [done_q])
            s_ready = self.v("tt", S, SG, quarter(bank_s.ap[:, 0:256]), ALU.add, after=[done_s, done_q, sg])
            bank_s.free = [s_ready]
            m = self.a(YD[:, :, c], quarter(bank_o.ap[:, 0:256]), ACT.Copy, after=[done_o, before])
            bank_o.free = [m]
            vn_free = [done_o]
        idle = self.everything()
        self.temps.banks[0].free = self.temps.banks[1].free = idle
        parts_ready = [self.split(YA[:, k, :], Y[0][:, k, :], Y[1][:, k, :], [self.attention_done, idle]) for k in range(4)]

        def gated(f, ps, done):
            m = self.v("tt", ZS[:, f, :], ZS[:, f, :], ps, ALU.mult, after=[done, got["z"]])
            m = self.v("stt", YD[:, f, :], YD[:, f, :], self.norm_g, ZS[:, f, :], ALU.mult, ALU.mult, after=[m, self.small_ready])
            parts_ready.append(self.split(YD[:, f, :], Y[0][:, 4 + f, :], Y[1][:, 4 + f, :], [m, idle]))
            return parts_ready[-1]
        self.head_norm([YD[:, f, :] for f in range(4)], 4, 1.0 / HD, EPS, [m], sum_rows, spread, norm_rows, gated)
        self.have_vectors(KT)
        m_g1 = self.mod_ready
        main_h = [()]

        def take_out(n, f, ps, done, bank):
            m = self.v("stt", main.h[:, f, :], ps, vec(2)[:, f:f + 1], main.h[:, f, :], ALU.mult, ALU.add, after=[done, m_g1])
            bank.free = main_h[0] = [m]
            self.square(main, f, [m])
        self.linear(i["w_out"][0], KT, 0, D, [(Y, SEQ, parts_ready)], take_out)
        self.have_vectors(3 * KT)
        main.h_ready = main_h[0]

        self.feed_forward_map()
        g = self.gains(0, "norm_ffn", vec(4), [self.mod_ready])
        self.modulated_norm(main, self.gain[:, :, 0:1], vec(3), [g])
        self.swiglu([main], [self.hidden["main"]], i["w_gate"][0], 0, i["w_up"][0], 0, i["w_down"][0], lambda part: vec(5),
                    self.hidden_free, meanwhile=lambda: self.norm_for_half_step(self.side, 0, "g_ffn1", 0))
        self.have_vectors(4 * KT)
        self.plain_norm(main, "final", True)

    def chain(self, *generators):
        for g in generators:
            yield from g

    def modulation_jobs(self, layer):
        bias = self.column(f"b_ada{layer}", N_MOD2 * KT)
        return [lambda j=j: self.modulation(self.inp["w_ada_2"][layer], j, self.mod2[layer], (1, 2), [self.cond_ready], bias)
                for j in range(N_MOD2 * KT)]

    def plain_norm(self, part, name, again):
        T = part.T
        rinv, ready, t = self.residual_root(part)
        for k in range(KT):
            m = self.v("stt", part.h[:, k, 0:T], part.h[:, k, 0:T], self.column(name, 1, skip=k), rinv, ALU.mult, ALU.mult,
                       after=[ready])
            if again:
                self.square(part, k, [m], total=self.root)
        t.free = [m]
        part.h_ready = [m]

    def feed_forward_map(self):
        before = self.everything()
        self.at = self.phase_base
        self.hidden = {}
        for part in (self.side, self.main):
            part.hn = self.halves("hn", KT, part.T)
            part.hn_free = before
            self.hidden[part.name] = self.halves("hidden", GROUPS[0][1], part.T)
        self.hidden_free = before

    def norm_for_half_step(self, part, layer, names, first):
        mod = self.mod2[layer]
        rows = lambda j, c: mod[:, j * KT:(j + 1) * KT, c]
        self.have_vectors((4 + N_MOD2 * layer + first + 2) * KT)
        g = self.gains(part.col, f"{names}{layer}", rows(first + 1, part.col), [self.mod_ready])
        self.modulated_norm(part, self.gain[:, :, part.col:part.col + 1], rows(first, part.col), [g])

    def half_step(self, parts, layer, names, first):
        half = {}

        def half_gate(part):
            if part.name not in half:
                self.have_vectors((4 + N_MOD2 * layer + first + 3) * KT)
                half[part.name] = self.small[:, 96 + part.col * KT:96 + (part.col + 1) * KT]
                gate = self.mod2[layer][:, (first + 2) * KT:(first + 3) * KT, part.col]
                m = self.v("ts", half[part.name], gate, 0.5, None, ALU.mult, after=[self.mod_ready])
                part.h_ready = [part.h_ready, m]
            return half[part.name]
        w13, w2 = self.inp[f"w13_{names[2:]}_2"][layer], self.inp[f"w2_{names[2:]}_2"][layer]
        self.swiglu(parts, [self.hidden[part.name] for part in parts], w13, 0, w13, D_FF, w2,
                    half_gate, self.hidden_free)

    def gelu(self, x, ready):
        t = self.temps.next()
        u = t.ap[:, 0:x.shape[1]]
        c = 2 * math.sqrt(2 / math.pi)
        m = self.v("tt", u, x, x, ALU.mult, after=[ready, t.free], lane=self.pool)
        m = self.v("ts", u, u, 0.044715 * c, c, ALU.mult, ALU.add, after=[m])
        m = self.v("tt", u, u, x, ALU.mult, after=[m], lane=self.pool)
        m = self.a(u, u, ACT.Sigmoid, after=[m])
        m = self.v("tt", x, x, u, ALU.mult, after=[m])
        t.free = [m]
        return m

    def mixers(self, part, layer, kv_only):
        i, T, name = self.inp, part.T, part.name
        nt = T // P
        w_in = i["w_in_2"][layer]
        self.have_vectors((4 + N_MOD2 * layer + 6) * KT)
        mod = self.mod2[layer]
        rows = lambda j: mod[:, j * KT:(j + 1) * KT, part.col]
        base = self.everything()
        keys = SEQ + CTX
        own = 0 if name == "main" else SEQ
        tiled = lambda name, k, n: self.area(name, k * n).rearrange("p (k n) -> p k n", k=k)
        self.at = self.phase_base
        if part is self.side:
            self.kv = tiled("keys", HEADS2, keys), tiled("values", keys // P, GW)
            self.kv_end = self.at
        KH, VT = self.kv
        self.at = self.kv_end
        CKV = self.area("kv_rank", T)
        after_kv = self.at
        if kv_only:
            part.hn = self.halves("hn", KT, T)
        else:
            CQ = tiled("q_rank", 2, T)[0:96]
            QH = tiled("queries", HEADS2, T)
            self.at -= 4 * HEADS2 * T
            F_, V_ = tiled("fourier", 2, T), tiled("sgu_v", nt, GW)
            U_, PZ = tiled("sgu_u", 2, T), tiled("pool", 2, T + 16)
            head_dft, turn = self.area("head_dft", P), self.area("turn", P)
            inv = tiled("inverse", 2, T)
            wf, wp = tiled("w_fnet", 2, HD), tiled("w_pool", 2, HD)
            WST, BB = tiled("w_sgu", HEADS2, P), tiled("b_sgu", 2, P)
            rope = tiled("rope", 2, SEQ)
            dft_area, pt_area = self.area("token_dft", 8 * SEQ), self.area("weights_t", max(6 * T, (nt + 1) * 512))
            score_area = self.area("scores", 2 * keys)
            dft = dft_area[:, 0:2 * nt * T].rearrange("p (c a t) -> p c a t", c=2, a=nt)
            self.at -= 4 * 2 * keys
            sums = [self.area("sums", T + 16) for _ in range(2)]
            R_ = tiled("head_products", 2, P)
            self.at += 4 * (2 * keys - 2 * (T + 16) - 2 * P)
            scores = Turn([Bank(score_area[:, n * keys:(n + 1) * keys]) for n in range(2)])
            PT = Turn([Bank(a[:, 0:6 * T].rearrange("p (a t) -> p a t", a=6)) for a in (pt_area, dft_area)])
            raw_ws = pt_area[:, nt * 512:nt * 512 + HEADS2 * P].rearrange("p (h n) -> p h n", h=HEADS2)
            YT = pt_area[:, 0:nt * 512].rearrange("p (a n) -> p a n", a=nt)
            hn_at = mixed_at = self.at
            part.hn = self.halves("hn", KT, T)
            self.at = hn_at
            YS = self.halves("mixed", KT, T)
        g = self.gains(part.col, f"g_mix{layer}", rows(4), [self.mod_ready])
        part.hn_free = base
        self.modulated_norm(part, self.gain[:, :, part.col:part.col + 1], rows(3), [g])
        sp = self.sp

        def section(c0, width, tile, put):
            self.linear(w_in, KT, c0, width, [(part.hn, T, part.hn_ready)], put, tile=tile, background=False)

        def mixed(k, x, after, rows_=slice(None)):
            return self.split(x, YS[0][rows_, k, :], YS[1][rows_, k, :], [after, hn_read])

        got = {}

        def copy_to(dst, key):
            def put(n, f, ps, done, bank):
                m = self.a(dst(f), ps, ACT.Copy, after=[done, base])
                bank.free = [m]
                got[key] = m
            return put

        def rank_norm(tiles, rows_, gain, ready):
            rinv, m, t = self.mean_square_root(tiles, T, self.ones, 1.0 / (rows_ * len(tiles)), [ready], rows=rows_)
            for f, x in enumerate(tiles):
                last = self.v("stt", x, x, self.column(gain, 1, skip=f)[0:rows_], rinv[0:rows_], ALU.mult, ALU.mult, after=[m])
            t.free = [last]
            return last

        section(448, KV_RANK, P, copy_to(lambda f: CKV, "ckv"))
        repeat = self.small_const("repeat", self.const["repeat"])

        def put_kr(n, f, ps, done, bank):
            t = self.temps.next()
            m = self.a(t.ap[0:ROPE, 0:T], ps, ACT.Copy, after=[done, t.free])
            bank.free = [m]
            wide = self.mix.next()
            done = self.mm(wide.ap[:, 0:T], [(repeat[0][0:ROPE], t.ap[0:ROPE, 0:T])], [m, repeat[1], wide.free])
            t.free = [done]
            t = self.temps.next()
            x = t.ap[HD:HD + ROPE, 0:T]
            m = self.a(x, wide.ap[HD:HD + ROPE, 0:T], ACT.Copy, after=[done, t.free])
            wide.free = [m]
            got["kr"] = t, x, m
        section(576, ROPE, ROPE, put_kr)
        kv_ready = rank_norm([CKV], P, f"g_kv{layer}", got["ckv"])
        if not kv_only:
            loads = [self.dma(sp, o, c, after=base) for o, c in (
                (head_dft, self.const["head_dft"]), (turn, self.const["turn"]), (inv, self.const["pool_" + name]),
                (rope, self.const["rope"]), (dft, self.const["token_dft_" + name]),
                (raw_ws, i["w_sgu_2"][layer].rearrange("h p q -> p h q")))]
            for h in range(HEADS2):
                half = slice(HD * (h % 2), HD * (h % 2 + 1))
                loads.append(self.dma(sp, wf[half, h // 2, :], i["w_fnet_2"][layer, h], after=base))
                loads.append(self.dma(sp, wp[half, h // 2, :], i["w_pool_2"][layer, h], after=base))
                b = i["b_sgu_2"][layer, h]
                loads.append(self.dma(sp, BB[half, h // 2, :], bass.AP(b.tensor, b.offset, [[0, HD], [1, P]]), after=base))
            pads = self.v("set", PZ, 0.0, after=base, lane=self.pool)
        t, x, kr_ready = got["kr"]
        if name == "main":
            kr_ready = self.turned(x, turn, rope, [kr_ready, loads])
        kr_ready = self.a(KH[HD:HD + ROPE, :, own:own + T], x.rearrange("p (o t) -> p o t", o=1)
                          .broadcast_to([ROPE, HEADS2, T]), ACT.Copy, after=[kr_ready, base])
        t.free = [kr_ready]
        if not kv_only:

            def put_p(n, f, ps, done, bank):
                m = self.a(PZ[:, f, 8:8 + T], ps, ACT.Copy, after=[done, pads])
                bank.free = [m]
                got["p"] = m
            section(1120, GW, P, put_p)
            E = T + 16
            prev, windows = [got["p"]], []
            for k in range(2):
                z = PZ[:, k, :]
                held = self.temps.next()
                pooled = held.ap[:, 0:T]
                prev = [prev, held.free]
                s = z
                for n in range(4 if k else 2):
                    reach = 2 ** n // 2 if n else 0
                    lo, hi = (1, E) if n == 0 else (2 ** n, E - 2 ** n + 1)
                    a_, b_ = (-1, 0) if n == 0 else (-reach, reach)
                    d = sums[n % 2]
                    prev = [self.v("tt", d[:, lo:hi], s[:, lo + a_:hi + a_], s[:, lo + b_:hi + b_], ALU.add, after=[prev, base])]
                    s = d
                    if n // 2 == k:
                        half = slice(HD * (n % 2), HD * (n % 2 + 1))
                        dst = pooled[half]
                        m = self.v("tt", dst, s[half, 8:8 + T], inv[half, k, :], ALU.mult, after=[prev, loads[2], base])
                        m = self.v("tt", dst, dst, z[half, 8:8 + T], ALU.subtract, after=[m])
                        prev = [m]
                windows.append((held, pooled, prev))

            def put_v(n, f, ps, done, bank):
                t = self.temps.next()
                x = t.ap[:, 0:T]
                m = self.a(x, ps, ACT.Copy, after=[done, t.free])
                bank.free = [m]
                m = self.gelu(x, [m])

                def turn_v():
                    turned = self.mix.next()
                    done = self.transposes([(turned.ap[:, a * P:(a + 1) * P], x[:, a * P:(a + 1) * P], P) for a in range(nt)],
                                           [m, turned.free])
                    t.free = [done]
                    got["v"] = self.a(V_[:, :, f * P:(f + 1) * P], turned.ap[:, 0:T].rearrange("p (a n) -> p a n", a=nt),
                                      ACT.Copy, after=[done, base])
                    turned.free = [got["v"]]
                self.jobs.append(turn_v)
            section(864, GW, P, put_v)

            def put_u(n, f, ps, done, bank):
                m = self.a(U_[:, f, :], ps, ACT.Copy, after=[done, base])
                bank.free = [m]
                got["u"] = self.gelu(U_[:, f, :], [m])
            section(608, GW, P, put_u)

            self.flush()
            for a in range(nt):
                t = self.temps.next()
                v3 = lambda x: x.rearrange("p (h d) -> p h d", h=HEADS2)
                sq, st = t.ap[:, 0:GW], t.ap[:, GW:GW + HEADS2]
                m = self.v("tt", sq, V_[:, a, :], V_[:, a, :], ALU.mult, after=[got["v"], t.free], lane=self.pool)
                m = self.v("sum", st, v3(sq), after=[m])
                m = self.v("ts", st, st, 1.0 / HD, EPS, ALU.mult, ALU.add, after=[m])
                m = self.a(st, st, ACT.Sqrt, after=[m])
                m = self.v("recip", st, st, after=[m])
                m = self.v("tt", v3(V_[:, a, :]), v3(V_[:, a, :]),
                           st.rearrange("p (h o) -> p h o", o=1).broadcast_to([P, HEADS2, HD]), ALU.mult, after=[m])
                t.free = [m]
            v_ready = m
            section(256, Q_RANK, 96, copy_to(lambda f: CQ[:, f, :], "cq"))
            q_ready = rank_norm([CQ[:, 0, :], CQ[:, 1, :]], 96, f"g_q{layer}", got["cq"])
            section(0, GW, P, copy_to(lambda f: F_[:, f, :], "f"))
            self.flush()
            hn_read = [(self.pe.sem, self.pe.count)]

        src = i["w_ukv_2"][layer].rearrange("(k p) (h n) -> p k h n", p=P, h=HEADS2)
        slot, (w_k, w_v), landed = self.pieces([(0, P, 1, GW, src[:, :, :, 0:HD]), (GW, P, 1, GW, src[:, :, :, HD:2 * HD])])
        for h in range(HEADS2):
            bank = self.mix.next()
            done = self.mm(bank.ap[0:HD, 0:T], [(w_k[:, 0, h * HD:(h + 1) * HD], CKV)], [landed, kv_ready, bank.free])
            m = self.a(KH[0:HD, h, own:own + T], bank.ap[0:HD, 0:T], ACT.Copy, after=[done, base])
            bank.free = [m]
        kn_ready = m
        for a in range(nt):
            bank = self.mix.next()
            done = self.mm(bank.ap[:, 0:GW], [(CKV[:, a * P:(a + 1) * P], w_v[:, 0, :])], [bank.free])
            m = self.a(VT[:, own // P + a, :], bank.ap[:, 0:GW], ACT.Copy, after=[done, base])
            bank.free = [m]
        slot.free = [done]
        vt_ready = m
        part.kv = [kn_ready, vt_ready, kr_ready]
        if kv_only:
            return
        for h in range(HEADS2):
            po, k = HD * (h % 2), h // 2
            bank = self.mix.next()

            def emit(e, bank=bank, po=po, k=k):
                for c in range(2):
                    last = e.matmul(bank.ap[po:po + HD, c * HD:(c + 1) * HD], head_dft[po:po + HD, c * HD:(c + 1) * HD],
                                    wf[po:po + HD, k, :], start=True, stop=True)
                return last
            done = self.pe.do(emit, [loads, bank.free])
            m = self.v("copy", R_[po:po + HD, k, :], bank.ap[po:po + HD, 0:P], after=[done])
            bank.free = [m]
        for a in range(nt):
            bank = [self.mix.next(), self.mix.next()]

            def emit(e, bank=bank, a=a):
                for h in range(HEADS2):
                    po, k = HD * (h % 2), h // 2
                    last = e.matmul(bank[h % 2].ap[:, k * P:(k + 1) * P], F_[po:po + HD, k, a * P:(a + 1) * P],
                                    R_[po:po + HD, k, :], start=True, stop=True)
                return last
            done = self.pe.do(emit, [m, got["f"], bank[0].free, bank[1].free])
            m2 = []
            for o in range(2):
                dst = YT[:, a, :].rearrange("p (c k o n) -> p o c k n", k=2, o=2, c=2)[:, o]
                m2.append(self.v("copy", dst, bank[o].ap[:, 0:2 * P].rearrange("p (k c n) -> p c k n", k=2, c=2),
                                 after=[done, base]))
                bank[o].free = [m2[-1]]
        for k in range(2):
            bank = self.mix.next()
            pairs = [(YT[:, a, c * GW + k * P:c * GW + (k + 1) * P], dft[:, c, a, :])
                     for c in range(2) for a in range(nt)]
            done = self.mm(bank.ap[:, 0:T], pairs, [m2, bank.free])
            m = mixed(k, bank.ap[:, 0:T], [done])
            bank.free = [m]
        fourier_ready = m
        bank = self.mix.next()
        done = self.transposes([(bank.ap[:, h * P:(h + 1) * P], raw_ws[:, h, :], P) for h in range(HEADS2)], [loads, bank.free])
        ws_ready = self.v("copy", WST.rearrange("p h n -> p (h n)"), bank.ap, after=[done])
        bank.free = [ws_ready]
        for k in range(2):
            bank = self.mix.next()

            def emit(e, bank=bank, k=k):
                for a in range(nt):
                    for o in range(2):
                        h = 2 * k + o
                        last = e.matmul(bank.ap[HD * o:HD * (o + 1), a * P:(a + 1) * P], V_[:, a, h * HD:(h + 1) * HD],
                                        WST[:, h, :], start=True, stop=True)
                return last
            done = self.pe.do(emit, [v_ready, ws_ready, bank.free])
            blocks = lambda x: x.rearrange("p (a n) -> p a n", n=P)
            t = self.temps.next()
            y = t.ap[:, 0:T]
            m = self.v("stt", blocks(y), blocks(bank.ap[:, 0:T]), self.column(f"g_sgu{layer}", 1, skip=k),
                       BB[:, k:k + 1, :].broadcast_to([P, nt, P]), ALU.mult, ALU.add, after=[done, t.free])
            bank.free = [m]
            m = self.v("tt", y, y, U_[:, k, :], ALU.mult, after=[m, got["u"]])
            m = mixed(4 + k, y, [m])
            t.free = [m]
        sgu_ready = m
        src = i["w_uq_2"][layer].rearrange("(k p) n -> p k n", p=96)
        slot, (w_q,), landed = self.pieces([(0, 96, 2, HEADS2 * (HD + ROPE), src)])
        turned = []
        read = [(self.pe.sem, self.pe.count)]
        for h in range(HEADS2):
            bank = self.mix.next()
            done = self.mm(bank.ap[0:HD + ROPE, 0:T], [(w_q[:, n, h * (HD + ROPE):(h + 1) * (HD + ROPE)], CQ[:, n, :])
                                                       for n in range(2)], [landed, q_ready, bank.free])
            m = self.a(QH[0:HD + ROPE, h, :], bank.ap[0:HD + ROPE, 0:T], ACT.Copy, after=[done, read])
            bank.free = [m]
            turned.append(m)
        slot.free = [done]
        if name == "main":
            turned = [turned, [self.turned(QH[HD:HD + ROPE, h, :], turn, rope, [m, loads]) for h, m in enumerate(turned)]]
        q_ready = turned

        for k, (held, pooled, prev) in enumerate(windows):
            bank = self.mix.next()

            def emit(e, bank=bank, k=k, pooled=pooled):
                for o in range(2):
                    half = slice(HD * o, HD * (o + 1))
                    last = e.matmul(bank.ap[half, 0:T], wp[half, k, :], pooled[half], start=True, stop=True)
                return last
            done = self.pe.do(emit, [prev, bank.free])
            m = self.v("ts", pooled, bank.ap[:, 0:T], self.column(f"s_pool{layer}", 1, skip=k), None, ALU.mult,
                       after=[done])
            bank.free = [m]
            m = mixed(6 + k, pooled, [m])
            held.free = [m]
        pool_ready = m
        k_lo, k_hi = (0, keys) if name == "main" else (SEQ, keys)
        nk = k_hi - k_lo
        scale = (HD + ROPE) ** -0.5
        mx, sm = self.small[:, 32:48], self.small[:, 48:64]
        pt_first = [(self.pe.sem, self.pe.count), (self.dve.sem, self.dve.count)]
        all_kv = [self.side.kv, part.kv]
        four = self.banks.banks + self.mix.banks
        assert not any(b.taken for b in four)
        pairs = Turn([Bank((self.ps[:, n:n + 2, :].rearrange("p a n -> p (a n)"), n)) for n in range(0, 8, 2)])
        for n, b in enumerate(pairs.banks):
            b.free = [four[2 * n].free, four[2 * n + 1].free]

        def rows_of_scores(h, qt):
            bank = pairs.next()
            wide = bank.ap[0]
            q = slice(qt * P, (qt + 1) * P)

            def emit(e):
                for lo in range(0, nk, 512):
                    n = min(512, nk - lo)
                    key = slice(k_lo + lo, k_lo + lo + n)
                    last = e.matmul(wide[:, lo:lo + n], QH[0:HD + ROPE, h, q], KH[0:HD + ROPE, h, key], start=True, stop=True)
                return last
            done = self.pe.do(emit, [all_kv, q_ready, bank.free])
            c = slice(h * nt + qt, h * nt + qt + 1)
            s = scores.next()
            m = self.v("max", mx[:, c], wide[:, 0:nk], after=[done])
            m = self.v("ts", mx[:, c], mx[:, c], -scale, None, ALU.mult, after=[m])
            m = self.a(s.ap[:, 0:nk], wide[:, 0:nk], ACT.Exp, after=[m, s.free, pt_first], bias=mx[:, c], scale=scale,
                       accum_out=sm[:, c])
            bank.free = [m]
            m = self.v("recip", sm[:, c], sm[:, c], after=[m])
            m = self.v("ts", s.ap[:, 0:nk], s.ap[:, 0:nk], sm[:, c], None, ALU.mult, after=[m])
            return h, qt, s, m

        def weigh_values(h, qt, s, m):
            po, k = HD * (h % 2), h // 2
            q = slice(qt * P, (qt + 1) * P)
            if qt == 0:
                got["pt"] = PT.next()
            pt = got["pt"]
            bank = pairs.next()
            wide = bank.ap[0]
            done = self.transposes([(wide[:, a * P:(a + 1) * P], s.ap[:, a * P:(a + 1) * P], P) for a in range(nk // P)],
                                   [m, bank.free])
            s.free = [done]
            m = self.a(pt.ap[:, 0:nk // P, q], wide[:, 0:nk].rearrange("p (a q) -> p a q", q=P), ACT.Copy,
                       after=[done, pt.free, pt_first])
            bank.free = [m]

            def values():
                bank = pairs.next()
                out = bank.ap[0][po:po + HD, 0:T]
                done = self.mm(out, [(VT[:, k_lo // P + a, h * HD:(h + 1) * HD], pt.ap[:, a, 0:T]) for a in range(nk // P)],
                               [m, bank.free])
                pt.free = [done]
                got["attention"] = mixed(2 + k, out, [done], slice(po, po + HD))
                bank.free = [got["attention"]]
            if qt == nt - 1:
                self.jobs.append(values)
        late = []
        for h in range(HEADS2):
            for qt in range(nt):
                if len(late) == 2:
                    weigh_values(*late.pop(0))
                late.append(rows_of_scores(h, qt))
                if qt == (2 if nt > 2 else 0):
                    self.pump()
        while late:
            weigh_values(*late.pop(0))
        self.flush()
        m = got["attention"]
        for n, b in enumerate(pairs.banks):
            four[2 * n].free = four[2 * n + 1].free = b.free
        y_ready = [m, fourier_ready, sgu_ready, pool_ready]
        last = [()]

        def take_out(n, f, ps, done, bank):
            m = self.v("stt", part.h[:, f, 0:T], ps, rows(5)[:, f:f + 1], part.h[:, f, 0:T], ALU.mult, ALU.add, after=[done])
            bank.free = last[0] = [m]
            self.square(part, f, [m])
        if name == "main":
            assert mixed_at >= self.phase_base + 4 * 2 * KT * (2 * CTX + SEQ)
            self.feed_forward_map()
            if layer == 0:
                self.norm_for_half_step(self.side, layer, "g_ffn2", 6)
        self.linear(i["w_out_2"][layer], KT, 0, D, [(YS, T, y_ready)], take_out, background=False)
        self.finish_square(part)
        part.h_ready = last[0]

    def turned(self, x, turn, rope, ready):
        bank, t = self.mix.next(), self.temps.next()
        at = slice(HD, HD + ROPE)
        done = self.mm(bank.ap[at], [(turn[at, at], x)], [ready, bank.free])
        m = self.v("tt", t.ap[at], bank.ap[at], rope[at, 1, :], ALU.mult, after=[done, t.free])
        bank.free = [m]
        m2 = self.v("tt", x, x, rope[at, 0, :], ALU.mult, after=[done])
        m = self.v("tt", x, x, t.ap[at], ALU.add, after=[m, m2])
        t.free = [m]
        return m

    def small_const(self, name, src):
        if name not in self.loaded:
            n = len(self.loaded)
            view = self.small_consts[0:src.shape[0], n * P:n * P + src.shape[1]]
            self.loaded[name] = (view, self.dma(self.sp, view, src))
        return self.loaded[name]

    def second_block(self):
        main, side = self.main, self.side
        both = [main, side]
        for layer in range(2):
            if layer == 1:
                self.feed_forward_map()
                self.norm_for_half_step(side, layer, "g_ffn1", 0)
            else:
                main.hn_free = self.hidden_free = self.everything()
            self.norm_for_half_step(main, layer, "g_ffn1", 0)
            self.half_step(both, layer, "g_ffn1", 0)
            self.mixers(side, layer, layer == 1)
            self.mixers(main, layer, False)
            self.hidden_free = self.everything()
            self.norm_for_half_step(main, layer, "g_ffn2", 6)
            self.half_step(both if layer == 0 else [main], layer, "g_ffn2", 6)
        self.plain_norm(main, "final2", False)
        free = self.everything()
        self.at = self.phase_base
        stage = self.area("tokens_out", 4 * D).rearrange("p (a n) -> p a n", a=4)
        for a in range(4):
            for half in range(2):
                bank = self.mix.next()
                done = self.transposes([(bank.ap[:, k * P:(k + 1) * P], main.h[:, 4 * half + k, a * P:(a + 1) * P], P)
                                        for k in range(4)], [main.h_ready, bank.free])
                m = self.v("copy", stage[:, a, half * 512:(half + 1) * 512], bank.ap, after=[done, free])
                bank.free = [m]
            self.dram_writes.append(self.dma(self.sp, self.out[0, a * P:(a + 1) * P, :], stage[:, a, :], after=[m],
                                             counter=self.out_landed))
        self.sp.steps.append((marks(self.dram_writes), lambda e: None, None, 0))


def build(nc, scratch, inp, const, out):
    plan = None
    for target in (scratch, nc):
        with ExitStack() as ctx:
            prog = Program(target, ctx, inp, const, out, plan)
            prog.setup()
            prog.first_block()
            prog.second_block()
            plan = prog.asked
            if target is scratch:
                continue
            block = ctx.enter_context(nc.Block())
            block.sync(lambda e: prog.sp.play(e))
            block.gpsimd(lambda e: prog.pool.play(e))
            block.scalar(lambda e: prog.act.play(e))
            block.tensor(lambda e: prog.pe.play(e))
            block.vector(lambda e: prog.dve.play(e))


def kernel(**inputs):
    import concourse.bacc as bacc
    from concourse.bass_utils import run_bass_kernel_spmd

    nc = bacc.Bacc("TRN2", target_bir_lowering=False, num_devices=1)
    arrays, inp, const = {}, {}, {}
    for name, a in inputs.items():
        a = np.ascontiguousarray(a)
        arrays["in_" + name] = a
        inp[name] = nc.dram_tensor("in_" + name, a.shape, F32, kind="ExternalInput").ap()
    for name, a in shape_constants().items():
        arrays["const_" + name] = np.ascontiguousarray(a)
        const[name] = nc.dram_tensor("const_" + name, a.shape, F32, kind="ExternalInput").ap()
    out = nc.dram_tensor("out", (1, SEQ, D), F32, kind="ExternalOutput").ap()
    scratch = bacc.Bacc("TRN2", target_bir_lowering=False, num_devices=1)
    build(nc, scratch, inp, const, out)
    result = run_bass_kernel_spmd(nc, [arrays], core_ids=[0])
    return result.results[0]["out"]
```
